# Optimizing a Trainium2 kernel written in Bass

```python
import math
import jax, jax.numpy as jnp
from jax import lax
import numpy as np

D_MODEL = 1024
BATCH = 1
SEQ = 256
DEPTH = 1

POOL_WINDOWS = (2, 4, 8, 16)
N_POOL_GROUPS = len(POOL_WINDOWS)
POOL_GROUP_DIM = D_MODEL // 8
POOL_WIDTH = N_POOL_GROUPS * POOL_GROUP_DIM

SSD_WIDTH = D_MODEL
SSD_HEAD_DIM = 64
SSD_HEADS = SSD_WIDTH // SSD_HEAD_DIM
SSD_GROUPS = 2
HEADS_PER_GROUP = SSD_HEADS // SSD_GROUPS
SSD_STATE = 128
SSD_CONV = 4
SSD_CHUNK = 128
CONV_DIM = SSD_WIDTH + 2 * SSD_GROUPS * SSD_STATE

MIX_WIDTH = POOL_WIDTH + SSD_WIDTH
IN_PROJ_DIM = POOL_WIDTH + SSD_WIDTH + CONV_DIM + SSD_HEADS

PEER_HEADS = 8
PEER_TOPK = 16
N_KEYS = 128
N_EXPERTS = N_KEYS * N_KEYS
D_KEY = 256
PEER_BLOCK = 128

N_MOD = 6
EPS = 1e-6


def rmsnorm(x, g):
    xf = x.astype(jnp.float32)
    y = xf * lax.rsqrt(jnp.mean(xf * xf, axis=-1, keepdims=True) + EPS)
    return (y * g.astype(jnp.float32)).astype(x.dtype)

def modulate(h, shift, scale):
    return h * (1 + scale[:, None, :]) + shift[:, None, :]

def pool_mixer(u, pool_w, pool_b, pool_scale):
    Bsz, S, _ = u.shape
    ug = u.astype(jnp.float32).reshape(Bsz, S, N_POOL_GROUPS, POOL_GROUP_DIM)
    cs = jnp.cumsum(ug, axis=1)
    t = jnp.arange(S)
    pooled = []
    for gi, w in enumerate(POOL_WINDOWS):
        csg = cs[:, :, gi]
        cs_pad = jnp.pad(csg, ((0, 0), (w, 0), (0, 0)))
        win_sum = cs_pad[:, w:] - cs_pad[:, :S]
        count = jnp.minimum(t + 1, w).astype(jnp.float32)[None, :, None]
        pooled.append(win_sum / count)
    pooled = jnp.stack(pooled, axis=2)
    mixed = pooled - ug
    y = jnp.einsum("bsgc,gcd->bsgd", mixed, pool_w.astype(jnp.float32)) + pool_b.astype(jnp.float32)
    y = y * pool_scale.astype(jnp.float32)
    return y.reshape(Bsz, S, POOL_WIDTH).astype(u.dtype)

def ssd_chunked(xdt, a, b, c):
    Bsz, S, G, R, P = xdt.shape
    N = b.shape[-1]
    L = SSD_CHUNK
    nc = S // L
    xdt = xdt.reshape(Bsz, nc, L, G, R, P)
    b = b.reshape(Bsz, nc, L, G, N)
    c = c.reshape(Bsz, nc, L, G, N)
    a = a.reshape(Bsz, nc, L, G, R).transpose(0, 3, 4, 1, 2)
    a_cs = jnp.cumsum(a, axis=-1)

    causal = jnp.tril(jnp.ones((L, L), dtype=bool))
    seg = a_cs[..., :, None] - a_cs[..., None, :]
    decay = jnp.exp(jnp.where(causal, seg, -jnp.inf))
    cb = jnp.einsum("bclgn,bcsgn->bcgls", c, b)
    y_diag = jnp.einsum("bcgls,bgrcls,bcsgrp->bclgrp", cb, decay, xdt)

    decay_to_end = jnp.exp(a_cs[..., -1:] - a_cs)
    states = jnp.einsum("bclgn,bgrcl,bclgrp->bcgrpn", b, decay_to_end, xdt)
    chunk_decay = jnp.exp(a_cs[..., -1])

    def step(h, inp):
        st, dec = inp
        return h * dec[..., None, None] + st, h

    h0 = jnp.zeros((Bsz, G, R, P, N), jnp.float32)
    _, h_prev = lax.scan(step, h0, (jnp.moveaxis(states, 1, 0), jnp.moveaxis(chunk_decay, -1, 0)))
    y_off = jnp.einsum("bclgn,cbgrpn,bgrcl->bclgrp", c, h_prev, jnp.exp(a_cs))
    return (y_diag + y_off).reshape(Bsz, S, G, R, P)

def ssd_mixer(z, xbc, dt_raw, conv_w, conv_b, dt_bias, a_log, d_skip, ssd_norm):
    Bsz, S, _ = xbc.shape
    dtype = xbc.dtype
    xf = xbc.astype(jnp.float32)
    conv = lax.conv_general_dilated(
        xf, conv_w.astype(jnp.float32).reshape(SSD_CONV, 1, CONV_DIM),
        window_strides=(1,), padding=[(SSD_CONV - 1, 0)],
        dimension_numbers=("NWC", "WIO", "NWC"), feature_group_count=CONV_DIM)
    conv = jax.nn.silu(conv + conv_b.astype(jnp.float32))
    xs = conv[..., :SSD_WIDTH].reshape(Bsz, S, SSD_GROUPS, HEADS_PER_GROUP, SSD_HEAD_DIM)
    bs = conv[..., SSD_WIDTH:SSD_WIDTH + SSD_GROUPS * SSD_STATE].reshape(Bsz, S, SSD_GROUPS, SSD_STATE)
    cs = conv[..., SSD_WIDTH + SSD_GROUPS * SSD_STATE:].reshape(Bsz, S, SSD_GROUPS, SSD_STATE)

    dt = jax.nn.softplus(dt_raw.astype(jnp.float32) + dt_bias.astype(jnp.float32))
    dt = dt.reshape(Bsz, S, SSD_GROUPS, HEADS_PER_GROUP)
    A = -jnp.exp(a_log.astype(jnp.float32)).reshape(SSD_GROUPS, HEADS_PER_GROUP)
    y = ssd_chunked(xs * dt[..., None], dt * A, bs, cs)
    y = y + xs * d_skip.astype(jnp.float32).reshape(SSD_GROUPS, HEADS_PER_GROUP)[..., None]
    y = y.reshape(Bsz, S, SSD_WIDTH) * jax.nn.silu(z.astype(jnp.float32))
    return rmsnorm(y, ssd_norm).astype(dtype)

def peer(h, w_query, sub_keys1, sub_keys2, expert_down, expert_up):
    Bsz, S, D = h.shape
    T = Bsz * S
    hf = h.reshape(T, D)
    q = (hf @ w_query).reshape(T, PEER_HEADS, 2, D_KEY // 2)
    s1 = jnp.einsum("thk,hnk->thn", q[:, :, 0], sub_keys1).astype(jnp.float32)
    s2 = jnp.einsum("thk,hnk->thn", q[:, :, 1], sub_keys2).astype(jnp.float32)
    v1, i1 = lax.top_k(s1, PEER_TOPK)
    v2, i2 = lax.top_k(s2, PEER_TOPK)
    cand = (v1[..., :, None] + v2[..., None, :]).reshape(T, PEER_HEADS, PEER_TOPK * PEER_TOPK)
    cand_idx = (i1[..., :, None] * N_KEYS + i2[..., None, :]).reshape(T, PEER_HEADS, PEER_TOPK * PEER_TOPK)
    top_s, pos = lax.top_k(cand, PEER_TOPK)
    idx = jnp.take_along_axis(cand_idx, pos, axis=-1)
    gates = jax.nn.softmax(top_s, axis=-1).astype(h.dtype)

    nb = T // PEER_BLOCK

    def block_fn(args):
        hb, ib, gb = args
        u = expert_down[ib]
        act = jax.nn.gelu(jnp.einsum("td,thkd->thk", hb, u), approximate=False)
        v = expert_up[ib]
        return jnp.einsum("thk,thkd->td", gb * act, v)

    out = lax.map(block_fn, (hf.reshape(nb, PEER_BLOCK, D),
                             idx.reshape(nb, PEER_BLOCK, PEER_HEADS, PEER_TOPK),
                             gates.reshape(nb, PEER_BLOCK, PEER_HEADS, PEER_TOPK)))
    return out.reshape(Bsz, S, D)

def first_inputs(seed: int = 0) -> dict:
    key = jax.random.key(seed)
    ks = jax.random.split(key, 24)

    def nrm(k, shape, s):
        return jax.random.normal(k, shape, jnp.float32) * s

    x = nrm(ks[0], (BATCH, SEQ, D_MODEL), 1.0)
    c = nrm(ks[1], (BATCH, D_MODEL), 1.0)
    w_ada = nrm(ks[2], (DEPTH, D_MODEL, N_MOD * D_MODEL), 0.5 * D_MODEL ** -0.5)
    b_ada = nrm(ks[3], (DEPTH, N_MOD * D_MODEL), 0.02)
    norm_mix = 1.0 + nrm(ks[4], (DEPTH, D_MODEL), 0.02)
    norm_ffn = 1.0 + nrm(ks[5], (DEPTH, D_MODEL), 0.02)
    w_in = nrm(ks[6], (DEPTH, D_MODEL, IN_PROJ_DIM), D_MODEL ** -0.5)
    pool_w = nrm(ks[7], (DEPTH, N_POOL_GROUPS, POOL_GROUP_DIM, POOL_GROUP_DIM), POOL_GROUP_DIM ** -0.5)
    pool_b = nrm(ks[8], (DEPTH, N_POOL_GROUPS, POOL_GROUP_DIM), 0.02)
    pool_scale = 1.0 + nrm(ks[9], (DEPTH, N_POOL_GROUPS, POOL_GROUP_DIM), 0.1)
    conv_w = nrm(ks[10], (DEPTH, SSD_CONV, CONV_DIM), SSD_CONV ** -0.5)
    conv_b = nrm(ks[11], (DEPTH, CONV_DIM), 0.02)
    dt0 = jnp.exp(jax.random.uniform(ks[12], (DEPTH, SSD_HEADS), jnp.float32,
                                     minval=math.log(1e-3), maxval=math.log(1e-1)))
    dt_bias = dt0 + jnp.log(-jnp.expm1(-dt0))
    a_log = jnp.log(jax.random.uniform(ks[13], (DEPTH, SSD_HEADS), jnp.float32, minval=1.0, maxval=16.0))
    d_skip = 1.0 + nrm(ks[14], (DEPTH, SSD_HEADS), 0.1)
    ssd_norm = 1.0 + nrm(ks[15], (DEPTH, SSD_WIDTH), 0.02)
    w_out = nrm(ks[16], (DEPTH, MIX_WIDTH, D_MODEL), MIX_WIDTH ** -0.5)
    w_query = nrm(ks[17], (DEPTH, D_MODEL, PEER_HEADS * D_KEY), D_MODEL ** -0.5)
    sub_keys1 = nrm(ks[18], (DEPTH, PEER_HEADS, N_KEYS, D_KEY // 2), (D_KEY // 2) ** -0.5)
    sub_keys2 = nrm(ks[19], (DEPTH, PEER_HEADS, N_KEYS, D_KEY // 2), (D_KEY // 2) ** -0.5)
    expert_down = nrm(ks[20], (DEPTH, N_EXPERTS, D_MODEL), D_MODEL ** -0.5)
    expert_up = nrm(ks[21], (DEPTH, N_EXPERTS, D_MODEL), PEER_HEADS ** -0.5)
    norm_final = 1.0 + nrm(ks[22], (D_MODEL,), 0.02)
    return {"x": x, "c": c, "w_ada": w_ada, "b_ada": b_ada, "norm_mix": norm_mix, "norm_ffn": norm_ffn,
            "w_in": w_in, "pool_w": pool_w, "pool_b": pool_b, "pool_scale": pool_scale,
            "conv_w": conv_w, "conv_b": conv_b, "dt_bias": dt_bias, "a_log": a_log, "d_skip": d_skip,
            "ssd_norm": ssd_norm, "w_out": w_out, "w_query": w_query, "sub_keys1": sub_keys1,
            "sub_keys2": sub_keys2, "expert_down": expert_down, "expert_up": expert_up,
            "norm_final": norm_final}

def first_block(x, c, w_ada, b_ada, norm_mix, norm_ffn, w_in, pool_w, pool_b, pool_scale,
              conv_w, conv_b, dt_bias, a_log, d_skip, ssd_norm, w_out, w_query, sub_keys1,
              sub_keys2, expert_down, expert_up, norm_final):
    Bsz = x.shape[0]
    c_act = jax.nn.silu(c)
    s_z = POOL_WIDTH
    s_xbc = POOL_WIDTH + SSD_WIDTH
    s_dt = POOL_WIDTH + SSD_WIDTH + CONV_DIM
    for l in range(DEPTH):
        mod = (c_act @ w_ada[l] + b_ada[l]).reshape(Bsz, N_MOD, D_MODEL)
        shift_m, scale_m, gate_m, shift_f, scale_f, gate_f = [mod[:, i] for i in range(N_MOD)]

        h = modulate(rmsnorm(x, norm_mix[l]), shift_m, scale_m)
        proj = h @ w_in[l]
        y_pool = pool_mixer(proj[..., :s_z], pool_w[l], pool_b[l], pool_scale[l])
        y_ssd = ssd_mixer(proj[..., s_z:s_xbc], proj[..., s_xbc:s_dt], proj[..., s_dt:],
                          conv_w[l], conv_b[l], dt_bias[l], a_log[l], d_skip[l], ssd_norm[l])
        y = jnp.concatenate([y_pool, y_ssd], axis=-1) @ w_out[l]
        x = x + gate_m[:, None, :] * y

        h = modulate(rmsnorm(x, norm_ffn[l]), shift_f, scale_f)
        y = peer(h, w_query[l], sub_keys1[l], sub_keys2[l], expert_down[l], expert_up[l])
        x = x + gate_f[:, None, :] * y
    return rmsnorm(x, norm_final)


CHUNK = 64

LRU_WIDTH = D_MODEL
LRU_HEADS = 8
LRU_HEAD_DIM = LRU_WIDTH // LRU_HEADS
LRU_CONV = 4
LRU_C = 8.0

CONV_WIDTH = D_MODEL
CONV_GROUPS = 8
CONV_K = 3

N_BRANCHES = 2
IN_COLS = 2 * LRU_WIDTH + 3 * CONV_WIDTH + N_BRANCHES * D_MODEL

PEER_NKEYS = 128
PEER_N = PEER_NKEYS * PEER_NKEYS
PEER_DKEY = 256
PEER_HALF = PEER_DKEY // 2


def rmsnorm_2(x, g):
    xf = x.astype(jnp.float32)
    y = xf * lax.rsqrt(jnp.mean(xf * xf, axis=-1, keepdims=True) + EPS)
    return (y * g.astype(jnp.float32)).astype(x.dtype)

def causal_dwconv(x, w):
    k, c = w.shape
    return lax.conv_general_dilated(
        x, w[:, None, :].astype(x.dtype), window_strides=(1,), padding=[(k - 1, 0)],
        dimension_numbers=("NWC", "WIO", "NWC"), feature_group_count=c)

def rg_lru(x, w_a, b_a, w_x, b_x, lam):
    b, s, _ = x.shape
    xh = x.reshape(b, s, LRU_HEADS, LRU_HEAD_DIM)
    r = jax.nn.sigmoid(jnp.einsum("bshi,hij->bshj", xh, w_a).reshape(b, s, LRU_WIDTH) + b_a)
    i = jax.nn.sigmoid(jnp.einsum("bshi,hij->bshj", xh, w_x).reshape(b, s, LRU_WIDTH) + b_x)
    log_a = (-LRU_C * r.astype(jnp.float32)) * jax.nn.softplus(-lam.astype(jnp.float32))
    a = jnp.exp(log_a)
    mult = jnp.sqrt(-jnp.expm1(2.0 * log_a))
    u = mult * (i * x).astype(jnp.float32)

    def combine(left, right):
        a1, b1 = left
        a2, b2 = right
        return a1 * a2, a2 * b1 + b2

    _, h = lax.associative_scan(combine, (a, u), axis=1)
    return h.astype(x.dtype)

def token_mixers(xn, w_in, conv_a_w, conv_a_b, w_a, b_a, w_x, b_x, lam, conv_b_w, w_out):
    p = xn @ w_in
    splits = [LRU_WIDTH, 2 * LRU_WIDTH, 2 * LRU_WIDTH + CONV_WIDTH,
              2 * LRU_WIDTH + 2 * CONV_WIDTH, 2 * LRU_WIDTH + 3 * CONV_WIDTH,
              2 * LRU_WIDTH + 3 * CONV_WIDTH + D_MODEL]
    xa, ga, vb, bb, cb, ma, mb = jnp.split(p, splits, axis=-1)
    ya = rg_lru(causal_dwconv(xa, conv_a_w) + conv_a_b, w_a, b_a, w_x, b_x, lam) * jax.nn.gelu(ga)
    yb = bb * causal_dwconv(cb * vb, conv_b_w)
    merged = jax.nn.sigmoid(ma) * ya + jax.nn.sigmoid(mb) * yb
    return merged @ w_out

def peer_2(xn, w_q, sub_keys, u_tab, v_tab):
    b, s, d = xn.shape
    t = xn.reshape(-1, d)
    n_tok = t.shape[0]
    q = (t @ w_q).reshape(n_tok, PEER_HEADS, 2, PEER_HALF)
    sc = jnp.einsum("thpk,hpnk->thpn", q, sub_keys).astype(jnp.float32)
    s_top, i_top = lax.top_k(sc, PEER_TOPK)
    cand = s_top[:, :, 0, :, None] + s_top[:, :, 1, None, :]
    cand_idx = i_top[:, :, 0, :, None] * PEER_NKEYS + i_top[:, :, 1, None, :]
    kk = PEER_TOPK * PEER_TOPK
    best, pos = lax.top_k(cand.reshape(n_tok, PEER_HEADS, kk), PEER_TOPK)
    idx = jnp.take_along_axis(cand_idx.reshape(n_tok, PEER_HEADS, kk), pos, axis=-1)
    g = jax.nn.softmax(best, axis=-1).astype(xn.dtype)

    nb = n_tok // PEER_BLOCK

    def block(args):
        tb, ib, gb = args
        ue = u_tab[ib]
        act = jax.nn.gelu(jnp.einsum("phkd,pd->phk", ue, tb))
        ve = v_tab[ib]
        return jnp.einsum("phk,phkd->pd", gb * act, ve)

    out = lax.map(block, (t.reshape(nb, PEER_BLOCK, d),
                          idx.reshape(nb, PEER_BLOCK, PEER_HEADS, PEER_TOPK),
                          g.reshape(nb, PEER_BLOCK, PEER_HEADS, PEER_TOPK)))
    return out.reshape(b, s, d)

def second_inputs(seed: int = 0) -> dict:
    key = jax.random.key(seed)
    ks = jax.random.split(key, 20)
    f = jnp.float32
    L = DEPTH

    def nrm(k, shape, scale):
        return jax.random.normal(k, shape, f) * scale

    x = nrm(ks[0], (BATCH, SEQ, D_MODEL), 1.0)
    norm1_g = 1.0 + nrm(ks[1], (L, D_MODEL), 0.02)
    w_in = nrm(ks[2], (L, D_MODEL, IN_COLS), D_MODEL ** -0.5)
    conv_a_w = nrm(ks[3], (L, LRU_CONV, LRU_WIDTH), LRU_CONV ** -0.5)
    conv_a_b = nrm(ks[4], (L, LRU_WIDTH), 0.01)
    w_a = nrm(ks[5], (L, LRU_HEADS, LRU_HEAD_DIM, LRU_HEAD_DIM), LRU_HEAD_DIM ** -0.5)
    b_a = nrm(ks[6], (L, LRU_WIDTH), 0.01)
    w_x = nrm(ks[7], (L, LRU_HEADS, LRU_HEAD_DIM, LRU_HEAD_DIM), LRU_HEAD_DIM ** -0.5)
    b_x = nrm(ks[8], (L, LRU_WIDTH), 0.01)
    a_init = jax.random.uniform(ks[9], (L, LRU_WIDTH), f, 0.9, 0.999)
    sig = a_init ** (1.0 / LRU_C)
    lru_lambda = jnp.log(sig) - jnp.log1p(-sig)
    conv_b_w = nrm(ks[10], (L, CONV_K, CONV_WIDTH), CONV_K ** -0.5)
    w_out = nrm(ks[11], (L, D_MODEL, D_MODEL), D_MODEL ** -0.5)
    norm2_g = 1.0 + nrm(ks[12], (L, D_MODEL), 0.02)
    peer_wq = nrm(ks[13], (L, D_MODEL, PEER_HEADS * PEER_DKEY), D_MODEL ** -0.5)
    peer_subkeys = nrm(ks[14], (L, PEER_HEADS, 2, PEER_NKEYS, PEER_HALF), PEER_HALF ** -0.5)
    peer_u = nrm(ks[15], (L, PEER_N, D_MODEL), D_MODEL ** -0.5)
    peer_v = nrm(ks[16], (L, PEER_N, D_MODEL), PEER_HEADS ** -0.5)
    final_g = 1.0 + nrm(ks[17], (D_MODEL,), 0.02)
    return {"x": x, "norm1_g": norm1_g, "w_in": w_in, "conv_a_w": conv_a_w, "conv_a_b": conv_a_b,
            "w_a": w_a, "b_a": b_a, "w_x": w_x, "b_x": b_x, "lru_lambda": lru_lambda,
            "conv_b_w": conv_b_w, "w_out": w_out, "norm2_g": norm2_g, "peer_wq": peer_wq,
            "peer_subkeys": peer_subkeys, "peer_u": peer_u, "peer_v": peer_v, "final_g": final_g}

def second_block(x, norm1_g, w_in, conv_a_w, conv_a_b, w_a, b_a, w_x, b_x, lru_lambda,
              conv_b_w, w_out, norm2_g, peer_wq, peer_subkeys, peer_u, peer_v, final_g):
    h = x
    for l in range(DEPTH):
        xn = rmsnorm_2(h, norm1_g[l])
        h = h + token_mixers(xn, w_in[l], conv_a_w[l], conv_a_b[l], w_a[l], b_a[l], w_x[l], b_x[l],
                             lru_lambda[l], conv_b_w[l], w_out[l])
        h = h + peer_2(rmsnorm_2(h, norm2_g[l]), peer_wq[l], peer_subkeys[l], peer_u[l], peer_v[l])
    return rmsnorm_2(h, final_g)


def setup_inputs(seed=0):
    out = dict(first_inputs(seed))
    for name, value in second_inputs(seed + 1).items():
        if name != "x":
            out[name + "_2"] = value
    return out


def reference(
    x, c, w_ada, b_ada, norm_mix, norm_ffn, w_in, pool_w, pool_b, pool_scale, conv_w, conv_b,
    dt_bias, a_log, d_skip, ssd_norm, w_out, w_query, sub_keys1, sub_keys2, expert_down,
    expert_up, norm_final, norm1_g_2, w_in_2, conv_a_w_2, conv_a_b_2, w_a_2, b_a_2, w_x_2,
    b_x_2, lru_lambda_2, conv_b_w_2, w_out_2, norm2_g_2, peer_wq_2, peer_subkeys_2, peer_u_2,
    peer_v_2, final_g_2,
):
    x = first_block(
        x, c, w_ada, b_ada, norm_mix, norm_ffn, w_in, pool_w, pool_b, pool_scale, conv_w,
        conv_b, dt_bias, a_log, d_skip, ssd_norm, w_out, w_query, sub_keys1, sub_keys2,
        expert_down, expert_up, norm_final,
    )
    return second_block(
        x, norm1_g_2, w_in_2, conv_a_w_2, conv_a_b_2, w_a_2, b_a_2, w_x_2, b_x_2, lru_lambda_2,
        conv_b_w_2, w_out_2, norm2_g_2, peer_wq_2, peer_subkeys_2, peer_u_2, peer_v_2,
        final_g_2,
    )


_drawn_inputs = setup_inputs


def setup_inputs(seed=0):
    import zlib

    import numpy as np

    out = dict(_drawn_inputs(seed))
    spreads = {}
    factors = {'norm_mix': 2.856,
     'norm_ffn': 3.074,
     'pool_b': 3.633,
     'conv_b': 3.037,
     'ssd_norm': 3.465,
     'conv_a_b_2': 2.71,
     'b_a_2': 41.267,
     'b_x_2': 28.609,
     'final_g_2': 23.828,
     'd_skip': 19.202}
    for name, (base, spread) in spreads.items():
        noise = np.random.default_rng([zlib.crc32(name.encode()), seed]).standard_normal(out[name].shape)
        drawn = base * np.exp(spread * noise) if base else spread * noise
        out[name] = __import__('jax').numpy.asarray(drawn.astype(out[name].dtype))
    for name, factor in factors.items():
        out[name] = (out[name] * factor).astype(out[name].dtype)
    return out
```

```python
import numpy as np
import concourse.bass as bass
from concourse import mybir
from contextlib import ExitStack

P = 128
D = 1024
KC = D // P
T = 256
TT = T // P
POOL_W = (2, 4, 8, 16)
NPOOL = len(POOL_W)
UPAD = max(POOL_W)
SSD_TILES = 8
XBC_TILES = 12
HEADS = 16
HPG = 8
HD = 64
CH = 128
NCH = T // CH
TAPS = 4
TAPS_B = 3
PH = 8
LISTS = 2 * PH
TOPK = 16
NKEYS = 128
EPS = 1e-6
RING = 3
BLK = KC * P
LOWEST = -3.0e38

_COLS = [("c", 8), ("b_ada", 48), ("norm_mix", 8), ("norm_ffn", 8), ("pool_b", 4), ("pool_scale", 4),
         ("conv_w", 48), ("conv_b", 12), ("d_skip", 8), ("ssd_norm", 8), ("norm_final", 8), ("dt_bias", 1),
         ("a_log", 1), ("norm1", 8), ("conv_a_w", 32), ("conv_a_b", 8), ("b_a", 8), ("b_x", 8), ("lam", 8),
         ("conv_b_w", 24), ("norm2", 8), ("final", 8)]
COL = {}
_at = 0
for _n, _w in _COLS:
    COL[_n] = (_at, _w)
    _at += _w
NCOL = _at
CIDENT, CONES, CMASK, CIOTA = 0, P, 2 * P, 3 * P
NCONST = 4 * P


def decoder_kernel(nc, A, out):
    fp32 = mybir.dt.float32
    fp32r = mybir.dt.float32r
    u32 = mybir.dt.uint32
    ALU = mybir.AluOpType
    ACT = mybir.ActivationFunctionType
    AX = mybir.AxisListType
    ds = bass.ds

    ctx = ExitStack()
    with ctx:
        def sb(name, shape, dt=fp32):
            return ctx.enter_context(nc.sbuf_tensor(name, shape, dt))

        sems = {}

        def S(name):
            if name not in sems:
                sems[name] = ctx.enter_context(nc.semaphore(name))
            return sems[name]

        xT = sb("xT", [P, KC, T])
        h_hi = sb("h_hi", [P, KC, T], fp32r)
        h_lo = sb("h_lo", [P, KC, T], fp32r)
        prm = sb("prm", [P, NCOL])
        cst = sb("cst", [P, NCONST])
        ring = sb("ring", [P, RING, BLK])
        ring_hi = sb("ring_hi", [P, RING, BLK], fp32r)
        ring_lo = sb("ring_lo", [P, RING, BLK], fp32r)
        arena = sb("arena", [P, 32768])
        wf = sb("wf", [P, 2, 512])
        w_hi = sb("w_hi", [P, 2, 512], fp32r)
        w_lo = sb("w_lo", [P, 2, 512], fp32r)
        selT = sb("selT", [P, 3, T])
        stage = sb("stage", [P, 3, 8])
        mod = sb("mod", [P, 48])
        cact = sb("cact", [P, 8])
        lru_s = sb("lru_s", [P, 8, 8])
        epsc = sb("epsc", [P, 1])
        PS = [ctx.enter_context(nc.psum_tensor(f"ps{i}", [P, 512], fp32)) for i in range(8)]

        ident = cst[:, CIDENT:CIDENT + P]
        ones = cst[:, CONES:CONES + P]
        mask = cst[:, CMASK:CMASK + P]
        iota = cst[:, CIOTA:CIOTA + P]

        def col(name, i, n=1):
            a = COL[name][0] + i
            return prm[:, a:a + n]

        def region(at, *shape):
            n = int(np.prod(shape))
            v = arena[:, at:at + n]
            if len(shape) == 2:
                return v.rearrange("p (a b) -> p a b", b=shape[1])
            if len(shape) == 3:
                return v.rearrange("p (a b c) -> p a b c", b=shape[1], c=shape[2])
            return v

        ada_buf = region(0, 2, KC * D)
        ada_acc = region(16384, 2, D)
        sq = region(18432, KC, T)
        rstd = region(20480, T)
        u_pad = region(20736, NPOOL, UPAD + T)
        zs = region(21824, KC, T)
        xbc_in = region(23872, XBC_TILES, TAPS - 1 + T)
        hT = region(26980, KC, T)
        inv = region(29028, NPOOL, T)
        dts = region(30052, 6, T)
        xdt = region(0, NCH, D)
        xdte = region(2048, D)
        btok = region(3072, 2, P)
        cbt = region(3328, 2, NCH * P)
        stT = region(3840, D)
        mixT = region(4864, NPOOL + SSD_TILES, T)
        tok = region(7936, 5, HEADS)
        seg = region(8192, 2, T)
        dec = region(8704, 2, T)
        mdec = region(9216, 2, T)
        ecs = region(9728, 2, P)
        cexp = region(9984, 2, P)
        p_sum = region(10240, 2, UPAD + T)
        p_mix = region(10784, NPOOL, T)
        p_t = region(11808, NPOOL, T)
        xbc = region(12832, XBC_TILES, T)

        qT = region(0, LISTS, T)
        sc = region(4096, TT, LISTS, NKEYS)
        sc2 = region(8192, TT, LISTS, NKEYS)
        NC2 = TOPK * TOPK
        cand = region(12288, TT, PH, NC2)
        cand2 = region(16384, TT, PH, NC2)
        vv = region(20480, TT, LISTS, TOPK)
        ii = region(20992, TT, LISTS, TOPK).bitcast(u32)
        iif = region(21504, TT, LISTS, TOPK)
        tv = region(22016, TT, PH, TOPK)
        tp = region(22272, TT, PH, TOPK).bitcast(u32)
        ab = region(22528, TT, 2, PH * TOPK).bitcast(u32)
        abf = region(23040, TT, 2, PH * TOPK)
        oh = region(24576, PH, TOPK, TOPK)
        pick = region(28672, TT, 3, PH * TOPK)
        gsum = region(29440, TT, PH, 1)
        grec = region(29504, TT, PH, 1)
        G = arena[:, :].rearrange("p (i t) -> p i t", t=T)
        ytok = region(0, TT, D)
        onehot = [[ring[:, k, half * 512:(half + 1) * 512] for half in range(2)] for k in range(2)]
        xa = region(0, KC, TAPS - 1 + T)
        xc = region(2080, KC, T)
        sma = region(4128, KC, T)
        smb = region(6176, KC, T)
        rg = region(8224, KC, T)
        ig = region(10272, KC, T)
        vb = region(12320, KC, T)
        cbv = region(14368, KC, TAPS_B - 1 + T)
        bb = region(20800, KC, T)
        gg = region(22848, KC, T)
        av = region(24896, KC, T)
        th = region(16440, KC, T)
        hs = region(29100, KC, T)

        blocks = []

        def add(label, src, width=BLK, split=None):
            blocks.append((label, src, width, split))

        first = {}

        def mark(label):
            first[label] = len(blocks)

        mark("w_in")
        for j in range(24):
            add("w_in", A["w_in"][j], split="pool")
        add("w_in", A["w_dt"], KC * HEADS)
        mark("pool_w")
        add("pool_w", A["pool_w"], NPOOL * P)
        mark("w_out")
        for m in range(KC):
            add("w_out", A["w_out"][m][:, 0:BLK])
            add("w_out", A["w_out"][m][:, BLK:BLK + 4 * P], 4 * P)
        PAIRS = NKEYS // 2
        LOOPS = PAIRS // 2
        TRIPLES = (LOOPS - 2) // 3

        def peer_blocks(l):
            mark(f"wq{l}")
            for j in range(LISTS):
                add("wq", A[f"wq{l}"][j], split="dve")
            mark(f"keys{l}")
            for j in range(2):
                add("keys", A[f"keys{l}"][:, j * BLK:(j + 1) * BLK])
            mark(f"exp{l}")
            for _ in range(2 + 8 * (LOOPS - 1) + 6):
                add("exp", None, split="dve")

        peer_blocks(0)
        mark("w_in2")
        SECT = 7
        for s in range(SECT * KC):
            if s == 3 * KC:
                mark("gates2")
                for i in range(2):
                    add("gates2", A["w_gates2"][i])
                mark("w_in2b")
            add("w_in2", A["w_in2"][s], split="pool")
        mark("w_out2")
        for m in range(KC):
            add("w_out2", A["w_out2"][m], split="dve")
        peer_blocks(1)

        split_no, low_no = [], []
        seen = {"all": 0, "dve": 0, "pool": 0}
        for _, _, _, who in blocks:
            split_no.append(seen["all"])
            low_no.append(seen[who] if who else None)
            if who:
                seen["all"] += 1
                seen[who] += 1

        def slot(n):
            return n % RING

        def part_slot(n):
            return split_no[n] % RING

        def last_split(n):
            before = [m for m in range(n) if blocks[m][3]]
            return before[-RING] if len(before) >= RING else None

        def wait_parts(eng, n, turn=0):
            eng.wait_ge(S(f"low_{blocks[n][3]}"), 8 * turn + (low_no[n] + 1))

        def wait_slot(eng, n):
            m = n - RING
            if m >= 0:
                if blocks[m][3]:
                    wait_parts(eng, m)
                else:
                    eng.wait_ge(S("block_used"), m + 1)

        def make_high(act, m, q=None):
            act.wait_ge(S(f"block_in{slot(m)}"), (16 * 24 // RING) * (q if q is not None else 0) + 16 * (m // RING + 1))
            if q is not None:
                act.wait_ge(S("block_used"), 24 * q + (m - RING + 1))
            elif last_split(m) is not None:
                act.wait_ge(S("block_used"), last_split(m) + 1)
            nc.scalar.activation(ring_hi[:, part_slot(m), :], ring[:, slot(m), :],
                                 ACT.Copy).then_inc(S("high"), 1)

        def make_low(eng, ns, n, turn=0):
            eng.wait_ge(S("high"), 8 * turn + (split_no[n] + 1))
            ns.tensor_tensor(ring_lo[:, part_slot(n), :], ring[:, slot(n), :],
                             ring_hi[:, part_slot(n), :].bitcast(fp32), ALU.subtract)\
                .then_inc(S(f"low_{blocks[n][3]}"), 1)

        def full(eng, n):
            eng.wait_ge(S(f"block_in{slot(n)}"), 16 * (n // RING + 1))

        block = ctx.enter_context(nc.Block())

        @block.sync
        def _(sp):
            sp.dma_start(prm[:, :], A["prm"]).then_inc(S("prm_in"), 16)
            sp.dma_start(cst[:, :], A["cst"]).then_inc(S("cst_in"), 16)
            sp.dma_start(xT[:, :, :], A["xT"]).then_inc(S("x_in"), 16)
            sp.dma_start(inv[:, :, :], A["inv"]).then_inc(S("inv_in"), 16)

            def load(n, src, width):
                wait_slot(sp, n)
                sp.dma_start(ring[:, slot(n), 0:width], src).then_inc(S(f"block_in{slot(n)}"), 16)

            def experts(l):
                n0 = first[f"exp{l}"]
                sp.wait_ge(S(f"g_ps{l}"), T // 4)
                for k in range(2):
                    load(n0 + k, A[f"down{l}"][k], BLK)

                def turn_loads(it, steps, q=0, rows=range(8)):
                    table = [("down", 2), ("down", 3), ("up", 0), ("up", 1), ("down", 4), ("down", 5), ("up", 2),
                             ("up", 3)]
                    for k, (name, add_i) in enumerate([table[r] for r in rows]):
                        m = n0 + 2 + 8 * steps + k
                        if isinstance(q, int):
                            wait_slot(sp, m)
                            src = A[f"{name}{l}"][4 * it + add_i]
                        else:
                            sp.wait_ge(S("low_dve"), 24 * q + (low_no[m - RING] + 1))
                            src = A[f"{name}{l}"][ds(4 * it + add_i, 1), :, :].rearrange("a p n -> (a p) n")
                        sp.dma_start(ring[:, slot(m), :], src).then_inc(S(f"block_in{slot(m)}"), 16)

                turn_loads(0, 0)
                with sp.Fori(0, TRIPLES) as q:
                    for r in range(3):
                        turn_loads(3 * q + (1 + r), 1 + r, q)
                turn_loads(LOOPS - 1, LOOPS - 1, rows=(0, 1, 2, 3, 6, 7))

            n = 0
            while n < len(blocks):
                label, src, width, _ = blocks[n]
                if label == "exp":
                    l = 0 if n == first["exp0"] else 1
                    experts(l)
                    n += 2 + 8 * (LOOPS - 1) + 6
                else:
                    load(n, src, width)
                    n += 1
            sp.wait_ge(S("norm_done_fin"), 1)
            sp.dma_start(out, hT[:, :, :]).then_inc(S("out_done"), 16)
            sp.wait_ge(S("out_done"), 16)

        @block.tensor
        def _(pe):
            mm = nc.tensor.matmul

            def norm_sum(tag, bank=4):
                pe.wait_ge(S(f"sq_ready_{tag}"), 1)
                for c in range(KC):
                    last = mm(PS[bank][:, 0:T], ones, sq[:, c, :], start=(c == 0), stop=(c == KC - 1))
                last.then_inc(S(f"sumsq_{tag}"), 1)

            def ada(s):
                pe.wait_ge(S("ada_acc"), s + 1)
                if s == 2:
                    pe.wait_ge(S("ada_bias"), 2)
                for j in range(KC):
                    last = mm(PS[7][:, s * KC + j:s * KC + j + 1], ada_acc[:, s % 2, j * P:(j + 1) * P],
                              ones[:, 0:1], start=True, stop=True)
                last.then_inc(S("ada_ps"), 1)

            def product(psum, stat, move, start, stop):
                (s_hi, s_lo), (m_hi, m_lo) = stat, move
                mm(psum, s_lo, m_hi, start=start, stop=False)
                mm(psum, s_hi, m_lo, start=False, stop=False)
                return mm(psum, s_hi, m_hi, start=False, stop=stop)

            def parts(n, a, b):
                return ring_hi[:, part_slot(n), a:b], ring_lo[:, part_slot(n), a:b]

            def split_linear(n, psum, turn=0, wait=True):
                if wait:
                    wait_parts(pe, n)
                for c in range(KC):
                    last = product(psum, parts(n, c * P, (c + 1) * P), (h_hi[:, c, :], h_lo[:, c, :]),
                                   c == 0, c == KC - 1)
                last.then_inc(S("block_used"), 1)

            def linear(n, psum, src, width=P, chunks=KC):
                full(pe, n)
                for c in range(chunks):
                    last = mm(psum, ring[:, slot(n), c * width:(c + 1) * width], src[:, c, :],
                              start=(c == 0), stop=(c == chunks - 1))
                last.then_inc(S("block_used"), 1)

            pe.wait_ge(S("cst_in"), 16)
            ada(0)
            ada(1)
            norm_sum("mix")
            pe.wait_ge(S("h_split_mix"), 1)
            for j in range(24):
                if j >= 4:
                    pe.wait_ge(S("w_in_evac"), j - 3)
                split_linear(first["w_in"] + j, PS[j % 4][:, 0:T])
            pe.wait_ge(S("w_in_evac"), 21)
            linear(first["w_in"] + 24, PS[0][0:HEADS, 0:T], hT, width=HEADS)
            for s in range(2, 6):
                ada(s)

            pe.wait_ge(S("acs_ready"), 1)
            pe.wait_ge(S("dte_ready"), 1)
            for i, (row, c) in enumerate([(2, 0), (2, 1), (4, 0), (4, 1), (5, 0)]):
                last = nc.tensor.transpose(PS[4][:, i * HEADS:(i + 1) * HEADS],
                                           dts[0:HEADS, row, c * CH:(c + 1) * CH], ident[0:HEADS, 0:HEADS])
            last.then_inc(S("tok_ps"), 1)
            pe.wait_ge(S("xbc_ready"), 1)
            pe.wait_ge(S("w_in_evac"), 25)
            for b in range(4):
                for k in range(4):
                    last = nc.tensor.transpose(PS[b][:, k * P:(k + 1) * P],
                                               xbc[:, (b % 2) * 4 + k, (b // 2) * CH:(b // 2 + 1) * CH], ident)
                last.then_inc(S("xtok_ps"), 1)
            for g in range(2):
                last = nc.tensor.transpose(PS[5][:, g * P:(g + 1) * P], xbc[:, 8 + g, 0:CH], ident)
            last.then_inc(S("btok_ps"), 1)
            for g in range(2):
                for c in range(NCH):
                    k = g * NCH + c
                    last = mm(PS[6][:, k * P:(k + 1) * P], xbc[:, 8 + g, c * CH:(c + 1) * CH],
                              xbc[:, 10 + g, c * CH:(c + 1) * CH], start=True, stop=True)
            last.then_inc(S("cb_ps"), 1)
            pe.wait_ge(S("btok_ready"), 1)
            pe.wait_ge(S("xdte_ready"), 1)
            pe.wait_ge(S("tok_ready"), 1)
            for g in range(2):
                last = mm(PS[4 + g][:, :], btok[:, g, :], xdte[:, g * 512:(g + 1) * 512], start=True, stop=True)
            last.then_inc(S("st_ps"), 1)

            def head_rows(h):
                if h >= 2:
                    pe.wait_ge(S("ecs_ready"), h - 1)
                mm(PS[h % 2][:, 0:T], ident[0:HEADS, h:h + 1].to_broadcast([HEADS, P]), dts[0:HEADS, 4, :],
                   start=True, stop=True).then_inc(S("rows_ps"), 1)

            pe.wait_ge(S("xdt_ready"), 4)
            head_rows(0)
            head_rows(1)
            pe.wait_ge(S("st_ready"), 1)
            for h in range(HEADS):
                g, j = h // HPG, h // 2
                pe.wait_ge(S("mdec_ready"), h + 1)
                pe.wait_ge(S("cexp_ready"), h + 1)
                if j >= 2 and h % 2 == 0:
                    pe.wait_ge(S("y_evac"), j - 1)
                o = (h % 2) * HD
                dst = PS[2 + j % 2]
                mm(dst[o:o + HD, 0:CH], xdt[:, 0, h * HD:(h + 1) * HD], mdec[:, h % 2, 0:CH],
                   start=True, stop=True)
                mm(dst[o:o + HD, CH:2 * CH], xdt[:, 1, h * HD:(h + 1) * HD], mdec[:, h % 2, CH:2 * CH],
                   start=True, stop=False)
                mm(dst[o:o + HD, CH:2 * CH], stT[:, h * HD:(h + 1) * HD], cexp[:, h % 2, :],
                   start=False, stop=True).then_inc(S("y_ps"), 1)
                if h + 2 < HEADS:
                    head_rows(h + 2)
            n = first["pool_w"]
            full(pe, n)
            pe.wait_ge(S("pmix_ready"), 1)
            pe.wait_ge(S("st_ready"), 1)
            for g in range(NPOOL):
                last = mm(PS[6 + g // 2][:, (g % 2) * T:(g % 2 + 1) * T], ring[:, slot(n), g * P:(g + 1) * P],
                          p_mix[:, g, :], start=True, stop=True)
            last.then_inc(S("block_used"), 1)
            norm_sum("ssd")
            pe.wait_ge(S("norm_done_ssd"), 1)
            pe.wait_ge(S("pool_out"), 1)
            pe.wait_ge(S("y_evac"), 8)
            for m in range(KC):
                n = first["w_out"] + 2 * m
                if m >= 4:
                    pe.wait_ge(S("w_out_evac"), m - 3)
                full(pe, n)
                for c in range(KC):
                    last = mm(PS[m % 4][:, 0:T], ring[:, slot(n), c * P:(c + 1) * P], mixT[:, c, :],
                              start=(c == 0), stop=False)
                last.then_inc(S("block_used"), 1)
                full(pe, n + 1)
                for c in range(4):
                    last = mm(PS[m % 4][:, 0:T], ring[:, slot(n + 1), c * P:(c + 1) * P], mixT[:, KC + c, :],
                              start=False, stop=(c == 3))
                last.then_inc(S("block_used"), 1)

            def peer(l):
                norm_sum(f"ffn{l}")
                pe.wait_ge(S(f"h_split_ffn{l}"), 1)
                for j in range(LISTS):
                    if j >= 4:
                        pe.wait_ge(S(f"q_evac{l}"), j - 3)
                    split_linear(first[f"wq{l}"] + j, PS[j % 4][:, 0:T])
                pe.wait_ge(S(f"q_evac{l}"), LISTS)
                for half in range(2):
                    n = first[f"keys{l}"] + half
                    full(pe, n)
                    for tt in range(TT):
                        for q in range(2):
                            for k in range(4):
                                i = half * 8 + q * 4 + k
                                last = mm(PS[(1 - tt) * 4 + half * 2 + q][:, k * P:(k + 1) * P],
                                          qT[:, i, tt * P:(tt + 1) * P],
                                          ring[:, slot(n), (i % 8) * P:(i % 8 + 1) * P], start=True, stop=True)
                    last.then_inc(S("block_used"), 1)
                for tt in range(TT):
                    pe.wait_ge(S(f"pick_ready{l}"), tt + 1)
                    for k in range(3):
                        last = nc.tensor.transpose(PS[2 + tt][:, k * P:(k + 1) * P], pick[:, tt, k, :], ident)
                    last.then_inc(S(f"pickT_ps{l}"), 1)

                def gates(it):
                    for half in range(2):
                        pe.wait_ge(S(f"onehot{l}"), 2 * it + (half + 1))
                        if not (isinstance(it, int) and it == 0):
                            pe.wait_ge(S(f"g_evac{l}"), 2 * it + (half - 1))
                        for k in range(4):
                            last = mm(PS[half][:, k * P:(k + 1) * P], onehot[0][half][:, k * P:(k + 1) * P],
                                      onehot[1][half][:, k * P:(k + 1) * P], start=True, stop=True)
                        last.then_inc(S(f"g_ps{l}"), 1)

                gates(0)
                with pe.Fori(1, T // 8) as it:
                    gates(it)

                n0 = first[f"exp{l}"]
                b0 = n0 + 2

                def down(m, q, parity):
                    for k in range(2):
                        wait_parts(pe, m + k, 3 * q)
                        split_linear(m + k, PS[4 + parity][:, k * T:(k + 1) * T], wait=False)

                def up(m, q, parity, start=False, stop=False):
                    for k in range(2):
                        wait_parts(pe, m + k, 3 * q)
                        for tt in range(TT):
                            a = k * T + tt * P
                            for f in range(2):
                                last = product(PS[tt * 2 + f][:, :],
                                               (w_hi[:, parity, a:a + P], w_lo[:, parity, a:a + P]),
                                               parts(m + k, f * 512, (f + 1) * 512),
                                               start and k == 0, stop and k == 1)
                        last.then_inc(S("block_used"), 1)

                pe.wait_ge(S(f"pickT_ready{l}"), TT)
                pe.wait_ge(S(f"g_evac{l}"), T // 4)
                down(n0, 0, 0)

                def turn(steps, q=0):
                    m = b0 + 8 * steps
                    if steps:
                        pe.wait_ge(S(f"wf_ready{l}"), 6 * q + 2 * steps)
                    down(m, q, 1)
                    pe.wait_ge(S(f"w_ready{l}"), 6 * q + (2 * steps + 1))
                    up(m + 2, q, 0, start=steps == 0)
                    pe.wait_ge(S(f"wf_ready{l}"), 6 * q + (2 * steps + 1))
                    down(m + 4, q, 0)
                    pe.wait_ge(S(f"w_ready{l}"), 6 * q + (2 * steps + 2))
                    up(m + 6, q, 1)

                turn(0)
                with pe.Fori(0, TRIPLES) as q:
                    for r in range(3):
                        turn(1 + r, q)
                last_it = LOOPS - 1
                m = b0 + 8 * last_it
                pe.wait_ge(S(f"wf_ready{l}"), 2 * last_it)
                down(m, 0, 1)
                pe.wait_ge(S(f"w_ready{l}"), 2 * last_it + 1)
                up(m + 2, 0, 0)
                pe.wait_ge(S(f"w_ready{l}"), 2 * last_it + 2)
                up(m + 4, 0, 1, stop=True)

                for tt in range(TT):
                    pe.wait_ge(S(f"ytok_ready{l}"), 2 * tt + 2)
                    for q in range(2):
                        for k in range(4):
                            last = nc.tensor.transpose(PS[4 + tt * 2 + q][:, k * P:(k + 1) * P],
                                                       ytok[:, tt, (q * 4 + k) * P:(q * 4 + k + 1) * P], ident)
                        last.then_inc(S(f"yT_ps{l}"), 1)

            peer(0)
            norm_sum("final")
            norm_sum("mix2")
            pe.wait_ge(S("h_split_mix2"), 1)
            for s in range(SECT * KC):
                if s >= 7:
                    pe.wait_ge(S("in2_evac"), s - 6)
                if s == 3 * KC:
                    n = first["gates2"]
                    pe.wait_ge(S("xc_ready"), 1)
                    for j in range(KC):
                        if j % 4 == 0:
                            full(pe, n + j // 4)
                        if j:
                            pe.wait_ge(S("gate_evac"), j)
                        for k in range(2):
                            last = mm(PS[7][:, k * T:(k + 1) * T],
                                      ring[:, slot(n + j // 4), (j % 4 * 2 + k) * P:(j % 4 * 2 + k + 1) * P],
                                      xc[:, j, :], start=True, stop=True)
                        last.then_inc(S("block_used" if j % 4 == 3 else "gate_ps"), 1)
                n = (first["w_in2"] if s < 3 * KC else first["w_in2b"] - 3 * KC) + s
                split_linear(n, PS[s % 7][:, 0:T])
            pe.wait_ge(S("in2_evac"), SECT * KC)
            pe.wait_ge(S("h_split_merged"), 1)
            for m in range(KC):
                if m >= 4:
                    pe.wait_ge(S("w_out2_evac"), m - 3)
                split_linear(first["w_out2"] + m, PS[m % 4][:, 0:T])
            peer(1)
            norm_sum("fin")

        @block.scalar
        def _(act):
            A_ = nc.scalar.activation

            def norm_act(tag, src, sem, val, bank=4):
                act.wait_ge(S(sem), val)
                A_(sq[:, :, :], src, ACT.Square).then_inc(S(f"sq_ready_{tag}"), 1)
                act.wait_ge(S(f"sumsq_{tag}"), 1)
                A_(rstd, PS[bank][:, 0:T], ACT.Sqrt, bias=epsc[:, 0:1], scale=1.0 / D).then_inc(S(f"rms_{tag}"), 1)

            def split_h(tag, src):
                act.wait_ge(S(f"norm_done_{tag}"), 1)
                A_(h_hi[:, :, :], src, ACT.Copy).then_inc(S(f"h_high_{tag}"), 1)

            def highs(n, count, evac):
                for j in range(min(RING, count)):
                    make_high(act, n + j)
                for j in range(count):
                    if j + RING < count:
                        make_high(act, n + j + RING)
                    evac(j)

            act.wait_ge(S("prm_in"), 16)
            A_(cact[:, :], col("c", 0, 8), ACT.Silu).then_inc(S("cact_ready"), 1)
            act.wait_ge(S("eps_ready"), 1)
            norm_act("mix", xT[:, :, :], "x_in", 16)
            act.wait_ge(S("pads_ready"), 1)
            split_h("mix", hT[:, :, :])

            def evac_in(j):
                act.wait_ge(S("block_used"), first["w_in"] + j + 1)
                src = PS[j % 4][:, 0:T]
                if j < 4:
                    A_(u_pad[:, j, UPAD:], src, ACT.Copy).then_inc(S("w_in_evac"), 1)
                elif j < 12:
                    A_(zs[:, j - 4, :], src, ACT.Silu).then_inc(S("w_in_evac"), 1)
                else:
                    A_(xbc_in[:, j - 12, TAPS - 1:], src, ACT.Copy).then_inc(S("w_in_evac"), 1)

            highs(first["w_in"], 24, evac_in)
            act.wait_ge(S("block_used"), first["w_in"] + 25)
            A_(dts[0:HEADS, 0, :], PS[0][0:HEADS, 0:T], ACT.Identity,
               bias=prm[0:HEADS, COL["dt_bias"][0]:COL["dt_bias"][0] + 1]).then_inc(S("w_in_evac"), 1)
            act.wait_ge(S("w_in_evac"), 25)
            A_(dts[0:HEADS, 1, :], dts[0:HEADS, 0, :], ACT.Abs).then_inc(S("dt_abs"), 1)
            act.wait_ge(S("dt_abs"), 1)
            A_(dts[0:HEADS, 1, :], dts[0:HEADS, 1, :], ACT.Exp, scale=-1.0).then_inc(S("dt_exp"), 1)
            A_(lru_s[0:HEADS, 0, 0:1], prm[0:HEADS, COL["a_log"][0]:COL["a_log"][0] + 1], ACT.Exp)\
                .then_inc(S("alog_exp"), 1)
            act.wait_ge(S("dt_1pe"), 1)
            A_(dts[0:HEADS, 3, :], dts[0:HEADS, 2, :], ACT.Ln).then_inc(S("dt_ln"), 1)
            act.wait_ge(S("acs_ready"), 1)
            A_(dts[0:HEADS, 5, 0:CH], dts[0:HEADS, 4, 0:CH], ACT.Exp, scale=-1.0,
               bias=dts[0:HEADS, 4, CH - 1:CH]).then_inc(S("dte_ready"), 1)
            act.wait_ge(S("conv_ready"), 1)
            A_(xbc[:, :, :], xbc[:, :, :], ACT.Silu).then_inc(S("xbc_ready"), 1)
            act.wait_ge(S("btok_ps"), 1)
            A_(btok[:, :, :], PS[5][:, 0:2 * P].rearrange("p (g n) -> p g n", g=2), ACT.Copy)\
                .then_inc(S("btok_ready"), 1)
            act.wait_ge(S("cb_ps"), 1)
            A_(cbt[:, :, :], PS[6][:, :].rearrange("p (g n) -> p g n", g=2), ACT.Copy).then_inc(S("cb_ready"), 1)
            act.wait_ge(S("st_ps"), 1)
            A_(stT[:, 0:512], PS[4][:, :], ACT.Copy)
            A_(stT[:, 512:1024], PS[5][:, :], ACT.Copy).then_inc(S("st_ready"), 1)
            act.wait_ge(S("tok_ready"), 1)
            for h in range(HEADS):
                act.wait_ge(S("seg_ready"), h + 1)
                if h >= 2:
                    act.wait_ge(S("cexp_ready"), h - 1)
                    act.wait_ge(S("mdec_ready"), h - 1)
                A_(ecs[:, h % 2, :], PS[h % 2][:, CH:2 * CH], ACT.Exp).then_inc(S("ecs_ready"), 1)
                for c in range(NCH):
                    last = A_(dec[:, h % 2, c * CH:(c + 1) * CH], seg[:, h % 2, c * CH:(c + 1) * CH], ACT.Exp,
                              bias=tok[:, 2 + c, h:h + 1])
                last.then_inc(S("dec_ready"), 1)
            norm_act("ssd", mixT[:, NPOOL:, :], "y_gated", 1)

            def peer(l, x_sem, x_val):
                gelu = ACT.Gelu if l == 0 else ACT.Gelu_apprx_tanh
                norm_act(f"ffn{l}", xT[:, :, :], x_sem, x_val)
                split_h(f"ffn{l}", hT[:, :, :])

                def evac_q(j):
                    act.wait_ge(S("block_used"), first[f"wq{l}"] + j + 1)
                    A_(qT[:, j, :], PS[j % 4][:, 0:T], ACT.Copy).then_inc(S(f"q_evac{l}"), 1)

                highs(first[f"wq{l}"], LISTS, evac_q)
                for half in range(2):
                    act.wait_ge(S("block_used"), first[f"keys{l}"] + half + 1)
                    for tt in range(TT):
                        for q in range(2):
                            i = half * 8 + q * 4
                            last = A_(sc[:, tt, i:i + 4, :],
                                      PS[(1 - tt) * 4 + half * 2 + q][:, :].rearrange("p (a n) -> p a n", a=4),
                                      ACT.Copy)
                    last.then_inc(S(f"sc_ready{l}"), 1)
                for tt in range(TT):
                    act.wait_ge(S(f"gate_sub{l}"), tt + 1)
                    A_(tv[:, tt, :, :], tv[:, tt, :, :], ACT.Exp).then_inc(S(f"gate_exp{l}"), 1)

                def gates(it):
                    for half in range(2):
                        act.wait_ge(S(f"g_ps{l}"), 2 * it + (half + 1))
                        t0 = it * 8 + half * 4
                        dst = G[:, :, t0:t0 + 4] if isinstance(it, int) else G[:, :, ds(t0, 4)]
                        A_(dst, PS[half][:, :].rearrange("p (t i) -> p i t", t=4), ACT.Copy)\
                            .then_inc(S(f"g_evac{l}"), 1)

                gates(0)
                with act.Fori(1, T // 8) as it:
                    gates(it)

                n0 = first[f"exp{l}"]
                b0 = n0 + 2

                def high(m, q=None):
                    make_high(act, m, q)

                def apply_gelu(m, parity, q=0):
                    act.wait_ge(S("block_used"), 24 * q + (m + 2))
                    A_(PS[4 + parity][:, :], PS[4 + parity][:, :], gelu).then_inc(S(f"act_done{l}"), 1)

                def weights_high(pair, parity, q=0):
                    act.wait_ge(S(f"wf_ready{l}"), 6 * q + (pair + 1))
                    A_(w_hi[:, parity, :], wf[:, parity, :], ACT.Copy).then_inc(S(f"w_high{l}"), 1)

                for k in range(5):
                    high(n0 + k)
                apply_gelu(n0, 0)
                weights_high(0, 0)

                def turn(steps, q=None):
                    m, z = b0 + 8 * steps, q if q is not None else 0
                    high(m + 3, q)
                    high(m + 4, q)
                    apply_gelu(m, 1, z)
                    high(m + 5, q)
                    weights_high(2 * steps + 1, 1, z)
                    for k in (6, 7, 8):
                        high(m + k, q)
                    apply_gelu(m + 4, 0, z)
                    high(m + 9, q)
                    weights_high(2 * steps + 2, 0, z)
                    high(m + 10, q)

                turn(0)
                with act.Fori(0, TRIPLES) as q:
                    for r in range(3):
                        turn(1 + r, q)
                m = b0 + 8 * (LOOPS - 1)
                high(m + 3)
                high(m + 4)
                apply_gelu(m, 1)
                high(m + 5)
                weights_high(PAIRS - 1, 1)
                act.wait_ge(S("block_used"), m + 6)
                for tt in range(TT):
                    for f in range(2):
                        A_(ytok[:, tt, f * 512:(f + 1) * 512], PS[tt * 2 + f][:, :], ACT.Copy)\
                            .then_inc(S(f"ytok_ready{l}"), 1)

            peer(0, "w_out_evac", KC)
            norm_act("final", xT[:, :, :], "x_peer0", 1)
            norm_act("mix2", xT[:, :, :], "norm_done_final", 1)
            split_h("mix2", hT[:, :, :])
            A_(lru_s[:, 1, :], col("lam", 0, 8), ACT.Abs).then_inc(S("lam_abs"), 1)
            act.wait_ge(S("lam_abs"), 1)
            A_(lru_s[:, 1, :], lru_s[:, 1, :], ACT.Exp, scale=-1.0).then_inc(S("lam_exp"), 1)
            act.wait_ge(S("lam_1pe"), 1)
            A_(lru_s[:, 3, :], lru_s[:, 2, :], ACT.Ln).then_inc(S("lam_ln"), 1)
            act.wait_ge(S("pads2_ready"), 1)

            def w_in2_block(s):
                return (first["w_in2"] if s < 3 * KC else first["w_in2b"] - 3 * KC) + s

            for s in range(RING):
                make_high(act, w_in2_block(s))
            for s in range(SECT * KC):
                sec, j = s // KC, s % KC
                if s == 3 * KC:
                    for k in range(KC):
                        if k % 4 == 3:
                            act.wait_ge(S("block_used"), first["gates2"] + k // 4 + 1)
                        else:
                            act.wait_ge(S("gate_ps"), k - k // 4 + 1)
                        A_(rg[:, k, :], PS[7][:, 0:T], ACT.Sigmoid, bias=col("b_a", k))
                        A_(ig[:, k, :], PS[7][:, T:2 * T], ACT.Sigmoid, bias=col("b_x", k))\
                            .then_inc(S("gate_evac"), 1)
                    make_high(act, w_in2_block(s + 1))
                    make_high(act, w_in2_block(s + 2))
                if s + RING < SECT * KC and s not in (3 * KC - 2, 3 * KC - 1):
                    make_high(act, w_in2_block(s + RING))
                act.wait_ge(S("block_used"), w_in2_block(s) + 1)
                src = PS[s % 7][:, 0:T]
                dst, fn = [(xa[:, j, TAPS - 1:], ACT.Copy), (sma[:, j, :], ACT.Sigmoid), (smb[:, j, :], ACT.Sigmoid),
                           (vb[:, j, :], ACT.Copy), (cbv[:, j, TAPS_B - 1:], ACT.Copy), (bb[:, j, :], ACT.Copy),
                           (gg[:, j, :], ACT.Gelu_apprx_tanh)][sec]
                if s == 4 * KC:
                    act.wait_ge(S("lam_ready"), 1)
                    act.wait_ge(S("gate_evac"), KC)
                    for k in range(KC):
                        last = A_(av[:, k, :], rg[:, k, :], ACT.Exp, scale=lru_s[:, 4, k:k + 1])
                    last.then_inc(S("av_ready"), 1)
                    for k in range(KC):
                        last = A_(th[:, k, :], rg[:, k, :], ACT.Tanh, scale=lru_s[:, 5, k:k + 1])
                    last.then_inc(S("th_ready"), 1)
                if s == 5 * KC:
                    act.wait_ge(S("mult_sq"), 1)
                    A_(th[:, :, :], th[:, :, :], ACT.Sqrt).then_inc(S("mult_ready"), 1)
                A_(dst, src, fn).then_inc(S("in2_evac"), 1)
            split_h("merged", gg[:, :, :])
            highs(first["w_out2"], KC, lambda j: None)
            peer(1, "w_out2_evac", KC)
            norm_act("fin", xT[:, :, :], "x_peer1", 1)

        @block.vector
        def _(dve):
            v = nc.vector
            counts = {}

            def link(ins, signal="dve_chain", by=1):
                counts[signal] = counts.get(signal, 0) + by
                ins.then_inc(S(signal), by)
                dve.wait_ge(S(signal), counts[signal])

            TTn, TS, STT = v.tensor_tensor, v.tensor_scalar, v.scalar_tensor_tensor

            def norm_dve(tag, src, dst, scale, shift=None):
                dve.wait_ge(S(f"rms_{tag}"), 1)
                link(v.reciprocal(rstd, rstd))
                link(TTn(dst, src, rstd[:, None, :].to_broadcast([P, KC, T]), ALU.mult))
                for c in range(KC):
                    d = dst[:, c, :]
                    if shift is None:
                        last = TS(d, d, scale(c), None, ALU.mult)
                    else:
                        last = TS(d, d, scale(c), shift(c), ALU.mult, ALU.add)
                link(last, f"norm_done_{tag}")

            def split_low(tag, src):
                dve.wait_ge(S(f"h_high_{tag}"), 1)
                link(TTn(h_lo[:, :, :], src, h_hi[:, :, :].bitcast(fp32), ALU.subtract), f"h_split_{tag}")

            def ada(s):
                dve.wait_ge(S(f"ada_in{s % 2}"), 16 * (s // 2 + 1))
                if s >= 2:
                    dve.wait_ge(S("ada_ps"), s - 1)
                w = ada_buf[:, s % 2, :].rearrange("p (c n) -> p c n", c=KC)
                acc = ada_acc[:, s % 2, :]
                link(TS(acc, w[:, 0, :], cact[:, 0:1], None, ALU.mult))
                for c in range(1, KC):
                    link(STT(acc, w[:, c, :], cact[:, c:c + 1], acc, ALU.mult, ALU.add),
                         "ada_acc" if c == KC - 1 else "dve_chain")

            def ada_out(s):
                dve.wait_ge(S("ada_ps"), 2 if s < 2 else 6)
                m = mod[:, s * KC:(s + 1) * KC]
                link(TTn(m, PS[7][:, s * KC:(s + 1) * KC], col("b_ada", s * KC, KC), ALU.add), "ada_bias")
                if s in (1, 4):
                    link(STT(m, m, 1.0, col("norm_mix" if s == 1 else "norm_ffn", 0, KC), ALU.add, ALU.mult))

            link(v.memset(epsc[:, :], EPS), "eps_ready")
            v.memset(u_pad[:, :, 0:UPAD], 0.0)
            link(v.memset(xbc_in[:, :, 0:TAPS - 1], 0.0), "pads_ready")
            dve.wait_ge(S("prm_in"), 16)
            dve.wait_ge(S("cact_ready"), 1)
            ada(0)
            ada(1)
            ada_out(0)
            ada_out(1)
            norm_dve("mix", xT[:, :, :], hT[:, :, :], lambda c: mod[:, KC + c:KC + c + 1], lambda c: mod[:, c:c + 1])
            split_low("mix", hT[:, :, :])
            for s in range(2, 6):
                ada(s)
            link(v.memset(p_sum[:, :, 0:UPAD], 0.0), "ada_free")
            dve.wait_ge(S("w_in_evac"), 24)
            for j in range(XBC_TILES):
                last = TS(xbc[:, j, :], xbc_in[:, j, 0:T], col("conv_w", j), col("conv_b", j), ALU.mult, ALU.add)
            link(last)
            for k in range(1, TAPS):
                for j in range(XBC_TILES):
                    last = STT(xbc[:, j, :], xbc_in[:, j, k:k + T], col("conv_w", k * XBC_TILES + j), xbc[:, j, :],
                               ALU.mult, ALU.add)
                link(last, "conv_ready" if k == TAPS - 1 else "dve_chain")

            def softplus_u(e, u, sem_in, sem_out):
                dve.wait_ge(S(sem_in), 1)
                link(TS(u, e, 1.0, None, ALU.add), sem_out)

            def log1p(e, u, ln, tmp):
                link(TS(u, u, -1.0, None, ALU.add))
                link(TS(tmp, u, 0.0, None, ALU.is_equal))
                link(TTn(u, u, tmp, ALU.add))
                link(v.reciprocal(u, u))
                link(TTn(u, u, ln, ALU.mult))
                link(TTn(u, u, tmp, ALU.add))
                link(TTn(ln, u, e, ALU.mult))

            H16 = slice(0, HEADS)
            softplus_u(dts[H16, 1, :], dts[H16, 2, :], "dt_exp", "dt_1pe")
            dve.wait_ge(S("dt_ln"), 1)
            log1p(dts[H16, 1, :], dts[H16, 2, :], dts[H16, 3, :], dts[H16, 4, :])
            link(STT(dts[H16, 2, :], dts[H16, 0, :], 0.0, dts[H16, 3, :], ALU.max, ALU.add))
            dve.wait_ge(S("alog_exp"), 1)
            link(TS(dts[H16, 3, :], dts[H16, 2, :], lru_s[H16, 0, 0:1], -1.0, ALU.mult, ALU.mult))
            for c in range(NCH):
                last = v.tensor_tensor_scan(dts[H16, 4, c * CH:(c + 1) * CH], cst[H16, CONES:CONES + CH],
                                            dts[H16, 3, c * CH:(c + 1) * CH], 0.0, ALU.mult, ALU.add)
            link(last, "acs_ready")
            dve.wait_ge(S("tok_ps"), 1)
            v.tensor_copy(tok[:, 0:2, :], PS[4][:, 0:2 * HEADS].rearrange("p (a h) -> p a h", a=2))
            TS(tok[:, 2:4, :], PS[4][:, 2 * HEADS:4 * HEADS].rearrange("p (a h) -> p a h", a=2), -1.0, None, ALU.mult)
            link(v.tensor_copy(tok[:, 4, :], PS[4][:, 4 * HEADS:5 * HEADS]), "tok_ready")
            for b in range(4):
                c, hf = b // 2, b % 2
                dve.wait_ge(S("xtok_ps"), b + 1)
                last = TTn(xdt[:, c, hf * 512:(hf + 1) * 512].rearrange("p (h d) -> p h d", d=HD),
                           PS[b][:, :].rearrange("p (h d) -> p h d", d=HD),
                           tok[:, c, hf * HPG:(hf + 1) * HPG][:, :, None].to_broadcast([P, HPG, HD]), ALU.mult)
                link(last, "xdt_ready")
            link(TTn(xdte.rearrange("p (h d) -> p h d", d=HD), xdt[:, 0, :].rearrange("p (h d) -> p h d", d=HD),
                     tok[:, 4, :][:, :, None].to_broadcast([P, HEADS, HD]), ALU.mult), "xdte_ready")
            dve.wait_ge(S("cb_ready"), 1)
            for s in range(2, 6):
                ada_out(s)

            def seg_head(h):
                dve.wait_ge(S("rows_ps"), h + 1)
                if h >= 2:
                    dve.wait_ge(S("dec_ready"), h - 1)
                TTn(seg[:, h % 2, :].rearrange("p (c l) -> p c l", c=NCH),
                    PS[h % 2][:, 0:T].rearrange("p (c l) -> p c l", c=NCH),
                    mask[:, None, :].to_broadcast([P, NCH, CH]), ALU.add).then_inc(S("seg_ready"), 1)

            def y_pair(j):
                dve.wait_ge(S("y_ps"), 2 * j + 2)
                STT(mixT[:, NPOOL + j, :], xbc[:, j, :], col("d_skip", j), PS[2 + j % 2][:, 0:T],
                    ALU.mult, ALU.add).then_inc(S("y_evac"), 1)

            seg_head(0)
            for h in range(HEADS):
                if h + 1 < HEADS:
                    seg_head(h + 1)
                g = h // HPG
                dve.wait_ge(S("ecs_ready"), h + 1)
                if h >= 2:
                    dve.wait_ge(S("y_ps"), h - 1)
                TTn(cexp[:, h % 2, :], xbc[:, 10 + g, CH:2 * CH], ecs[:, h % 2, :], ALU.mult)\
                    .then_inc(S("cexp_ready"), 1)
                dve.wait_ge(S("dec_ready"), h + 1)
                TTn(mdec[:, h % 2, :], dec[:, h % 2, :], cbt[:, g, :], ALU.mult).then_inc(S("mdec_ready"), 1)
                if h % 2 == 1 and h >= 3:
                    y_pair(h // 2 - 1)
            y_pair(HEADS // 2 - 1)
            dve.wait_ge(S("y_evac"), HEADS // 2)
            link(TTn(mixT[:, NPOOL:, :], mixT[:, NPOOL:, :], zs[:, :, :], ALU.mult), "y_gated")
            dve.wait_ge(S("block_used"), first["pool_w"] + 1)
            for g in range(NPOOL):
                last = TS(mixT[:, g, :], PS[6 + g // 2][:, (g % 2) * T:(g % 2 + 1) * T], col("pool_b", g),
                          col("pool_scale", g), ALU.add, ALU.mult)
            last.then_inc(S("pool_out"), 1)
            norm_dve("ssd", mixT[:, NPOOL:, :], mixT[:, NPOOL:, :], lambda c: col("ssd_norm", c))
            for m in range(KC):
                dve.wait_ge(S("block_used"), first["w_out"] + 2 * m + 2)
                STT(xT[:, m, :], PS[m % 4][:, 0:T], mod[:, 2 * KC + m:2 * KC + m + 1], xT[:, m, :],
                    ALU.mult, ALU.add).then_inc(S("w_out_evac"), 1)
            dve.wait_ge(S("w_out_evac"), KC)

            def top16(src, src2, vals, idx, rows, finish):
                for r in rows:
                    last = v.max(vals(r)[:, 0:8], src(r))
                link(last)
                for r in rows:
                    last = v.max_index(idx(r)[:, 0:8], vals(r)[:, 0:8], src(r))
                for r in rows:
                    last = v.match_replace(src2(r), vals(r)[:, 0:8], src(r), LOWEST)
                link(last)
                for r in rows:
                    last = v.max(vals(r)[:, 8:16], src2(r))
                link(last)
                for r in rows:
                    last = v.max_index(idx(r)[:, 8:16], vals(r)[:, 8:16], src2(r))
                link(last, finish)

            def peer(l, scale, shift):
                norm_dve(f"ffn{l}", xT[:, :, :], hT[:, :, :], scale, shift)
                split_low(f"ffn{l}", hT[:, :, :])
                for j in range(LISTS):
                    make_low(dve, v, first[f"wq{l}"] + j)
                dve.wait_ge(S(f"sc_ready{l}"), 2)
                for tt in range(TT):
                    top16(lambda r: sc[:, tt, r, :], lambda r: sc2[:, tt, r, :], lambda r: vv[:, tt, r, :],
                          lambda r: ii[:, tt, r, :], range(LISTS), "dve_chain")
                    link(v.tensor_copy(iif[:, tt, :, :], ii[:, tt, :, :]))
                    v4 = vv[:, tt, :, :].rearrange("p (h s) k -> p h s k", s=2)
                    for h in range(PH):
                        last = TTn(cand[:, tt, h, :].rearrange("p (a b) -> p a b", a=TOPK),
                                   v4[:, h, 0, :][:, :, None].to_broadcast([P, TOPK, TOPK]),
                                   v4[:, h, 1, :][:, None, :].to_broadcast([P, TOPK, TOPK]), ALU.add)
                    link(last)
                    top16(lambda r: cand[:, tt, r, :], lambda r: cand2[:, tt, r, :], lambda r: tv[:, tt, r, :],
                          lambda r: tp[:, tt, r, :], range(PH), "dve_chain")
                    pos = tp[:, tt, :, :].rearrange("p h k -> p (h k)")
                    TS(ab[:, tt, 0, :], pos, 4, None, ALU.logical_shift_right)
                    link(TS(ab[:, tt, 1, :], pos, TOPK - 1, None, ALU.bitwise_and))
                    link(v.tensor_copy(abf[:, tt, :, :], ab[:, tt, :, :]))
                    link(TTn(pick[:, tt, 2, :].rearrange("p (h k) -> p h k", h=PH), tv[:, tt, :, :],
                             tv[:, tt, :, 0:1].to_broadcast([P, PH, TOPK]), ALU.subtract))
                    link(v.tensor_copy(tv[:, tt, :, :], pick[:, tt, 2, :].rearrange("p (h k) -> p h k", h=PH)),
                         f"gate_sub{l}")
                    i4 = iif[:, tt, :, :].rearrange("p (h s) k -> p h s k", s=2)
                    for s in range(2):
                        rk = abf[:, tt, s, :]
                        link(TTn(oh[:, :, :, :].rearrange("p h k a -> p (h k) a"),
                                 rk[:, :, None].to_broadcast([P, PH * TOPK, TOPK]),
                                 iota[:, None, 0:TOPK].to_broadcast([P, PH * TOPK, TOPK]), ALU.is_equal))
                        for h in range(PH):
                            last = TTn(oh[:, h, :, :], oh[:, h, :, :],
                                       i4[:, h, s, :][:, None, :].to_broadcast([P, TOPK, TOPK]), ALU.mult)
                        link(last)
                        link(v.tensor_reduce(pick[:, tt, s, :], oh[:, :, :, :].rearrange("p h k a -> p (h k) a"),
                                             AX.X, ALU.add))
                    dve.wait_ge(S(f"gate_exp{l}"), tt + 1)
                    link(v.tensor_reduce(gsum[:, tt, :, 0], tv[:, tt, :, :], AX.X, ALU.add))
                    link(v.reciprocal(grec[:, tt, :, :], gsum[:, tt, :, :]))
                    link(TTn(pick[:, tt, 2, :].rearrange("p (h k) -> p h k", h=PH), tv[:, tt, :, :],
                             grec[:, tt, :, :].to_broadcast([P, PH, TOPK]), ALU.mult), f"pick_ready{l}")
                for tt in range(TT):
                    dve.wait_ge(S(f"pickT_ps{l}"), tt + 1)
                    link(v.tensor_copy(selT[:, :, tt * P:(tt + 1) * P],
                                       PS[2 + tt][:, 0:3 * P].rearrange("p (a t) -> p a t", a=3)), f"pickT_ready{l}")

                def gates(it, is_first):
                    src = selT[:, :, 0:8] if is_first else selT[:, :, ds(it * 8, 8)]
                    if not is_first:
                        dve.wait_ge(S(f"onehot{l}"), 2 * it)
                    v.tensor_copy(stage[:, :, :], src).then_inc(S(f"stage{l}"), 1)
                    dve.wait_ge(S(f"stage{l}"), it + 1)
                    for half in range(2):
                        if not is_first:
                            dve.wait_ge(S(f"g_ps{l}"), 2 * it + (half - 1))
                        for k in range(4):
                            t = half * 4 + k
                            TS(onehot[0][half][:, k * P:(k + 1) * P], iota, stage[:, 0, t:t + 1], None,
                               ALU.is_equal)
                            last = TS(onehot[1][half][:, k * P:(k + 1) * P], iota, stage[:, 1, t:t + 1],
                                      stage[:, 2, t:t + 1], ALU.is_equal, ALU.mult)
                        last.then_inc(S(f"onehot{l}"), 1)

                gates(0, True)
                with dve.Fori(1, T // 8) as it:
                    gates(it, False)

                n0 = first[f"exp{l}"]
                b0 = n0 + 2

                def low(m, q=0):
                    make_low(dve, v, m, 3 * q)

                def weigh(pair, parity, q=0):
                    dve.wait_ge(S(f"act_done{l}"), 6 * q + (pair + 1))
                    i2 = 12 * q + 2 * pair
                    g2 = G[:, i2:i2 + 2, :] if isinstance(i2, int) else G[:, ds(i2, 2), :]
                    TTn(wf[:, parity, :].rearrange("p (i t) -> p i t", i=2),
                        PS[4 + parity][:, :].rearrange("p (i t) -> p i t", i=2), g2, ALU.mult)\
                        .then_inc(S(f"wf_ready{l}"), 1)

                def weights_low(pair, parity, q=0):
                    dve.wait_ge(S(f"w_high{l}"), 6 * q + (pair + 1))
                    TTn(w_lo[:, parity, :], wf[:, parity, :], w_hi[:, parity, :].bitcast(fp32), ALU.subtract)\
                        .then_inc(S(f"w_ready{l}"), 1)

                dve.wait_ge(S(f"g_evac{l}"), T // 4)
                for k in range(5):
                    low(n0 + k)
                weigh(0, 0)
                weights_low(0, 0)

                def turn(steps, q=0):
                    m = b0 + 8 * steps
                    low(m + 3, q)
                    low(m + 4, q)
                    weigh(2 * steps + 1, 1, q)
                    low(m + 5, q)
                    weights_low(2 * steps + 1, 1, q)
                    for k in (6, 7, 8):
                        low(m + k, q)
                    weigh(2 * steps + 2, 0, q)
                    low(m + 9, q)
                    weights_low(2 * steps + 2, 0, q)
                    low(m + 10, q)

                turn(0)
                with dve.Fori(0, TRIPLES) as q:
                    for r in range(3):
                        turn(1 + r, q)
                m = b0 + 8 * (LOOPS - 1)
                low(m + 3)
                low(m + 4)
                weigh(PAIRS - 1, 1)
                low(m + 5)
                weights_low(PAIRS - 1, 1)
                for tt in range(TT):
                    for q in range(2):
                        dve.wait_ge(S(f"yT_ps{l}"), tt * 2 + q + 1)
                        for k in range(4):
                            c = q * 4 + k
                            d = xT[:, c, tt * P:(tt + 1) * P]
                            src = PS[4 + tt * 2 + q][:, k * P:(k + 1) * P]
                            if l == 0:
                                last = STT(d, src, mod[:, 5 * KC + c:5 * KC + c + 1], d, ALU.mult, ALU.add)
                            else:
                                last = TTn(d, src, d, ALU.add)
                link(last, f"x_peer{l}")

            peer(0, lambda c: mod[:, 4 * KC + c:4 * KC + c + 1], lambda c: mod[:, 3 * KC + c:3 * KC + c + 1])
            norm_dve("final", xT[:, :, :], xT[:, :, :], lambda c: col("norm_final", c))
            norm_dve("mix2", xT[:, :, :], hT[:, :, :], lambda c: col("norm1", c))
            split_low("mix2", hT[:, :, :])
            v.memset(xa[:, :, 0:TAPS - 1], 0.0)
            link(v.memset(cbv[:, :, 0:TAPS_B - 1], 0.0), "pads2_ready")
            softplus_u(lru_s[:, 1, :], lru_s[:, 2, :], "lam_exp", "lam_1pe")
            dve.wait_ge(S("lam_ln"), 1)
            log1p(lru_s[:, 1, :], lru_s[:, 2, :], lru_s[:, 3, :], lru_s[:, 6, :])
            link(TS(lru_s[:, 2, :], col("lam", 0, 8), -1.0, 0.0, ALU.mult, ALU.max))
            link(TTn(lru_s[:, 3, :], lru_s[:, 3, :], lru_s[:, 2, :], ALU.add))
            link(TS(lru_s[:, 4, :], lru_s[:, 3, :], -8.0, None, ALU.mult))
            link(TS(lru_s[:, 5, :], lru_s[:, 3, :], 8.0, None, ALU.mult), "lam_ready")

            def conv(dst, src, name, bias, taps):
                for j in range(KC):
                    if bias:
                        last = TS(dst[:, j, :], src[:, j, 0:T], col(name, j), col(bias, j), ALU.mult, ALU.add)
                    else:
                        last = TS(dst[:, j, :], src[:, j, 0:T], col(name, j), None, ALU.mult)
                link(last)
                for k in range(1, taps):
                    for j in range(KC):
                        last = STT(dst[:, j, :], src[:, j, k:k + T], col(name, k * KC + j), dst[:, j, :],
                                   ALU.mult, ALU.add)
                    if k < taps - 1:
                        link(last)
                return last

            dve.wait_ge(S("in2_evac"), KC)
            link(conv(xc, xa, "conv_a_w", "conv_a_b", TAPS), "xc_ready")
            dve.wait_ge(S("av_ready"), 1)
            link(TTn(hs[:, :, :], av[:, :, :], av[:, :, :], ALU.mult))
            dve.wait_ge(S("th_ready"), 1)
            link(STT(th[:, :, :].rearrange("p a b -> p (a b)"), hs[:, :, :].rearrange("p a b -> p (a b)"), 1.0,
                     th[:, :, :].rearrange("p a b -> p (a b)"), ALU.add, ALU.mult), "mult_sq")
            link(TTn(ig[:, :, :], ig[:, :, :], xc[:, :, :], ALU.mult))
            dve.wait_ge(S("mult_ready"), 1)
            link(TTn(ig[:, :, :], ig[:, :, :], th[:, :, :], ALU.mult))
            for j in range(KC):
                last = v.tensor_tensor_scan(hs[:, j, :], av[:, j, :], ig[:, j, :], 0.0, ALU.mult, ALU.add)
            link(last)
            link(TTn(hs[:, :, :], hs[:, :, :], sma[:, :, :], ALU.mult))
            dve.wait_ge(S("in2_evac"), 5 * KC)
            link(TTn(cbv[:, :, TAPS_B - 1:], cbv[:, :, TAPS_B - 1:], vb[:, :, :], ALU.mult))
            link(conv(rg, cbv, "conv_b_w", None, TAPS_B))
            link(TTn(rg[:, :, :], rg[:, :, :], smb[:, :, :], ALU.mult))
            dve.wait_ge(S("in2_evac"), 6 * KC)
            link(TTn(rg[:, :, :], rg[:, :, :], bb[:, :, :], ALU.mult))
            dve.wait_ge(S("in2_evac"), 7 * KC)
            link(TTn(gg[:, :, :], gg[:, :, :], hs[:, :, :], ALU.mult))
            link(TTn(gg[:, :, :], gg[:, :, :], rg[:, :, :], ALU.add), "norm_done_merged")
            split_low("merged", gg[:, :, :])
            for m in range(RING):
                make_low(dve, v, first["w_out2"] + m)
            for m in range(KC):
                if m + RING < KC:
                    make_low(dve, v, first["w_out2"] + m + RING)
                dve.wait_ge(S("block_used"), first["w_out2"] + m + 1)
                TTn(xT[:, m, :], PS[m % 4][:, 0:T], xT[:, m, :], ALU.add).then_inc(S("w_out2_evac"), 1)
            dve.wait_ge(S("w_out2_evac"), KC)
            peer(1, lambda c: col("norm2", c), None)
            norm_dve("fin", xT[:, :, :], hT[:, :, :], lambda c: col("final", c))

        @block.gpsimd
        def _(pool):
            for s in range(6):
                if s >= 2:
                    pool.wait_ge(S("ada_acc"), s - 1)
                pool.dma_start(ada_buf[:, s % 2, :], A["w_ada"][s]).then_inc(S(f"ada_in{s % 2}"), 16)
            for j in range(24):
                make_low(pool, nc.gpsimd, first["w_in"] + j)
            pool.wait_ge(S("w_in_evac"), 4)
            pool.wait_ge(S("ada_free"), 1)
            pool.wait_ge(S("inv_in"), 16)
            g_ = nc.gpsimd
            n = 0

            def link(ins):
                nonlocal n
                n += 1
                ins.then_inc(S("pool_chain"), 1)
                pool.wait_ge(S("pool_chain"), n)

            for g, w in enumerate(POOL_W):
                cur, half = u_pad[:, g, :], 0
                step = 1
                while step < w:
                    dst = p_sum[:, half, :]
                    link(g_.tensor_tensor(dst[:, UPAD:], cur[:, UPAD:], cur[:, UPAD - step:UPAD - step + T], ALU.add))
                    cur, half, step = dst, 1 - half, step * 2
                link(g_.tensor_tensor(p_t[:, g, :], cur[:, UPAD:], inv[:, g, :], ALU.mult))
                ins = g_.tensor_tensor(p_mix[:, g, :], p_t[:, g, :], u_pad[:, g, UPAD:], ALU.subtract)
                if g == NPOOL - 1:
                    ins.then_inc(S("pmix_ready"), 1)
                else:
                    link(ins)
            for s in range(SECT * KC):
                make_low(pool, nc.gpsimd, (first["w_in2"] if s < 3 * KC else first["w_in2b"] - 3 * KC) + s)


def _chunks(w, n):
    k, m = w.shape
    return np.ascontiguousarray(w.reshape(k // P, P, m // n, n).transpose(2, 1, 0, 3)).reshape(m // n, P, -1)


def _columns(v):
    return np.ascontiguousarray(v.reshape(-1, P).T)


def kernel(**inputs):
    import concourse.bacc as bacc
    from concourse.bass_utils import run_bass_kernel_spmd

    I = {k: np.asarray(v) for k, v in inputs.items()}
    f = np.float32
    prm = {
        "c": _columns(I["c"][0]), "b_ada": _columns(I["b_ada"][0]), "norm_mix": _columns(I["norm_mix"][0]),
        "norm_ffn": _columns(I["norm_ffn"][0]), "pool_b": _columns(I["pool_b"][0]),
        "pool_scale": _columns(I["pool_scale"][0]), "conv_w": _columns(I["conv_w"][0]),
        "conv_b": _columns(I["conv_b"][0]), "d_skip": _columns(np.repeat(I["d_skip"][0], HD)),
        "ssd_norm": _columns(I["ssd_norm"][0]), "norm_final": _columns(I["norm_final"]),
        "dt_bias": np.pad(I["dt_bias"][0], (0, P - HEADS))[:, None],
        "a_log": np.pad(I["a_log"][0], (0, P - HEADS))[:, None],
        "norm1": _columns(I["norm1_g_2"][0]), "conv_a_w": _columns(I["conv_a_w_2"][0]),
        "conv_a_b": _columns(I["conv_a_b_2"][0]), "b_a": _columns(I["b_a_2"][0]), "b_x": _columns(I["b_x_2"][0]),
        "lam": _columns(I["lru_lambda_2"][0]), "conv_b_w": _columns(I["conv_b_w_2"][0]),
        "norm2": _columns(I["norm2_g_2"][0]), "final": _columns(I["final_g_2"]),
    }
    cst = np.zeros((P, NCONST), f)
    cst[:, CIDENT:CIDENT + P] = np.eye(P)
    cst[:, CONES:CONES + P] = 1.0
    cst[:, CMASK:CMASK + P] = np.where(np.arange(P)[:, None] <= np.arange(P)[None, :], 0.0, -1e38)
    cst[:, CIOTA:CIOTA + P] = np.arange(P)
    inv = np.zeros((P, NPOOL, T), f)
    for g, w in enumerate(POOL_W):
        inv[:, g] = 1.0 / np.minimum(np.arange(T) + 1, w)

    w_in = I["w_in"][0]
    w_in2 = I["w_in_2"][0].reshape(D, 7, D)[:, [0, 5, 6, 2, 4, 3, 1]].reshape(D, 7 * D)
    keys0 = np.stack([I["sub_keys1"][0], I["sub_keys2"][0]], axis=1)
    keys1 = I["peer_subkeys_2"][0]

    def down(t):
        return np.ascontiguousarray(t.reshape(NKEYS, NKEYS, KC, P).transpose(1, 3, 2, 0)).reshape(NKEYS, P, D)

    def up(t):
        return np.ascontiguousarray(t.reshape(NKEYS, NKEYS, D).transpose(1, 0, 2))

    def keys(k):
        return np.ascontiguousarray(k.reshape(LISTS, NKEYS, P).transpose(2, 0, 1)).reshape(P, LISTS * NKEYS)

    def heads(a, x):
        w = np.stack([a, x], axis=1).reshape(2, 4, 2, P, P)
        return np.ascontiguousarray(w.transpose(0, 3, 1, 2, 4)).reshape(2, P, BLK)

    arrays = {
        "prm": np.concatenate([prm[n] for n, _ in _COLS], axis=1),
        "cst": cst, "inv": inv,
        "xT": I["x"][0].T.reshape(KC, P, T).transpose(1, 0, 2),
        "w_ada": I["w_ada"][0].reshape(KC, P, 6, D).transpose(2, 1, 0, 3).reshape(6, P, KC * D),
        "w_in": _chunks(w_in[:, :24 * P], P), "w_dt": _chunks(w_in[:, 24 * P:], HEADS)[0],
        "pool_w": I["pool_w"][0].transpose(1, 0, 2).reshape(P, NPOOL * P),
        "w_out": _chunks(I["w_out"][0], P),
        "wq0": _chunks(I["w_query"][0], P), "keys0": keys(keys0),
        "down0": down(I["expert_down"][0]), "up0": up(I["expert_up"][0]),
        "w_in2": _chunks(w_in2, P), "w_gates2": heads(I["w_a_2"][0], I["w_x_2"][0]),
        "w_out2": _chunks(I["w_out_2"][0], P),
        "wq1": _chunks(I["peer_wq_2"][0], P), "keys1": keys(keys1),
        "down1": down(I["peer_u_2"][0]), "up1": up(I["peer_v_2"][0]),
    }
    nc = bacc.Bacc("TRN2", target_bir_lowering=False, num_devices=1)
    feed, A = {}, {}
    for name, a in arrays.items():
        a = np.ascontiguousarray(a)
        feed[f"in_{name}"] = a
        A[name] = nc.dram_tensor(f"in_{name}", a.shape, mybir.dt.from_np(a.dtype), kind="ExternalInput").ap()
    out = nc.dram_tensor("out", (P, KC, T), mybir.dt.float32, kind="ExternalOutput").ap()
    decoder_kernel(nc, A, out)
    r = run_bass_kernel_spmd(nc, [feed], core_ids=[0])
    y = r.results[0]["out"]
    return np.ascontiguousarray(y.transpose(2, 1, 0)).reshape(1, T, D)
```

```python
import numpy as np
import concourse.bass as bass
from concourse import mybir
from contextlib import ExitStack

P = 128
D = 1024
KC = D // P
T = 256
TT = T // P
POOL_W = (2, 4, 8, 16)
NPOOL = len(POOL_W)
UPAD = max(POOL_W)
SSD_TILES = 8
XBC_TILES = 12
HEADS = 16
HPG = 8
HD = 64
CH = 128
NCH = T // CH
TAPS = 4
TAPS_B = 3
PH = 8
LISTS = 2 * PH
TOPK = 16
NKEYS = 128
EPS = 1e-6
RING = 3
BLK = KC * P
LOWEST = -3.0e38

_COLS = [("c", 8), ("b_ada", 48), ("norm_mix", 8), ("norm_ffn", 8), ("pool_b", 4), ("pool_scale", 4),
         ("conv_w", 48), ("conv_b", 12), ("d_skip", 8), ("ssd_norm", 8), ("norm_final", 8), ("dt_bias", 1),
         ("a_log", 1), ("norm1", 8), ("conv_a_w", 32), ("conv_a_b", 8), ("b_a", 8), ("b_x", 8), ("lam", 8),
         ("conv_b_w", 24), ("norm2", 8), ("final", 8)]
COL = {}
_at = 0
for _n, _w in _COLS:
    COL[_n] = (_at, _w)
    _at += _w
NCOL = _at
CIDENT, CONES, CMASK, CIOTA = 0, P, 2 * P, 3 * P
NCONST = 4 * P


def decoder_kernel(nc, A, out):
    fp32 = mybir.dt.float32
    fp32r = mybir.dt.float32r
    u32 = mybir.dt.uint32
    ALU = mybir.AluOpType
    ACT = mybir.ActivationFunctionType
    AX = mybir.AxisListType
    ds = bass.ds

    ctx = ExitStack()
    with ctx:
        def sb(name, shape, dt=fp32):
            return ctx.enter_context(nc.sbuf_tensor(name, shape, dt))

        sems = {}

        def S(name):
            if name not in sems:
                sems[name] = ctx.enter_context(nc.semaphore(name))
            return sems[name]

        NORMS = ["mix", "ssd", "ffn0", "final", "mix2", "ffn1", "fin"]
        NORMED = ["mix", "ssd", "ffn0", "final", "mix2", "merged", "ffn1", "fin"]
        SPLITS = ["mix", "ffn0", "mix2", "merged", "ffn1"]

        def normed(eng, tag):
            eng.wait_ge(S("norm_done"), NORMED.index(tag) + 1)

        def split_ready(eng, tag):
            eng.wait_ge(S("h_split"), SPLITS.index(tag) + 1)

        xT = sb("xT", [P, KC, T])
        h_hi = sb("h_hi", [P, KC, T], fp32r)
        h_lo = sb("h_lo", [P, KC, T], fp32r)
        prm = sb("prm", [P, NCOL])
        cst = sb("cst", [P, NCONST])
        ring = sb("ring", [P, RING, BLK])
        ring_hi = sb("ring_hi", [P, RING, BLK], fp32r)
        ring_lo = sb("ring_lo", [P, RING, BLK], fp32r)
        arena = sb("arena", [P, 32768])
        wf = sb("wf", [P, 2, 512])
        w_hi = sb("w_hi", [P, 2, 512], fp32r)
        w_lo = sb("w_lo", [P, 2, 512], fp32r)
        selT = sb("selT", [P, 3, T])
        stage = sb("stage", [P, 3, 8])
        mod = sb("mod", [P, 48])
        cact = sb("cact", [P, 8])
        lru_s = sb("lru_s", [P, 8, 8])
        epsc = sb("epsc", [P, 1])
        PS = [ctx.enter_context(nc.psum_tensor(f"ps{i}", [P, 512], fp32)) for i in range(8)]

        ident = cst[:, CIDENT:CIDENT + P]
        ones = cst[:, CONES:CONES + P]
        mask = cst[:, CMASK:CMASK + P]
        iota = cst[:, CIOTA:CIOTA + P]

        def col(name, i, n=1):
            a = COL[name][0] + i
            return prm[:, a:a + n]

        def region(at, *shape):
            n = int(np.prod(shape))
            v = arena[:, at:at + n]
            if len(shape) == 2:
                return v.rearrange("p (a b) -> p a b", b=shape[1])
            if len(shape) == 3:
                return v.rearrange("p (a b c) -> p a b c", b=shape[1], c=shape[2])
            return v

        ada_buf = region(0, 2, KC * D)
        ada_acc = region(16384, 2, D)
        sq = region(18432, KC, T)
        rstd = region(20480, T)
        u_pad = region(20736, NPOOL, UPAD + T)
        zs = region(21824, KC, T)
        xbc_in = region(23872, XBC_TILES, TAPS - 1 + T)
        hT = region(26980, KC, T)
        inv = region(29028, NPOOL, T)
        dts = region(30052, 6, T)
        xdt = region(0, NCH, D)
        xdte = region(2048, D)
        btok = region(3072, 2, P)
        cbt = region(3328, 2, NCH * P)
        stT = region(3840, D)
        mixT = region(4864, NPOOL + SSD_TILES, T)
        tok = region(7936, 5, HEADS)
        seg = region(8192, 2, T)
        dec = region(8704, 2, T)
        mdec = region(9216, 2, T)
        ecs = region(9728, 2, P)
        cexp = region(9984, 2, P)
        p_sum = region(10240, 2, UPAD + T)
        p_mix = region(10784, NPOOL, T)
        p_t = region(11808, NPOOL, T)
        xbc = region(12832, XBC_TILES, T)

        qT = region(0, LISTS, T)
        sc = region(4096, TT, LISTS, NKEYS)
        sc2 = region(8192, TT, LISTS, NKEYS)
        NC2 = TOPK * TOPK
        cand = region(12288, TT, PH, NC2)
        cand2 = region(16384, TT, PH, NC2)
        vv = region(20480, TT, LISTS, TOPK)
        ii = region(20992, TT, LISTS, TOPK).bitcast(u32)
        iif = region(21504, TT, LISTS, TOPK)
        tv = region(22016, TT, PH, TOPK)
        tp = region(22272, TT, PH, TOPK).bitcast(u32)
        ab = region(22528, TT, 2, PH * TOPK).bitcast(u32)
        abf = region(23040, TT, 2, PH * TOPK)
        oh = region(24576, PH, TOPK, TOPK)
        pick = region(28672, TT, 3, PH * TOPK)
        gsum = region(29440, TT, PH, 1)
        grec = region(29504, TT, PH, 1)
        G = arena[:, :].rearrange("p (i t) -> p i t", t=T)
        ytok = region(0, TT, D)
        x_flat = xT[:, :, :].rearrange("p c t -> p (c t)")
        onehot = [[x_flat[:, (2 * k + half) * 512:(2 * k + half + 1) * 512] for half in range(2)] for k in range(2)]
        z_back = [x_flat[:, k * 512:(k + 1) * 512] for k in range(3)]
        xa = region(0, KC, TAPS - 1 + T)
        xc = region(2080, KC, T)
        sma = region(4128, KC, T)
        smb = region(6176, KC, T)
        rg = region(8224, KC, T)
        ig = region(10272, KC, T)
        vb = region(12320, KC, T)
        cbv = region(14368, KC, TAPS_B - 1 + T)
        bb = region(20800, KC, T)
        gg = region(22848, KC, T)
        av = region(24896, KC, T)
        th = region(16440, KC, T)
        hs = region(29100, KC, T)

        blocks = []

        def add(label, src, width=BLK, split=None):
            blocks.append((label, src, width, split))

        first = {}

        def mark(label):
            first[label] = len(blocks)

        AHEAD, AHEAD_TOP = 34, 18

        mark("w_in")
        for j in range(24):
            add("w_in", A["w_in"][j], split="pool")
        add("w_in", A["w_dt"], KC * HEADS)
        mark("pool_w")
        add("pool_w", A["pool_w"], NPOOL * P)
        mark("w_out")
        for m in range(KC):
            add("w_out", A["w_out"][m][:, 0:BLK])
            add("w_out", A["w_out"][m][:, BLK:BLK + 4 * P], 4 * P)
        PAIRS = NKEYS // 2
        TURNS = (PAIRS - AHEAD) // 2

        def peer_blocks(l):
            mark(f"wq{l}")
            for j in range(LISTS):
                add("wq", A[f"wq{l}"][j], split="dve")
            mark(f"keys{l}")
            for j in range(2):
                add("keys", A[f"keys{l}"][:, j * BLK:(j + 1) * BLK])
            mark(f"exp{l}")
            for i in range(4 * PAIRS):
                add("exp", None, split="pool" if i < 2 * AHEAD else "dve")

        peer_blocks(0)
        mark("w_in2")
        SECT = 7
        for s in range(SECT * KC):
            if s == 3 * KC:
                mark("gates2")
                for i in range(2):
                    add("gates2", A["w_gates2"][i])
                mark("w_in2b")
            add("w_in2", A["w_in2"][s], split="pool")
        mark("w_out2")
        for m in range(KC):
            add("w_out2", A["w_out2"][m], split="dve")
        peer_blocks(1)

        def down_ahead(l, p):
            return first[f"exp{l}"] + 2 * p

        def up_ahead(l, p):
            return first[f"exp{l}"] + 2 * AHEAD + 2 * p

        def turn_block(l, s):
            return first[f"exp{l}"] + 4 * AHEAD + 2 + 8 * s

        def more(at):
            return at[0] * at[1] if at else 0

        def more_in(at):
            return at[0] * (16 * at[1] // RING) if at else 0

        def more_pairs(at):
            return 6 * at[0] if at else 0

        split_no, low_no = [], []
        seen = {"all": 0, "dve": 0, "pool": 0}
        for _, _, _, who in blocks:
            split_no.append(seen["all"])
            low_no.append(seen[who] if who else None)
            if who:
                seen["all"] += 1
                seen[who] += 1

        def slot(n):
            return n % RING

        def part_slot(n):
            return split_no[n] % RING

        def last_split(n):
            before = [m for m in range(n) if blocks[m][3]]
            return before[-RING] if len(before) >= RING else None

        def wait_parts(eng, n, at=None):
            eng.wait_ge(S(f"low_{blocks[n][3]}"), more(at) + (low_no[n] + 1))

        def wait_slot(eng, n):
            m = n - RING
            if m >= 0:
                if blocks[m][3]:
                    wait_parts(eng, m)
                else:
                    eng.wait_ge(S("block_used"), m + 1)

        def make_high(act, m, at=None):
            act.wait_ge(S(f"block_in{slot(m)}"), more_in(at) + 16 * (m // RING + 1))
            if at:
                act.wait_ge(S("block_used"), more(at) + (m - RING + 1))
            elif last_split(m) is not None:
                act.wait_ge(S("block_used"), last_split(m) + 1)
            nc.scalar.activation(ring_hi[:, part_slot(m), :], ring[:, slot(m), :],
                                 ACT.Copy).then_inc(S("high"), 1)

        def make_low(eng, ns, n, at=None):
            eng.wait_ge(S("high"), more(at) + (split_no[n] + 1))
            ns.tensor_tensor(ring_lo[:, part_slot(n), :], ring[:, slot(n), :],
                             ring_hi[:, part_slot(n), :].bitcast(fp32), ALU.subtract)\
                .then_inc(S(f"low_{blocks[n][3]}"), 1)

        def full(eng, n):
            eng.wait_ge(S(f"block_in{slot(n)}"), 16 * (n // RING + 1))

        block = ctx.enter_context(nc.Block())

        @block.sync
        def _(sp):
            sp.dma_start(prm[:, :], A["prm"]).then_inc(S("prm_in"), 16)
            sp.dma_start(cst[:, :], A["cst"]).then_inc(S("cst_in"), 16)
            sp.dma_start(xT[:, :, :], A["xT"]).then_inc(S("x_in"), 16)
            sp.dma_start(inv[:, :, :], A["inv"]).then_inc(S("inv_in"), 16)

            def load(n, src, width):
                wait_slot(sp, n)
                sp.dma_start(ring[:, slot(n), 0:width], src).then_inc(S(f"block_in{slot(n)}"), 16)

            def experts(l):
                def table_load(name, i2, m, at=None):
                    if at:
                        sp.wait_ge(S(f"low_{blocks[m - RING][3]}"), more(at) + (low_no[m - RING] + 1))
                        src = A[f"{name}{l}"][ds(i2, 1), :, :].rearrange("a p n -> (a p) n")
                    else:
                        wait_slot(sp, m)
                        src = A[f"{name}{l}"][i2]
                    sp.dma_start(ring[:, slot(m), :], src).then_inc(S(f"block_in{slot(m)}"), 16)

                def down_loads(p, at=None):
                    for k in range(2):
                        table_load("down", more(at) + (2 * p + k), down_ahead(l, p) + k, at)

                for p in range(4):
                    down_loads(p)
                with sp.Fori(0, 5) as q:
                    for p in range(4, 10):
                        down_loads(p, (q, 12))

                def z_load(p, at=None):
                    if p >= 3:
                        sp.wait_ge(S(f"wf_ready{l}"), more_pairs(at) + (p - 2))
                    src = A[f"z{l}"][ds(more_pairs(at) + p, 1), :, :].rearrange("a p n -> (a p) n") if at \
                        else A[f"z{l}"][p]
                    sp.dma_start(z_back[p % 3], src).then_inc(S(f"z_in{l}_{p % 3}"), 16)

                def up_loads(p, at=None):
                    for k in range(2):
                        table_load("up", more(at) + (2 * p + k), up_ahead(l, p) + k, at)

                up_loads(0)
                sp.wait_ge(S(f"g_ps{l}"), T // 4)
                for k in range(2):
                    sp.wait_ge(S(f"z_out{l}_{k}"), 16 * AHEAD_TOP // 2)
                z_load(0)
                z_load(1)
                for p in range(1, 3):
                    up_loads(p)
                    z_load(p + 1)
                with sp.Fori(0, 5) as q:
                    for p in range(3, 9):
                        up_loads(p, (q, 12))
                        if p == 8:
                            for k in range(2):
                                sp.wait_ge(S(f"z_out{l}_{k}"), 16 * AHEAD // 2)
                        z_load(p + 1, (q, 12))
                up_loads(AHEAD - 1)

                table = [("down", 2), ("down", 3), ("up", 0), ("up", 1), ("down", 4), ("down", 5), ("up", 2), ("up", 3)]

                def turn_loads(s, q=None, rows=range(8)):
                    for k, (name, add_i) in enumerate([table[r] for r in rows]):
                        i2 = 2 * AHEAD + 4 * s + add_i
                        table_load(name, 12 * q + i2 if q is not None else i2, turn_block(l, s) + k,
                                   (q, 24) if q is not None else None)

                for k in range(2):
                    table_load("down", 2 * AHEAD + k, turn_block(l, 0) - 2 + k)
                turn_loads(0)
                turn_loads(1)
                with sp.Fori(0, 4) as q:
                    for r in range(3):
                        turn_loads(2 + r, q)
                turn_loads(TURNS - 1, rows=(0, 1, 2, 3, 6, 7))
                sp.wait_ge(S(f"wf_ready{l}"), AHEAD)
                sp.dma_start(xT[:, :, :], A["x_spill"]).then_inc(S(f"x_back{l}"), 16)

            n = 0
            while n < len(blocks):
                label, src, width, _ = blocks[n]
                if label == "exp":
                    l = 0 if n == first["exp0"] else 1
                    experts(l)
                    n += 4 * PAIRS
                else:
                    load(n, src, width)
                    n += 1
            normed(sp, "fin")
            sp.dma_start(out, hT[:, :, :]).then_inc(S("out_done"), 16)
            sp.wait_ge(S("out_done"), 16)

        @block.tensor
        def _(pe):
            mm = nc.tensor.matmul

            def norm_sum(tag, bank=4):
                pe.wait_ge(S("sq_ready"), NORMS.index(tag) + 1)
                for c in range(KC):
                    last = mm(PS[bank][:, 0:T], ones, sq[:, c, :], start=(c == 0), stop=(c == KC - 1))
                last.then_inc(S("sumsq"), 1)

            def ada(s):
                pe.wait_ge(S("ada_acc"), s + 1)
                if s == 2:
                    pe.wait_ge(S("ada_bias"), 2)
                for j in range(KC):
                    last = mm(PS[7][:, s * KC + j:s * KC + j + 1], ada_acc[:, s % 2, j * P:(j + 1) * P],
                              ones[:, 0:1], start=True, stop=True)
                last.then_inc(S("ada_ps"), 1)

            def product(psum, stat, move, start, stop):
                (s_hi, s_lo), (m_hi, m_lo) = stat, move
                mm(psum, s_lo, m_hi, start=start, stop=False)
                mm(psum, s_hi, m_lo, start=False, stop=False)
                return mm(psum, s_hi, m_hi, start=False, stop=stop)

            def parts(n, a, b):
                return ring_hi[:, part_slot(n), a:b], ring_lo[:, part_slot(n), a:b]

            def split_linear(n, psum, at=None):
                wait_parts(pe, n, at)
                for c in range(KC):
                    last = product(psum, parts(n, c * P, (c + 1) * P), (h_hi[:, c, :], h_lo[:, c, :]),
                                   c == 0, c == KC - 1)
                last.then_inc(S("block_used"), 1)

            def linear(n, psum, src, width=P, chunks=KC):
                full(pe, n)
                for c in range(chunks):
                    last = mm(psum, ring[:, slot(n), c * width:(c + 1) * width], src[:, c, :],
                              start=(c == 0), stop=(c == chunks - 1))
                last.then_inc(S("block_used"), 1)

            pe.wait_ge(S("cst_in"), 16)
            ada(0)
            ada(1)
            norm_sum("mix")
            split_ready(pe, "mix")
            for j in range(24):
                if j >= 4:
                    pe.wait_ge(S("w_in_evac"), j - 3)
                split_linear(first["w_in"] + j, PS[j % 4][:, 0:T])
            pe.wait_ge(S("w_in_evac"), 21)
            linear(first["w_in"] + 24, PS[0][0:HEADS, 0:T], hT, width=HEADS)
            for s in range(2, 6):
                ada(s)

            pe.wait_ge(S("acs_ready"), 1)
            pe.wait_ge(S("dte_ready"), 1)
            for i, (row, c) in enumerate([(2, 0), (2, 1), (4, 0), (4, 1), (5, 0)]):
                last = nc.tensor.transpose(PS[4][:, i * HEADS:(i + 1) * HEADS],
                                           dts[0:HEADS, row, c * CH:(c + 1) * CH], ident[0:HEADS, 0:HEADS])
            last.then_inc(S("tok_ps"), 1)
            pe.wait_ge(S("xbc_ready"), 1)
            pe.wait_ge(S("w_in_evac"), 25)
            for b in range(4):
                for k in range(4):
                    last = nc.tensor.transpose(PS[b][:, k * P:(k + 1) * P],
                                               xbc[:, (b % 2) * 4 + k, (b // 2) * CH:(b // 2 + 1) * CH], ident)
                last.then_inc(S("xtok_ps"), 1)
            for g in range(2):
                last = nc.tensor.transpose(PS[5][:, g * P:(g + 1) * P], xbc[:, 8 + g, 0:CH], ident)
            last.then_inc(S("btok_ps"), 1)
            for g in range(2):
                for c in range(NCH):
                    k = g * NCH + c
                    last = mm(PS[6][:, k * P:(k + 1) * P], xbc[:, 8 + g, c * CH:(c + 1) * CH],
                              xbc[:, 10 + g, c * CH:(c + 1) * CH], start=True, stop=True)
            last.then_inc(S("cb_ps"), 1)
            pe.wait_ge(S("btok_ready"), 1)
            pe.wait_ge(S("xdte_ready"), 1)
            pe.wait_ge(S("tok_ready"), 1)
            for g in range(2):
                last = mm(PS[4 + g][:, :], btok[:, g, :], xdte[:, g * 512:(g + 1) * 512], start=True, stop=True)
            last.then_inc(S("st_ps"), 1)

            def head_rows(h):
                if h >= 2:
                    pe.wait_ge(S("ecs_ready"), h - 1)
                mm(PS[h % 2][:, 0:T], ident[0:HEADS, h:h + 1].to_broadcast([HEADS, P]), dts[0:HEADS, 4, :],
                   start=True, stop=True).then_inc(S("rows_ps"), 1)

            pe.wait_ge(S("xdt_ready"), 4)
            head_rows(0)
            head_rows(1)
            pe.wait_ge(S("st_ready"), 1)
            for h in range(HEADS):
                g, j = h // HPG, h // 2
                pe.wait_ge(S("mdec_ready"), h + 1)
                pe.wait_ge(S("cexp_ready"), h + 1)
                if j >= 2 and h % 2 == 0:
                    pe.wait_ge(S("y_evac"), j - 1)
                o = (h % 2) * HD
                dst = PS[2 + j % 2]
                mm(dst[o:o + HD, 0:CH], xdt[:, 0, h * HD:(h + 1) * HD], mdec[:, h % 2, 0:CH],
                   start=True, stop=True)
                mm(dst[o:o + HD, CH:2 * CH], xdt[:, 1, h * HD:(h + 1) * HD], mdec[:, h % 2, CH:2 * CH],
                   start=True, stop=False)
                mm(dst[o:o + HD, CH:2 * CH], stT[:, h * HD:(h + 1) * HD], cexp[:, h % 2, :],
                   start=False, stop=True).then_inc(S("y_ps"), 1)
                if h + 2 < HEADS:
                    head_rows(h + 2)
            n = first["pool_w"]
            full(pe, n)
            pe.wait_ge(S("pmix_ready"), 1)
            pe.wait_ge(S("st_ready"), 1)
            for g in range(NPOOL):
                last = mm(PS[6 + g // 2][:, (g % 2) * T:(g % 2 + 1) * T], ring[:, slot(n), g * P:(g + 1) * P],
                          p_mix[:, g, :], start=True, stop=True)
            last.then_inc(S("block_used"), 1)
            norm_sum("ssd")
            normed(pe, "ssd")
            pe.wait_ge(S("pool_out"), 1)
            pe.wait_ge(S("y_evac"), 8)
            for m in range(KC):
                n = first["w_out"] + 2 * m
                if m >= 4:
                    pe.wait_ge(S("w_out_evac"), m - 3)
                full(pe, n)
                for c in range(KC):
                    last = mm(PS[m % 4][:, 0:T], ring[:, slot(n), c * P:(c + 1) * P], mixT[:, c, :],
                              start=(c == 0), stop=False)
                last.then_inc(S("block_used"), 1)
                full(pe, n + 1)
                for c in range(4):
                    last = mm(PS[m % 4][:, 0:T], ring[:, slot(n + 1), c * P:(c + 1) * P], mixT[:, KC + c, :],
                              start=False, stop=(c == 3))
                last.then_inc(S("block_used"), 1)

            def peer(l):
                norm_sum(f"ffn{l}")
                split_ready(pe, f"ffn{l}")
                for j in range(LISTS):
                    if j >= 4:
                        pe.wait_ge(S(f"q_evac{l}"), j - 3)
                    split_linear(first[f"wq{l}"] + j, PS[j % 4][:, 0:T])
                pe.wait_ge(S(f"q_evac{l}"), LISTS)
                for half in range(2):
                    n = first[f"keys{l}"] + half
                    full(pe, n)
                    for tt in range(TT):
                        for q in range(2):
                            for k in range(4):
                                i = half * 8 + q * 4 + k
                                last = mm(PS[(1 - tt) * 4 + half * 2 + q][:, k * P:(k + 1) * P],
                                          qT[:, i, tt * P:(tt + 1) * P],
                                          ring[:, slot(n), (i % 8) * P:(i % 8 + 1) * P], start=True, stop=True)
                    last.then_inc(S("block_used"), 1)
                def down_block(m, p, k, at=None):
                    split_linear(m + k, PS[4 + p % 2][:, k * T:(k + 1) * T], at)

                def down_ahead_pair(p, at=None, gate_turn=None):
                    if p >= 2:
                        pe.wait_ge(S(f"act_done{l}"), more_pairs(at) + (p - 1))
                    for k in range(2):
                        if gate_turn is not None:
                            gates(gate_turn + k)
                        down_block(down_ahead(l, p), p, k, at)

                def gates(it):
                    for half in range(2):
                        pe.wait_ge(S(f"onehot{l}"), 2 * it + (half + 1))
                        if not (isinstance(it, int) and it == 0):
                            pe.wait_ge(S(f"g_evac{l}"), 2 * it + (half - 1))
                        for k in range(4):
                            last = mm(PS[half][:, k * P:(k + 1) * P], onehot[0][half][:, k * P:(k + 1) * P],
                                      onehot[1][half][:, k * P:(k + 1) * P], start=True, stop=True)
                        last.then_inc(S(f"g_ps{l}"), 1)

                pe.wait_ge(S(f"sc_ready{l}"), 2)
                for p in range(6):
                    down_ahead_pair(p)
                with pe.Fori(0, 2) as q:
                    for p in range(6, 12):
                        down_ahead_pair(p, (q, 12))
                for tt in range(TT):
                    pe.wait_ge(S(f"pick_ready{l}"), tt + 1)
                    for k in range(3):
                        last = nc.tensor.transpose(PS[2 + tt][:, k * P:(k + 1) * P], pick[:, tt, k, :], ident)
                    last.then_inc(S(f"pickT_ps{l}"), 1)
                for p in range(AHEAD_TOP, AHEAD_TOP + 4):
                    down_ahead_pair(p, None, 2 * (p - AHEAD_TOP))
                with pe.Fori(0, 2) as q:
                    for p in range(AHEAD_TOP + 4, AHEAD_TOP + 10):
                        down_ahead_pair(p, (q, 12), 12 * q + 2 * (p - AHEAD_TOP))

                def up(m, p, at=None, start=False, stop=False):
                    pe.wait_ge(S(f"w_ready{l}"), more_pairs(at) + (p + 1))
                    for k in range(2):
                        wait_parts(pe, m + k, at)
                        for tt in range(TT):
                            a = k * T + tt * P
                            for f in range(2):
                                last = product(PS[tt * 2 + f][:, :],
                                               (w_hi[:, p % 2, a:a + P], w_lo[:, p % 2, a:a + P]),
                                               parts(m + k, f * 512, (f + 1) * 512),
                                               start and k == 0, stop and k == 1)
                        last.then_inc(S("block_used"), 1)

                def down(m, p, at=None):
                    pe.wait_ge(S(f"wf_ready{l}"), more_pairs(at) + (p - 1))
                    for k in range(2):
                        down_block(m, p, k, at)

                pe.wait_ge(S(f"pickT_ready{l}"), TT)
                pe.wait_ge(S(f"g_evac{l}"), T // 4)
                for p in range(3):
                    up(up_ahead(l, p), p, start=p == 0)
                with pe.Fori(0, 5) as q:
                    for p in range(3, 9):
                        up(up_ahead(l, p), p, (q, 12))
                up(up_ahead(l, AHEAD - 1), AHEAD - 1)

                def turn(s, at=None):
                    m, p = turn_block(l, s), AHEAD + 2 * s
                    down(m, p + 1, at)
                    up(m + 2, p, at)
                    down(m + 4, p + 2, at)
                    up(m + 6, p + 1, at)

                pe.wait_ge(S(f"act_done{l}"), AHEAD)
                down(turn_block(l, 0) - 2, AHEAD)
                turn(0)
                turn(1)
                with pe.Fori(0, 4) as q:
                    for r in range(3):
                        turn(2 + r, (q, 24))
                m = turn_block(l, TURNS - 1)
                down(m, PAIRS - 1)
                up(m + 2, PAIRS - 2)
                up(m + 4, PAIRS - 1, stop=True)

                for tt in range(TT):
                    pe.wait_ge(S(f"ytok_ready{l}"), 2 * tt + 2)
                    for q in range(2):
                        for k in range(4):
                            last = nc.tensor.transpose(PS[4 + tt * 2 + q][:, k * P:(k + 1) * P],
                                                       ytok[:, tt, (q * 4 + k) * P:(q * 4 + k + 1) * P], ident)
                        last.then_inc(S(f"yT_ps{l}"), 1)

            peer(0)
            norm_sum("final")
            norm_sum("mix2")
            split_ready(pe, "mix2")
            for s in range(SECT * KC):
                if s >= 7:
                    pe.wait_ge(S("in2_evac"), s - 6)
                if s == 3 * KC:
                    n = first["gates2"]
                    pe.wait_ge(S("xc_ready"), 1)
                    for j in range(KC):
                        if j % 4 == 0:
                            full(pe, n + j // 4)
                        if j:
                            pe.wait_ge(S("gate_evac"), j)
                        for k in range(2):
                            last = mm(PS[7][:, k * T:(k + 1) * T],
                                      ring[:, slot(n + j // 4), (j % 4 * 2 + k) * P:(j % 4 * 2 + k + 1) * P],
                                      xc[:, j, :], start=True, stop=True)
                        last.then_inc(S("block_used" if j % 4 == 3 else "gate_ps"), 1)
                n = (first["w_in2"] if s < 3 * KC else first["w_in2b"] - 3 * KC) + s
                split_linear(n, PS[s % 7][:, 0:T])
            pe.wait_ge(S("in2_evac"), SECT * KC)
            split_ready(pe, "merged")
            for m in range(KC):
                if m >= 4:
                    pe.wait_ge(S("w_out2_evac"), m - 3)
                split_linear(first["w_out2"] + m, PS[m % 4][:, 0:T])
            peer(1)
            norm_sum("fin")

        @block.scalar
        def _(act):
            A_ = nc.scalar.activation

            def norm_act(tag, src, sem, val, bank=4):
                act.wait_ge(S(sem), val)
                A_(sq[:, :, :], src, ACT.Square).then_inc(S("sq_ready"), 1)
                act.wait_ge(S("sumsq"), NORMS.index(tag) + 1)
                A_(rstd, PS[bank][:, 0:T], ACT.Sqrt, bias=epsc[:, 0:1], scale=1.0 / D).then_inc(S("rms"), 1)

            def split_h(tag, src):
                normed(act, tag)
                A_(h_hi[:, :, :], src, ACT.Copy).then_inc(S("h_high"), 1)

            def highs(n, count, evac):
                for j in range(min(RING, count)):
                    make_high(act, n + j)
                for j in range(count):
                    if j + RING < count:
                        make_high(act, n + j + RING)
                    evac(j)

            act.wait_ge(S("prm_in"), 16)
            A_(cact[:, :], col("c", 0, 8), ACT.Silu).then_inc(S("cact_ready"), 1)
            act.wait_ge(S("eps_ready"), 1)
            norm_act("mix", xT[:, :, :], "x_in", 16)
            act.wait_ge(S("pads_ready"), 1)
            split_h("mix", hT[:, :, :])

            def evac_in(j):
                act.wait_ge(S("block_used"), first["w_in"] + j + 1)
                src = PS[j % 4][:, 0:T]
                if j < 4:
                    A_(u_pad[:, j, UPAD:], src, ACT.Copy).then_inc(S("w_in_evac"), 1)
                elif j < 12:
                    A_(zs[:, j - 4, :], src, ACT.Silu).then_inc(S("w_in_evac"), 1)
                else:
                    A_(xbc_in[:, j - 12, TAPS - 1:], src, ACT.Copy).then_inc(S("w_in_evac"), 1)

            highs(first["w_in"], 24, evac_in)
            act.wait_ge(S("block_used"), first["w_in"] + 25)
            A_(dts[0:HEADS, 0, :], PS[0][0:HEADS, 0:T], ACT.Identity,
               bias=prm[0:HEADS, COL["dt_bias"][0]:COL["dt_bias"][0] + 1]).then_inc(S("w_in_evac"), 1)
            act.wait_ge(S("w_in_evac"), 25)
            A_(dts[0:HEADS, 1, :], dts[0:HEADS, 0, :], ACT.Abs).then_inc(S("dt_abs"), 1)
            act.wait_ge(S("dt_abs"), 1)
            A_(dts[0:HEADS, 1, :], dts[0:HEADS, 1, :], ACT.Exp, scale=-1.0).then_inc(S("dt_exp"), 1)
            A_(lru_s[0:HEADS, 0, 0:1], prm[0:HEADS, COL["a_log"][0]:COL["a_log"][0] + 1], ACT.Exp)\
                .then_inc(S("alog_exp"), 1)
            act.wait_ge(S("dt_1pe"), 1)
            A_(dts[0:HEADS, 3, :], dts[0:HEADS, 2, :], ACT.Ln).then_inc(S("dt_ln"), 1)
            act.wait_ge(S("acs_ready"), 1)
            A_(dts[0:HEADS, 5, 0:CH], dts[0:HEADS, 4, 0:CH], ACT.Exp, scale=-1.0,
               bias=dts[0:HEADS, 4, CH - 1:CH]).then_inc(S("dte_ready"), 1)
            act.wait_ge(S("conv_ready"), 1)
            A_(xbc[:, :, :], xbc[:, :, :], ACT.Silu).then_inc(S("xbc_ready"), 1)
            act.wait_ge(S("btok_ps"), 1)
            A_(btok[:, :, :], PS[5][:, 0:2 * P].rearrange("p (g n) -> p g n", g=2), ACT.Copy)\
                .then_inc(S("btok_ready"), 1)
            act.wait_ge(S("cb_ps"), 1)
            A_(cbt[:, :, :], PS[6][:, :].rearrange("p (g n) -> p g n", g=2), ACT.Copy).then_inc(S("cb_ready"), 1)
            act.wait_ge(S("st_ps"), 1)
            A_(stT[:, 0:512], PS[4][:, :], ACT.Copy)
            A_(stT[:, 512:1024], PS[5][:, :], ACT.Copy).then_inc(S("st_ready"), 1)
            act.wait_ge(S("tok_ready"), 1)
            for h in range(HEADS):
                act.wait_ge(S("seg_ready"), h + 1)
                if h >= 2:
                    act.wait_ge(S("cexp_ready"), h - 1)
                    act.wait_ge(S("mdec_ready"), h - 1)
                A_(ecs[:, h % 2, :], PS[h % 2][:, CH:2 * CH], ACT.Exp).then_inc(S("ecs_ready"), 1)
                for c in range(NCH):
                    last = A_(dec[:, h % 2, c * CH:(c + 1) * CH], seg[:, h % 2, c * CH:(c + 1) * CH], ACT.Exp,
                              bias=tok[:, 2 + c, h:h + 1])
                last.then_inc(S("dec_ready"), 1)
            norm_act("ssd", mixT[:, NPOOL:, :], "y_gated", 1)

            def peer(l, x_sem, x_val):
                gelu = ACT.Gelu if l == 0 else ACT.Gelu_apprx_tanh
                norm_act(f"ffn{l}", xT[:, :, :], x_sem, x_val)
                split_h(f"ffn{l}", hT[:, :, :])

                def evac_q(j):
                    act.wait_ge(S("block_used"), first[f"wq{l}"] + j + 1)
                    A_(qT[:, j, :], PS[j % 4][:, 0:T], ACT.Copy).then_inc(S(f"q_evac{l}"), 1)

                highs(first[f"wq{l}"], LISTS, evac_q)
                for half in range(2):
                    act.wait_ge(S("block_used"), first[f"keys{l}"] + half + 1)
                    for tt in range(TT):
                        for q in range(2):
                            i = half * 8 + q * 4
                            last = A_(sc[:, tt, i:i + 4, :],
                                      PS[(1 - tt) * 4 + half * 2 + q][:, :].rearrange("p (a n) -> p a n", a=4),
                                      ACT.Copy)
                    last.then_inc(S(f"sc_ready{l}"), 1)
                def ahead_pair(p, at=None, gate_turn=None):
                    m = down_ahead(l, p)
                    for k in range(2):
                        if gate_turn is not None:
                            gates(gate_turn + k)
                        make_high(act, m + RING + k, at)
                    act.wait_ge(S("block_used"), more(at) + (m + 2))
                    if p >= 2:
                        act.wait_ge(S(f"z_out{l}_{p % 2}"), 8 * more_pairs(at) + 16 * (p // 2))
                    A_(wf[:, p % 2, :], PS[4 + p % 2][:, :], gelu).then_inc(S(f"act_done{l}"), 1)
                    act.wait_ge(S(f"act_done{l}"), more_pairs(at) + (p + 1))
                    dst = A[f"z{l}"][ds(more_pairs(at) + p, 1), :, :].rearrange("a p n -> (a p) n") if at \
                        else A[f"z{l}"][p]
                    act.dma_start(dst, wf[:, p % 2, :]).then_inc(S(f"z_out{l}_{p % 2}"), 16)

                def gates(it):
                    for half in range(2):
                        act.wait_ge(S(f"g_ps{l}"), 2 * it + (half + 1))
                        t0 = it * 8 + half * 4
                        dst = G[:, :, t0:t0 + 4] if isinstance(it, int) else G[:, :, ds(t0, 4)]
                        A_(dst, PS[half][:, :].rearrange("p (t i) -> p i t", t=4), ACT.Copy)\
                            .then_inc(S(f"g_evac{l}"), 1)

                for k in range(RING):
                    make_high(act, down_ahead(l, 0) + k)
                for p in range(6):
                    ahead_pair(p)
                with act.Fori(0, 2) as q:
                    for p in range(6, 12):
                        ahead_pair(p, (q, 12))
                for tt in range(TT):
                    act.wait_ge(S(f"gate_sub{l}"), tt + 1)
                    A_(tv[:, tt, :, :], tv[:, tt, :, :], ACT.Exp).then_inc(S(f"gate_exp{l}"), 1)
                for p in range(AHEAD_TOP, AHEAD_TOP + 4):
                    ahead_pair(p, None, 2 * (p - AHEAD_TOP))
                with act.Fori(0, 2) as q:
                    for p in range(AHEAD_TOP + 4, AHEAD_TOP + 10):
                        ahead_pair(p, (q, 12), 12 * q + 2 * (p - AHEAD_TOP))

                def weights_high(p, at=None, used=None):
                    act.wait_ge(S(f"wf_ready{l}"), more_pairs(at) + (p + 1))
                    if used is not None:
                        act.wait_ge(S("block_used"), more(at) + used)
                    A_(w_hi[:, p % 2, :], wf[:, p % 2, :], ACT.Copy).then_inc(S(f"w_high{l}"), 1)

                def up_pair(p, at=None, following=True):
                    m = up_ahead(l, p)
                    if following:
                        weights_high(p + 1, at, used=m)
                    for k in range(2):
                        make_high(act, m + RING + k, at)

                weights_high(0)
                for p in range(3):
                    up_pair(p)
                with act.Fori(0, 5) as q:
                    for p in range(3, 9):
                        up_pair(p, (q, 12))
                up_pair(AHEAD - 1, following=False)

                def apply_gelu(m, p, at=None):
                    act.wait_ge(S("block_used"), more(at) + (m + 2))
                    A_(PS[4 + p % 2][:, :], PS[4 + p % 2][:, :], gelu).then_inc(S(f"act_done{l}"), 1)

                def turn(s, at=None):
                    m, p = turn_block(l, s), AHEAD + 2 * s
                    make_high(act, m + 3, at)
                    make_high(act, m + 4, at)
                    apply_gelu(m, p + 1, at)
                    make_high(act, m + 5, at)
                    weights_high(p + 1, at)
                    if s == TURNS - 1:
                        return
                    for k in (6, 7, 8):
                        make_high(act, m + k, at)
                    apply_gelu(m + 4, p + 2, at)
                    make_high(act, m + 9, at)
                    weights_high(p + 2, at)
                    make_high(act, m + 10, at)

                m = turn_block(l, 0)
                make_high(act, m + 1)
                make_high(act, m + 2)
                apply_gelu(m - 2, AHEAD)
                weights_high(AHEAD)
                turn(0)
                turn(1)
                with act.Fori(0, 4) as q:
                    for r in range(3):
                        turn(2 + r, (q, 24))
                turn(TURNS - 1)
                act.wait_ge(S("block_used"), turn_block(l, TURNS - 1) + 6)
                for tt in range(TT):
                    for f in range(2):
                        A_(ytok[:, tt, f * 512:(f + 1) * 512], PS[tt * 2 + f][:, :], ACT.Copy)\
                            .then_inc(S(f"ytok_ready{l}"), 1)

            peer(0, "w_out_evac", KC)
            norm_act("final", xT[:, :, :], "x_peer0", 1)
            norm_act("mix2", xT[:, :, :], "norm_done", NORMED.index("final") + 1)
            split_h("mix2", hT[:, :, :])
            A_(lru_s[:, 1, :], col("lam", 0, 8), ACT.Abs).then_inc(S("lam_abs"), 1)
            act.wait_ge(S("lam_abs"), 1)
            A_(lru_s[:, 1, :], lru_s[:, 1, :], ACT.Exp, scale=-1.0).then_inc(S("lam_exp"), 1)
            act.wait_ge(S("lam_1pe"), 1)
            A_(lru_s[:, 3, :], lru_s[:, 2, :], ACT.Ln).then_inc(S("lam_ln"), 1)
            act.wait_ge(S("pads2_ready"), 1)

            def w_in2_block(s):
                return (first["w_in2"] if s < 3 * KC else first["w_in2b"] - 3 * KC) + s

            for s in range(RING):
                make_high(act, w_in2_block(s))
            for s in range(SECT * KC):
                sec, j = s // KC, s % KC
                if s == 3 * KC:
                    for k in range(KC):
                        if k % 4 == 3:
                            act.wait_ge(S("block_used"), first["gates2"] + k // 4 + 1)
                        else:
                            act.wait_ge(S("gate_ps"), k - k // 4 + 1)
                        A_(rg[:, k, :], PS[7][:, 0:T], ACT.Sigmoid, bias=col("b_a", k))
                        A_(ig[:, k, :], PS[7][:, T:2 * T], ACT.Sigmoid, bias=col("b_x", k))\
                            .then_inc(S("gate_evac"), 1)
                    make_high(act, w_in2_block(s + 1))
                    make_high(act, w_in2_block(s + 2))
                if s + RING < SECT * KC and s not in (3 * KC - 2, 3 * KC - 1):
                    make_high(act, w_in2_block(s + RING))
                act.wait_ge(S("block_used"), w_in2_block(s) + 1)
                src = PS[s % 7][:, 0:T]
                dst, fn = [(xa[:, j, TAPS - 1:], ACT.Copy), (sma[:, j, :], ACT.Sigmoid), (smb[:, j, :], ACT.Sigmoid),
                           (vb[:, j, :], ACT.Copy), (cbv[:, j, TAPS_B - 1:], ACT.Copy), (bb[:, j, :], ACT.Copy),
                           (gg[:, j, :], ACT.Gelu_apprx_tanh)][sec]
                if s == 4 * KC:
                    act.wait_ge(S("lam_ready"), 1)
                    act.wait_ge(S("gate_evac"), KC)
                    for k in range(KC):
                        last = A_(av[:, k, :], rg[:, k, :], ACT.Exp, scale=lru_s[:, 4, k:k + 1])
                    last.then_inc(S("av_ready"), 1)
                    for k in range(KC):
                        last = A_(th[:, k, :], rg[:, k, :], ACT.Tanh, scale=lru_s[:, 5, k:k + 1])
                    last.then_inc(S("th_ready"), 1)
                if s == 5 * KC:
                    act.wait_ge(S("mult_sq"), 1)
                    A_(th[:, :, :], th[:, :, :], ACT.Sqrt).then_inc(S("mult_ready"), 1)
                A_(dst, src, fn).then_inc(S("in2_evac"), 1)
            split_h("merged", gg[:, :, :])
            highs(first["w_out2"], KC, lambda j: None)
            peer(1, "w_out2_evac", KC)
            norm_act("fin", xT[:, :, :], "x_peer1", 1)

        @block.vector
        def _(dve):
            v = nc.vector
            counts = {}

            def link(ins, signal="dve_chain", by=1):
                counts[signal] = counts.get(signal, 0) + by
                ins.then_inc(S(signal), by)
                dve.wait_ge(S(signal), counts[signal])

            TTn, TS, STT = v.tensor_tensor, v.tensor_scalar, v.scalar_tensor_tensor

            def norm_dve(tag, src, dst, scale, shift=None):
                dve.wait_ge(S("rms"), NORMS.index(tag) + 1)
                link(v.reciprocal(rstd, rstd))
                link(TTn(dst, src, rstd[:, None, :].to_broadcast([P, KC, T]), ALU.mult))
                for c in range(KC):
                    d = dst[:, c, :]
                    if shift is None:
                        last = TS(d, d, scale(c), None, ALU.mult)
                    else:
                        last = TS(d, d, scale(c), shift(c), ALU.mult, ALU.add)
                link(last, "norm_done")

            def split_low(tag, src):
                dve.wait_ge(S("h_high"), SPLITS.index(tag) + 1)
                link(TTn(h_lo[:, :, :], src, h_hi[:, :, :].bitcast(fp32), ALU.subtract), "h_split")

            def ada(s):
                dve.wait_ge(S(f"ada_in{s % 2}"), 16 * (s // 2 + 1))
                if s >= 2:
                    dve.wait_ge(S("ada_ps"), s - 1)
                w = ada_buf[:, s % 2, :].rearrange("p (c n) -> p c n", c=KC)
                acc = ada_acc[:, s % 2, :]
                link(TS(acc, w[:, 0, :], cact[:, 0:1], None, ALU.mult))
                for c in range(1, KC):
                    link(STT(acc, w[:, c, :], cact[:, c:c + 1], acc, ALU.mult, ALU.add),
                         "ada_acc" if c == KC - 1 else "dve_chain")

            def ada_out(s):
                dve.wait_ge(S("ada_ps"), 2 if s < 2 else 6)
                m = mod[:, s * KC:(s + 1) * KC]
                link(TTn(m, PS[7][:, s * KC:(s + 1) * KC], col("b_ada", s * KC, KC), ALU.add), "ada_bias")
                if s in (1, 4):
                    link(STT(m, m, 1.0, col("norm_mix" if s == 1 else "norm_ffn", 0, KC), ALU.add, ALU.mult))

            link(v.memset(epsc[:, :], EPS), "eps_ready")
            v.memset(u_pad[:, :, 0:UPAD], 0.0)
            link(v.memset(xbc_in[:, :, 0:TAPS - 1], 0.0), "pads_ready")
            dve.wait_ge(S("prm_in"), 16)
            dve.wait_ge(S("cact_ready"), 1)
            ada(0)
            ada(1)
            ada_out(0)
            ada_out(1)
            norm_dve("mix", xT[:, :, :], hT[:, :, :], lambda c: mod[:, KC + c:KC + c + 1], lambda c: mod[:, c:c + 1])
            split_low("mix", hT[:, :, :])
            for s in range(2, 6):
                ada(s)
            link(v.memset(p_sum[:, :, 0:UPAD], 0.0), "ada_free")
            dve.wait_ge(S("w_in_evac"), 24)
            for j in range(XBC_TILES):
                last = TS(xbc[:, j, :], xbc_in[:, j, 0:T], col("conv_w", j), col("conv_b", j), ALU.mult, ALU.add)
            link(last)
            for k in range(1, TAPS):
                for j in range(XBC_TILES):
                    last = STT(xbc[:, j, :], xbc_in[:, j, k:k + T], col("conv_w", k * XBC_TILES + j), xbc[:, j, :],
                               ALU.mult, ALU.add)
                link(last, "conv_ready" if k == TAPS - 1 else "dve_chain")

            def softplus_u(e, u, sem_in, sem_out):
                dve.wait_ge(S(sem_in), 1)
                link(TS(u, e, 1.0, None, ALU.add), sem_out)

            def log1p(e, u, ln, tmp):
                link(TS(u, u, -1.0, None, ALU.add))
                link(TS(tmp, u, 0.0, None, ALU.is_equal))
                link(TTn(u, u, tmp, ALU.add))
                link(v.reciprocal(u, u))
                link(TTn(u, u, ln, ALU.mult))
                link(TTn(u, u, tmp, ALU.add))
                link(TTn(ln, u, e, ALU.mult))

            H16 = slice(0, HEADS)
            softplus_u(dts[H16, 1, :], dts[H16, 2, :], "dt_exp", "dt_1pe")
            dve.wait_ge(S("dt_ln"), 1)
            log1p(dts[H16, 1, :], dts[H16, 2, :], dts[H16, 3, :], dts[H16, 4, :])
            link(STT(dts[H16, 2, :], dts[H16, 0, :], 0.0, dts[H16, 3, :], ALU.max, ALU.add))
            dve.wait_ge(S("alog_exp"), 1)
            link(TS(dts[H16, 3, :], dts[H16, 2, :], lru_s[H16, 0, 0:1], -1.0, ALU.mult, ALU.mult))
            for c in range(NCH):
                last = v.tensor_tensor_scan(dts[H16, 4, c * CH:(c + 1) * CH], cst[H16, CONES:CONES + CH],
                                            dts[H16, 3, c * CH:(c + 1) * CH], 0.0, ALU.mult, ALU.add)
            link(last, "acs_ready")
            dve.wait_ge(S("tok_ps"), 1)
            v.tensor_copy(tok[:, 0:2, :], PS[4][:, 0:2 * HEADS].rearrange("p (a h) -> p a h", a=2))
            TS(tok[:, 2:4, :], PS[4][:, 2 * HEADS:4 * HEADS].rearrange("p (a h) -> p a h", a=2), -1.0, None, ALU.mult)
            link(v.tensor_copy(tok[:, 4, :], PS[4][:, 4 * HEADS:5 * HEADS]), "tok_ready")
            for b in range(4):
                c, hf = b // 2, b % 2
                dve.wait_ge(S("xtok_ps"), b + 1)
                last = TTn(xdt[:, c, hf * 512:(hf + 1) * 512].rearrange("p (h d) -> p h d", d=HD),
                           PS[b][:, :].rearrange("p (h d) -> p h d", d=HD),
                           tok[:, c, hf * HPG:(hf + 1) * HPG][:, :, None].to_broadcast([P, HPG, HD]), ALU.mult)
                link(last, "xdt_ready")
            link(TTn(xdte.rearrange("p (h d) -> p h d", d=HD), xdt[:, 0, :].rearrange("p (h d) -> p h d", d=HD),
                     tok[:, 4, :][:, :, None].to_broadcast([P, HEADS, HD]), ALU.mult), "xdte_ready")
            dve.wait_ge(S("cb_ready"), 1)
            for s in range(2, 6):
                ada_out(s)

            def seg_head(h):
                dve.wait_ge(S("rows_ps"), h + 1)
                if h >= 2:
                    dve.wait_ge(S("dec_ready"), h - 1)
                TTn(seg[:, h % 2, :].rearrange("p (c l) -> p c l", c=NCH),
                    PS[h % 2][:, 0:T].rearrange("p (c l) -> p c l", c=NCH),
                    mask[:, None, :].to_broadcast([P, NCH, CH]), ALU.add).then_inc(S("seg_ready"), 1)

            def y_pair(j):
                dve.wait_ge(S("y_ps"), 2 * j + 2)
                STT(mixT[:, NPOOL + j, :], xbc[:, j, :], col("d_skip", j), PS[2 + j % 2][:, 0:T],
                    ALU.mult, ALU.add).then_inc(S("y_evac"), 1)

            seg_head(0)
            for h in range(HEADS):
                if h + 1 < HEADS:
                    seg_head(h + 1)
                g = h // HPG
                dve.wait_ge(S("ecs_ready"), h + 1)
                if h >= 2:
                    dve.wait_ge(S("y_ps"), h - 1)
                TTn(cexp[:, h % 2, :], xbc[:, 10 + g, CH:2 * CH], ecs[:, h % 2, :], ALU.mult)\
                    .then_inc(S("cexp_ready"), 1)
                dve.wait_ge(S("dec_ready"), h + 1)
                TTn(mdec[:, h % 2, :], dec[:, h % 2, :], cbt[:, g, :], ALU.mult).then_inc(S("mdec_ready"), 1)
                if h % 2 == 1 and h >= 3:
                    y_pair(h // 2 - 1)
            y_pair(HEADS // 2 - 1)
            dve.wait_ge(S("y_evac"), HEADS // 2)
            link(TTn(mixT[:, NPOOL:, :], mixT[:, NPOOL:, :], zs[:, :, :], ALU.mult), "y_gated")
            dve.wait_ge(S("block_used"), first["pool_w"] + 1)
            for g in range(NPOOL):
                last = TS(mixT[:, g, :], PS[6 + g // 2][:, (g % 2) * T:(g % 2 + 1) * T], col("pool_b", g),
                          col("pool_scale", g), ALU.add, ALU.mult)
            last.then_inc(S("pool_out"), 1)
            norm_dve("ssd", mixT[:, NPOOL:, :], mixT[:, NPOOL:, :], lambda c: col("ssd_norm", c))
            for m in range(KC):
                dve.wait_ge(S("block_used"), first["w_out"] + 2 * m + 2)
                STT(xT[:, m, :], PS[m % 4][:, 0:T], mod[:, 2 * KC + m:2 * KC + m + 1], xT[:, m, :],
                    ALU.mult, ALU.add).then_inc(S("w_out_evac"), 1)
            dve.wait_ge(S("w_out_evac"), KC)

            def top16(src, src2, vals, idx, rows, finish):
                for r in rows:
                    last = v.max(vals(r)[:, 0:8], src(r))
                link(last)
                for r in rows:
                    last = v.max_index(idx(r)[:, 0:8], vals(r)[:, 0:8], src(r))
                for r in rows:
                    last = v.match_replace(src2(r), vals(r)[:, 0:8], src(r), LOWEST)
                link(last)
                for r in rows:
                    last = v.max(vals(r)[:, 8:16], src2(r))
                link(last)
                for r in rows:
                    last = v.max_index(idx(r)[:, 8:16], vals(r)[:, 8:16], src2(r))
                link(last, finish)

            def peer(l, scale, shift):
                norm_dve(f"ffn{l}", xT[:, :, :], hT[:, :, :], scale, shift)
                split_low(f"ffn{l}", hT[:, :, :])
                for j in range(LISTS):
                    make_low(dve, v, first[f"wq{l}"] + j)
                dve.wait_ge(S(f"sc_ready{l}"), 2)
                for tt in range(TT):
                    top16(lambda r: sc[:, tt, r, :], lambda r: sc2[:, tt, r, :], lambda r: vv[:, tt, r, :],
                          lambda r: ii[:, tt, r, :], range(LISTS), "dve_chain")
                    link(v.tensor_copy(iif[:, tt, :, :], ii[:, tt, :, :]))
                    v4 = vv[:, tt, :, :].rearrange("p (h s) k -> p h s k", s=2)
                    for h in range(PH):
                        last = TTn(cand[:, tt, h, :].rearrange("p (a b) -> p a b", a=TOPK),
                                   v4[:, h, 0, :][:, :, None].to_broadcast([P, TOPK, TOPK]),
                                   v4[:, h, 1, :][:, None, :].to_broadcast([P, TOPK, TOPK]), ALU.add)
                    link(last)
                    top16(lambda r: cand[:, tt, r, :], lambda r: cand2[:, tt, r, :], lambda r: tv[:, tt, r, :],
                          lambda r: tp[:, tt, r, :], range(PH), "dve_chain")
                    pos = tp[:, tt, :, :].rearrange("p h k -> p (h k)")
                    TS(ab[:, tt, 0, :], pos, 4, None, ALU.logical_shift_right)
                    link(TS(ab[:, tt, 1, :], pos, TOPK - 1, None, ALU.bitwise_and))
                    link(v.tensor_copy(abf[:, tt, :, :], ab[:, tt, :, :]))
                    link(TTn(pick[:, tt, 2, :].rearrange("p (h k) -> p h k", h=PH), tv[:, tt, :, :],
                             tv[:, tt, :, 0:1].to_broadcast([P, PH, TOPK]), ALU.subtract))
                    link(v.tensor_copy(tv[:, tt, :, :], pick[:, tt, 2, :].rearrange("p (h k) -> p h k", h=PH)),
                         f"gate_sub{l}")
                    i4 = iif[:, tt, :, :].rearrange("p (h s) k -> p h s k", s=2)
                    for s in range(2):
                        rk = abf[:, tt, s, :]
                        link(TTn(oh[:, :, :, :].rearrange("p h k a -> p (h k) a"),
                                 rk[:, :, None].to_broadcast([P, PH * TOPK, TOPK]),
                                 iota[:, None, 0:TOPK].to_broadcast([P, PH * TOPK, TOPK]), ALU.is_equal))
                        for h in range(PH):
                            last = TTn(oh[:, h, :, :], oh[:, h, :, :],
                                       i4[:, h, s, :][:, None, :].to_broadcast([P, TOPK, TOPK]), ALU.mult)
                        link(last)
                        link(v.tensor_reduce(pick[:, tt, s, :], oh[:, :, :, :].rearrange("p h k a -> p (h k) a"),
                                             AX.X, ALU.add))
                for tt in range(TT):
                    dve.wait_ge(S(f"gate_exp{l}"), tt + 1)
                    link(v.tensor_reduce(gsum[:, tt, :, 0], tv[:, tt, :, :], AX.X, ALU.add))
                    link(v.reciprocal(grec[:, tt, :, :], gsum[:, tt, :, :]))
                    link(TTn(pick[:, tt, 2, :].rearrange("p (h k) -> p h k", h=PH), tv[:, tt, :, :],
                             grec[:, tt, :, :].to_broadcast([P, PH, TOPK]), ALU.mult), f"pick_ready{l}")
                for tt in range(TT):
                    dve.wait_ge(S(f"pickT_ps{l}"), tt + 1)
                    link(v.tensor_copy(selT[:, :, tt * P:(tt + 1) * P],
                                       PS[2 + tt][:, 0:3 * P].rearrange("p (a t) -> p a t", a=3)), f"pickT_ready{l}")

                def gates(it, is_first):
                    src = selT[:, :, 0:8] if is_first else selT[:, :, ds(it * 8, 8)]
                    if not is_first:
                        dve.wait_ge(S(f"onehot{l}"), 2 * it)
                    v.tensor_copy(stage[:, :, :], src).then_inc(S(f"stage{l}"), 1)
                    dve.wait_ge(S(f"stage{l}"), it + 1)
                    for half in range(2):
                        if not is_first:
                            dve.wait_ge(S(f"g_ps{l}"), 2 * it + (half - 1))
                        for k in range(4):
                            t = half * 4 + k
                            TS(onehot[0][half][:, k * P:(k + 1) * P], iota, stage[:, 0, t:t + 1], None,
                               ALU.is_equal)
                            last = TS(onehot[1][half][:, k * P:(k + 1) * P], iota, stage[:, 1, t:t + 1],
                                      stage[:, 2, t:t + 1], ALU.is_equal, ALU.mult)
                        last.then_inc(S(f"onehot{l}"), 1)

                dve.wait_ge(S(f"x_out{l}"), 16)
                gates(0, True)
                with dve.Fori(1, T // 8) as it:
                    gates(it, False)

                def low(m, at=None):
                    make_low(dve, v, m, at)

                def weigh(p, src, at=None):
                    i2 = 2 * more_pairs(at) + 2 * p
                    g2 = G[:, ds(i2, 2), :] if at else G[:, i2:i2 + 2, :]
                    TTn(wf[:, p % 2, :].rearrange("p (i t) -> p i t", i=2),
                        src.rearrange("p (i t) -> p i t", i=2), g2, ALU.mult).then_inc(S(f"wf_ready{l}"), 1)

                def weigh_back(p, at=None):
                    in_loop = 32 * at[0] if at else 0
                    dve.wait_ge(S(f"z_in{l}_{p % 3}"), in_loop + 16 * (p // 3 + 1))
                    weigh(p, z_back[p % 3], at)

                def weigh_bank(p, at=None):
                    dve.wait_ge(S(f"act_done{l}"), more_pairs(at) + (p + 1))
                    weigh(p, PS[4 + p % 2][:, :], at)

                def weights_low(p, at=None):
                    dve.wait_ge(S(f"w_high{l}"), more_pairs(at) + (p + 1))
                    TTn(w_lo[:, p % 2, :], wf[:, p % 2, :], w_hi[:, p % 2, :].bitcast(fp32), ALU.subtract)\
                        .then_inc(S(f"w_ready{l}"), 1)

                dve.wait_ge(S(f"g_evac{l}"), T // 4)
                for k in range(2):
                    dve.wait_ge(S(f"z_out{l}_{k}"), 16 * AHEAD // 2)
                for k in range(RING):
                    low(up_ahead(l, 0) + k)
                weigh_back(0)
                weights_low(0)

                def up_pair(p, at=None, following=True):
                    m = up_ahead(l, p)
                    if following:
                        weigh_back(p + 1, at)
                    low(m + RING, at)
                    if following:
                        weights_low(p + 1, at)
                    low(m + RING + 1, at)

                for p in range(3):
                    up_pair(p)
                with dve.Fori(0, 5) as q:
                    for p in range(3, 9):
                        up_pair(p, (q, 12))
                up_pair(AHEAD - 1, following=False)

                def turn(s, at=None):
                    m, p = turn_block(l, s), AHEAD + 2 * s
                    low(m + 3, at)
                    low(m + 4, at)
                    weigh_bank(p + 1, at)
                    low(m + 5, at)
                    weights_low(p + 1, at)
                    if s == TURNS - 1:
                        return
                    for k in (6, 7, 8):
                        low(m + k, at)
                    weigh_bank(p + 2, at)
                    low(m + 9, at)
                    weights_low(p + 2, at)
                    low(m + 10, at)

                m = turn_block(l, 0)
                low(m + 1)
                low(m + 2)
                weigh_bank(AHEAD)
                weights_low(AHEAD)
                turn(0)
                turn(1)
                with dve.Fori(0, 4) as q:
                    for r in range(3):
                        turn(2 + r, (q, 24))
                turn(TURNS - 1)
                dve.wait_ge(S(f"x_back{l}"), 16)
                for tt in range(TT):
                    for q in range(2):
                        dve.wait_ge(S(f"yT_ps{l}"), tt * 2 + q + 1)
                        for k in range(4):
                            c = q * 4 + k
                            d = xT[:, c, tt * P:(tt + 1) * P]
                            src = PS[4 + tt * 2 + q][:, k * P:(k + 1) * P]
                            if l == 0:
                                last = STT(d, src, mod[:, 5 * KC + c:5 * KC + c + 1], d, ALU.mult, ALU.add)
                            else:
                                last = TTn(d, src, d, ALU.add)
                link(last, f"x_peer{l}")

            peer(0, lambda c: mod[:, 4 * KC + c:4 * KC + c + 1], lambda c: mod[:, 3 * KC + c:3 * KC + c + 1])
            norm_dve("final", xT[:, :, :], xT[:, :, :], lambda c: col("norm_final", c))
            norm_dve("mix2", xT[:, :, :], hT[:, :, :], lambda c: col("norm1", c))
            split_low("mix2", hT[:, :, :])
            v.memset(xa[:, :, 0:TAPS - 1], 0.0)
            link(v.memset(cbv[:, :, 0:TAPS_B - 1], 0.0), "pads2_ready")
            softplus_u(lru_s[:, 1, :], lru_s[:, 2, :], "lam_exp", "lam_1pe")
            dve.wait_ge(S("lam_ln"), 1)
            log1p(lru_s[:, 1, :], lru_s[:, 2, :], lru_s[:, 3, :], lru_s[:, 6, :])
            link(TS(lru_s[:, 2, :], col("lam", 0, 8), -1.0, 0.0, ALU.mult, ALU.max))
            link(TTn(lru_s[:, 3, :], lru_s[:, 3, :], lru_s[:, 2, :], ALU.add))
            link(TS(lru_s[:, 4, :], lru_s[:, 3, :], -8.0, None, ALU.mult))
            link(TS(lru_s[:, 5, :], lru_s[:, 3, :], 8.0, None, ALU.mult), "lam_ready")

            def conv(dst, src, name, bias, taps):
                for j in range(KC):
                    if bias:
                        last = TS(dst[:, j, :], src[:, j, 0:T], col(name, j), col(bias, j), ALU.mult, ALU.add)
                    else:
                        last = TS(dst[:, j, :], src[:, j, 0:T], col(name, j), None, ALU.mult)
                link(last)
                for k in range(1, taps):
                    for j in range(KC):
                        last = STT(dst[:, j, :], src[:, j, k:k + T], col(name, k * KC + j), dst[:, j, :],
                                   ALU.mult, ALU.add)
                    if k < taps - 1:
                        link(last)
                return last

            dve.wait_ge(S("in2_evac"), KC)
            link(conv(xc, xa, "conv_a_w", "conv_a_b", TAPS), "xc_ready")
            dve.wait_ge(S("av_ready"), 1)
            link(TTn(hs[:, :, :], av[:, :, :], av[:, :, :], ALU.mult))
            dve.wait_ge(S("th_ready"), 1)
            link(STT(th[:, :, :].rearrange("p a b -> p (a b)"), hs[:, :, :].rearrange("p a b -> p (a b)"), 1.0,
                     th[:, :, :].rearrange("p a b -> p (a b)"), ALU.add, ALU.mult), "mult_sq")
            link(TTn(ig[:, :, :], ig[:, :, :], xc[:, :, :], ALU.mult))
            dve.wait_ge(S("mult_ready"), 1)
            link(TTn(ig[:, :, :], ig[:, :, :], th[:, :, :], ALU.mult))
            for j in range(KC):
                last = v.tensor_tensor_scan(hs[:, j, :], av[:, j, :], ig[:, j, :], 0.0, ALU.mult, ALU.add)
            link(last)
            link(TTn(hs[:, :, :], hs[:, :, :], sma[:, :, :], ALU.mult))
            dve.wait_ge(S("in2_evac"), 5 * KC)
            link(TTn(cbv[:, :, TAPS_B - 1:], cbv[:, :, TAPS_B - 1:], vb[:, :, :], ALU.mult))
            link(conv(rg, cbv, "conv_b_w", None, TAPS_B))
            link(TTn(rg[:, :, :], rg[:, :, :], smb[:, :, :], ALU.mult))
            dve.wait_ge(S("in2_evac"), 6 * KC)
            link(TTn(rg[:, :, :], rg[:, :, :], bb[:, :, :], ALU.mult))
            dve.wait_ge(S("in2_evac"), 7 * KC)
            link(TTn(gg[:, :, :], gg[:, :, :], hs[:, :, :], ALU.mult))
            link(TTn(gg[:, :, :], gg[:, :, :], rg[:, :, :], ALU.add), "norm_done")
            split_low("merged", gg[:, :, :])
            for m in range(RING):
                make_low(dve, v, first["w_out2"] + m)
            for m in range(KC):
                if m + RING < KC:
                    make_low(dve, v, first["w_out2"] + m + RING)
                dve.wait_ge(S("block_used"), first["w_out2"] + m + 1)
                TTn(xT[:, m, :], PS[m % 4][:, 0:T], xT[:, m, :], ALU.add).then_inc(S("w_out2_evac"), 1)
            dve.wait_ge(S("w_out2_evac"), KC)
            peer(1, lambda c: col("norm2", c), None)
            norm_dve("fin", xT[:, :, :], hT[:, :, :], lambda c: col("final", c))

        @block.gpsimd
        def _(pool):
            for s in range(6):
                if s >= 2:
                    pool.wait_ge(S("ada_acc"), s - 1)
                pool.dma_start(ada_buf[:, s % 2, :], A["w_ada"][s]).then_inc(S(f"ada_in{s % 2}"), 16)
            for j in range(24):
                make_low(pool, nc.gpsimd, first["w_in"] + j)
            pool.wait_ge(S("w_in_evac"), 4)
            pool.wait_ge(S("ada_free"), 1)
            pool.wait_ge(S("inv_in"), 16)
            g_ = nc.gpsimd
            n = 0

            def link(ins):
                nonlocal n
                n += 1
                ins.then_inc(S("pool_chain"), 1)
                pool.wait_ge(S("pool_chain"), n)

            for g, w in enumerate(POOL_W):
                cur, half = u_pad[:, g, :], 0
                step = 1
                while step < w:
                    dst = p_sum[:, half, :]
                    link(g_.tensor_tensor(dst[:, UPAD:], cur[:, UPAD:], cur[:, UPAD - step:UPAD - step + T], ALU.add))
                    cur, half, step = dst, 1 - half, step * 2
                link(g_.tensor_tensor(p_t[:, g, :], cur[:, UPAD:], inv[:, g, :], ALU.mult))
                ins = g_.tensor_tensor(p_mix[:, g, :], p_t[:, g, :], u_pad[:, g, UPAD:], ALU.subtract)
                if g == NPOOL - 1:
                    ins.then_inc(S("pmix_ready"), 1)
                else:
                    link(ins)

            def peer(l):
                normed(pool, f"ffn{l}")
                pool.dma_start(A["x_spill"], xT[:, :, :]).then_inc(S(f"x_out{l}"), 16)
                for p in range(4):
                    for k in range(2):
                        make_low(pool, g_, down_ahead(l, p) + k)
                with pool.Fori(0, 5) as q:
                    for p in range(4, 10):
                        for k in range(2):
                            make_low(pool, g_, down_ahead(l, p) + k, (q, 12))

            peer(0)
            for s in range(SECT * KC):
                make_low(pool, nc.gpsimd, (first["w_in2"] if s < 3 * KC else first["w_in2b"] - 3 * KC) + s)
            peer(1)


def _chunks(w, n):
    k, m = w.shape
    return np.ascontiguousarray(w.reshape(k // P, P, m // n, n).transpose(2, 1, 0, 3)).reshape(m // n, P, -1)


def _columns(v):
    return np.ascontiguousarray(v.reshape(-1, P).T)


def kernel(**inputs):
    import concourse.bacc as bacc
    from concourse.bass_utils import run_bass_kernel_spmd

    I = {k: np.asarray(v) for k, v in inputs.items()}
    f = np.float32
    prm = {
        "c": _columns(I["c"][0]), "b_ada": _columns(I["b_ada"][0]), "norm_mix": _columns(I["norm_mix"][0]),
        "norm_ffn": _columns(I["norm_ffn"][0]), "pool_b": _columns(I["pool_b"][0]),
        "pool_scale": _columns(I["pool_scale"][0]), "conv_w": _columns(I["conv_w"][0]),
        "conv_b": _columns(I["conv_b"][0]), "d_skip": _columns(np.repeat(I["d_skip"][0], HD)),
        "ssd_norm": _columns(I["ssd_norm"][0]), "norm_final": _columns(I["norm_final"]),
        "dt_bias": np.pad(I["dt_bias"][0], (0, P - HEADS))[:, None],
        "a_log": np.pad(I["a_log"][0], (0, P - HEADS))[:, None],
        "norm1": _columns(I["norm1_g_2"][0]), "conv_a_w": _columns(I["conv_a_w_2"][0]),
        "conv_a_b": _columns(I["conv_a_b_2"][0]), "b_a": _columns(I["b_a_2"][0]), "b_x": _columns(I["b_x_2"][0]),
        "lam": _columns(I["lru_lambda_2"][0]), "conv_b_w": _columns(I["conv_b_w_2"][0]),
        "norm2": _columns(I["norm2_g_2"][0]), "final": _columns(I["final_g_2"]),
    }
    cst = np.zeros((P, NCONST), f)
    cst[:, CIDENT:CIDENT + P] = np.eye(P)
    cst[:, CONES:CONES + P] = 1.0
    cst[:, CMASK:CMASK + P] = np.where(np.arange(P)[:, None] <= np.arange(P)[None, :], 0.0, -1e38)
    cst[:, CIOTA:CIOTA + P] = np.arange(P)
    inv = np.zeros((P, NPOOL, T), f)
    for g, w in enumerate(POOL_W):
        inv[:, g] = 1.0 / np.minimum(np.arange(T) + 1, w)

    w_in = I["w_in"][0]
    w_in2 = I["w_in_2"][0].reshape(D, 7, D)[:, [0, 5, 6, 2, 4, 3, 1]].reshape(D, 7 * D)
    keys0 = np.stack([I["sub_keys1"][0], I["sub_keys2"][0]], axis=1)
    keys1 = I["peer_subkeys_2"][0]

    def down(t):
        return np.ascontiguousarray(t.reshape(NKEYS, NKEYS, KC, P).transpose(1, 3, 2, 0)).reshape(NKEYS, P, D)

    def up(t):
        return np.ascontiguousarray(t.reshape(NKEYS, NKEYS, D).transpose(1, 0, 2))

    def keys(k):
        return np.ascontiguousarray(k.reshape(LISTS, NKEYS, P).transpose(2, 0, 1)).reshape(P, LISTS * NKEYS)

    def heads(a, x):
        w = np.stack([a, x], axis=1).reshape(2, 4, 2, P, P)
        return np.ascontiguousarray(w.transpose(0, 3, 1, 2, 4)).reshape(2, P, BLK)

    arrays = {
        "prm": np.concatenate([prm[n] for n, _ in _COLS], axis=1),
        "cst": cst, "inv": inv,
        "xT": I["x"][0].T.reshape(KC, P, T).transpose(1, 0, 2),
        "w_ada": I["w_ada"][0].reshape(KC, P, 6, D).transpose(2, 1, 0, 3).reshape(6, P, KC * D),
        "w_in": _chunks(w_in[:, :24 * P], P), "w_dt": _chunks(w_in[:, 24 * P:], HEADS)[0],
        "pool_w": I["pool_w"][0].transpose(1, 0, 2).reshape(P, NPOOL * P),
        "w_out": _chunks(I["w_out"][0], P),
        "wq0": _chunks(I["w_query"][0], P), "keys0": keys(keys0),
        "down0": down(I["expert_down"][0]), "up0": up(I["expert_up"][0]),
        "w_in2": _chunks(w_in2, P), "w_gates2": heads(I["w_a_2"][0], I["w_x_2"][0]),
        "w_out2": _chunks(I["w_out_2"][0], P),
        "wq1": _chunks(I["peer_wq_2"][0], P), "keys1": keys(keys1),
        "down1": down(I["peer_u_2"][0]), "up1": up(I["peer_v_2"][0]),
    }
    nc = bacc.Bacc("TRN2", target_bir_lowering=False, num_devices=1)
    feed, A = {}, {}
    for name, a in arrays.items():
        a = np.ascontiguousarray(a)
        feed[f"in_{name}"] = a
        A[name] = nc.dram_tensor(f"in_{name}", a.shape, mybir.dt.from_np(a.dtype), kind="ExternalInput").ap()
    out = nc.dram_tensor("out", (P, KC, T), mybir.dt.float32, kind="ExternalOutput").ap()
    for name, shape in (("z0", (NKEYS // 2, P, 512)), ("z1", (NKEYS // 2, P, 512)), ("x_spill", (P, KC, T))):
        A[name] = nc.dram_tensor(f"kept_{name}", shape, mybir.dt.float32, kind="Internal").ap()
    decoder_kernel(nc, A, out)
    r = run_bass_kernel_spmd(nc, [feed], core_ids=[0])
    y = r.results[0]["out"]
    return np.ascontiguousarray(y.transpose(2, 1, 0)).reshape(1, T, D)
```

```python
import numpy as np
import concourse.bass as bass
from concourse import mybir
from contextlib import ExitStack

P = 128
D = 1024
KC = D // P
T = 256
TT = T // P
POOL_W = (2, 4, 8, 16)
NPOOL = len(POOL_W)
UPAD = max(POOL_W)
SSD_TILES = 8
XBC_TILES = 12
HEADS = 16
HPG = 8
HD = 64
CH = 128
NCH = T // CH
TAPS = 4
TAPS_B = 3
PH = 8
LISTS = 2 * PH
TOPK = 16
NKEYS = 128
EPS = 1e-6
RING = 3
BLK = KC * P
LOWEST = -3.0e38

_COLS = [("c", 8), ("b_ada", 48), ("norm_mix", 8), ("norm_ffn", 8), ("pool_b", 4), ("pool_scale", 4),
         ("conv_w", 48), ("conv_b", 12), ("d_skip", 8), ("ssd_norm", 8), ("norm_final", 8), ("dt_bias", 1),
         ("a_log", 1), ("norm1", 8), ("conv_a_w", 32), ("conv_a_b", 8), ("b_a", 8), ("b_x", 8), ("lam", 8),
         ("conv_b_w", 24), ("norm2", 8), ("final", 8)]
COL = {}
_at = 0
for _n, _w in _COLS:
    COL[_n] = (_at, _w)
    _at += _w
NCOL = _at
CIDENT, CONES, CMASK, CIOTA = 0, P, 2 * P, 3 * P
NCONST = 4 * P


def decoder_kernel(nc, A, out):
    fp32 = mybir.dt.float32
    fp32r = mybir.dt.float32r
    u32 = mybir.dt.uint32
    ALU = mybir.AluOpType
    ACT = mybir.ActivationFunctionType
    AX = mybir.AxisListType
    ds = bass.ds

    ctx = ExitStack()
    with ctx:
        def sb(name, shape, dt=fp32):
            return ctx.enter_context(nc.sbuf_tensor(name, shape, dt))

        sems = {}

        def S(name):
            if name not in sems:
                sems[name] = ctx.enter_context(nc.semaphore(name))
            return sems[name]

        NORMS = ["mix", "ssd", "ffn0", "final", "mix2", "ffn1", "fin"]
        NORMED = ["mix", "ssd", "ffn0", "final", "mix2", "merged", "ffn1", "fin"]
        SPLITS = ["mix", "ffn0", "mix2", "merged", "ffn1"]

        HC = KC // 2

        def normed(eng, tag, halves=2):
            eng.wait_ge(S("norm_done"), 2 * NORMED.index(tag) + halves)

        def split_ready(eng, tag, halves=2):
            eng.wait_ge(S("h_split"), 2 * SPLITS.index(tag) + halves)

        xT = sb("xT", [P, KC, T])
        h_hi = sb("h_hi", [P, KC, T], fp32r)
        h_lo = sb("h_lo", [P, KC, T], fp32r)
        prm = sb("prm", [P, NCOL])
        cst = sb("cst", [P, NCONST])
        ring = sb("ring", [P, RING, BLK])
        ring_hi = sb("ring_hi", [P, RING, BLK], fp32r)
        ring_lo = sb("ring_lo", [P, RING, BLK], fp32r)
        arena = sb("arena", [P, 32768])
        wf = sb("wf", [P, 2, 512])
        w_hi = sb("w_hi", [P, 2, 512], fp32r)
        w_lo = sb("w_lo", [P, 2, 512], fp32r)
        selT = sb("selT", [P, 3, T])
        stage = sb("stage", [P, 3, 8])
        mod = sb("mod", [P, 48])
        cact = sb("cact", [P, 8])
        epsc = sb("epsc", [P, 1])
        lru_s = sb("lru_s", [P, 8, 8])
        PS = [ctx.enter_context(nc.psum_tensor(f"ps{i}", [P, 512], fp32)) for i in range(8)]

        ident = cst[:, CIDENT:CIDENT + P]
        ones = cst[:, CONES:CONES + P]
        mask = cst[:, CMASK:CMASK + P]
        iota = cst[:, CIOTA:CIOTA + P]

        def col(name, i, n=1):
            a = COL[name][0] + i
            return prm[:, a:a + n]

        def region(at, *shape):
            n = int(np.prod(shape))
            v = arena[:, at:at + n]
            if len(shape) == 2:
                return v.rearrange("p (a b) -> p a b", b=shape[1])
            if len(shape) == 3:
                return v.rearrange("p (a b c) -> p a b c", b=shape[1], c=shape[2])
            return v

        ada_buf = [region(0, KC, D), region(8192, KC, D)]
        ada_buf_late = [region(20544, KC, D), region(8192, KC, D)]
        ada_acc = region(16384, 2, D)
        sq = region(18432, KC, T)
        xbc = region(18432, XBC_TILES, T)
        u_pad = region(21504, NPOOL, UPAD + T)
        zs = region(22592, KC, T)
        xbc_in = region(24640, XBC_TILES, TAPS - 1 + T)
        hT = region(27748, KC, T)
        inv = region(29796, NPOOL, T)
        dts = region(30820, 6, T)
        rstd = region(32356, T)
        xdt = region(0, NCH, D)
        xdte = region(2048, D)
        btok = region(3072, 2, P)
        cbt = region(3328, 2, NCH * P)
        stT = region(3840, D)
        mixT = region(4864, NPOOL + SSD_TILES, T)
        tok = region(7936, 5, HEADS)
        seg = region(8192, 2, T)
        dec = region(8704, 2, T)
        mdec = region(9216, 2, T)
        ecs = region(9728, 2, P)
        cexp = region(9984, 2, P)
        p_sum = region(10240, 2, UPAD + T)
        p_mix = region(10784, NPOOL, T)
        p_t = region(11808, NPOOL, T)

        qT = region(0, LISTS, T)
        sc = region(4096, TT, LISTS, NKEYS)
        sc2 = region(8192, TT, LISTS, NKEYS)
        NC2 = TOPK * TOPK
        cand = region(12288, TT, PH, NC2)
        cand2 = region(16384, TT, PH, NC2)
        vv = region(20480, TT, LISTS, TOPK)
        ii = region(20992, TT, LISTS, TOPK).bitcast(u32)
        iif = region(21504, TT, LISTS, TOPK)
        tv = region(22016, TT, PH, TOPK)
        tp = region(22272, TT, PH, TOPK).bitcast(u32)
        ab = region(22528, TT, 2, PH * TOPK).bitcast(u32)
        abf = region(23040, TT, 2, PH * TOPK)
        oh = region(24576, PH, TOPK, TOPK)
        pick = region(28672, TT, 3, PH * TOPK)
        gsum = region(29440, TT, PH, 1)
        grec = region(29504, TT, PH, 1)
        G = arena[:, :].rearrange("p (i t) -> p i t", t=T)
        ytok = region(0, TT, D)
        x_flat = xT[:, :, :].rearrange("p c t -> p (c t)")
        onehot = [[x_flat[:, (2 * k + half) * 512:(2 * k + half + 1) * 512] for half in range(2)] for k in range(2)]
        z_back = [x_flat[:, k * 512:(k + 1) * 512] for k in range(3)]
        xa = region(0, KC, TAPS - 1 + T)
        xc = region(2080, KC, T)
        sma = region(4128, KC, T)
        smb = region(6176, KC, T)
        rg = region(8224, KC, T)
        ig = region(10272, KC, T)
        vb = region(12320, KC, T)
        cbv = region(14368, KC, TAPS_B - 1 + T)
        bb = region(20800, KC, T)
        gg = region(22848, KC, T)
        av = region(24896, KC, T)
        th = region(16440, KC, T)
        hs = region(29100, KC, T)

        ROW_BANKS = (0, 1, 6, 7)

        def ada_order(s):
            return (2, 3, 0, 1) if s == 4 else (0, 1, 2, 3)

        blocks = []

        def add(label, src, width=BLK, split=None):
            blocks.append((label, src, width, split))

        first = {}

        def mark(label):
            first[label] = len(blocks)

        AHEAD, AHEAD_TOP = 36, 19

        mark("w_in")
        for j in [*range(12, 24), *range(0, 12)]:
            if j == 0:
                mark("w_dt")
                add("w_in", A["w_dt"], KC * HEADS)
            add("w_in", A["w_in"][j], split="pool")

        def w_in_block(i):
            return first["w_in"] + i + (i >= XBC_TILES)

        mark("pool_w")
        add("pool_w", A["pool_w"], NPOOL * P)
        mark("w_out")
        for m in range(KC):
            add("w_out", A["w_out"][m][:, 0:BLK])
            add("w_out", A["w_out"][m][:, BLK:BLK + 4 * P], 4 * P)
        PAIRS = NKEYS // 2
        TURNS = (PAIRS - AHEAD) // 2

        def peer_blocks(l):
            mark(f"wq{l}")
            for j in range(LISTS):
                add("wq", A[f"wq{l}"][j], split="dve")
            mark(f"keys{l}")
            for j in range(2):
                add("keys", A[f"keys{l}"][:, j * BLK:(j + 1) * BLK])
            mark(f"exp{l}")
            for i in range(4 * PAIRS):
                add("exp", None, split="pool" if i < 2 * AHEAD + 2 else "dve")

        peer_blocks(0)
        mark("w_in2")
        SECT = 7
        for s in range(SECT * KC):
            if s == 3 * KC:
                mark("gates2")
                for i in range(2):
                    add("gates2", A["w_gates2"][i])
                mark("w_in2b")
            add("w_in2", A["w_in2"][s], split="pool")
        mark("w_out2")
        for m in range(KC):
            add("w_out2", A["w_out2"][m], split="dve")
        peer_blocks(1)

        def down_ahead(l, p):
            return first[f"exp{l}"] + 2 * p

        def up_ahead(l, p):
            return first[f"exp{l}"] + 2 * AHEAD + 2 + 2 * p

        def turn_block(l, s):
            return first[f"exp{l}"] + 4 * AHEAD + 2 + 8 * s

        def more(at):
            return at[0] * at[1] if at else 0

        def more_in(at):
            return at[0] * (16 * at[1] // RING) if at else 0

        def more_pairs(at):
            return 6 * at[0] if at else 0

        split_no, low_no = [], []
        seen = {"all": 0, "dve": 0, "pool": 0}
        for _, _, _, who in blocks:
            split_no.append(seen["all"])
            low_no.append(seen[who] if who else None)
            if who:
                seen["all"] += 1
                seen[who] += 1

        def slot(n):
            return n % RING

        def part_slot(n):
            return split_no[n] % RING

        def last_split(n):
            before = [m for m in range(n) if blocks[m][3]]
            return before[-RING] if len(before) >= RING else None

        def wait_parts(eng, n, at=None):
            eng.wait_ge(S(f"low_{blocks[n][3]}"), more(at) + (low_no[n] + 1))

        def wait_slot(eng, n):
            m = n - RING
            if m >= 0:
                if blocks[m][3]:
                    wait_parts(eng, m)
                else:
                    eng.wait_ge(S("block_used"), m + 1)

        def make_high(act, m, at=None):
            act.wait_ge(S(f"block_in{slot(m)}"), more_in(at) + 16 * (m // RING + 1))
            if at:
                act.wait_ge(S("block_used"), more(at) + (m - RING + 1))
            elif last_split(m) is not None:
                act.wait_ge(S("block_used"), last_split(m) + 1)
            nc.scalar.activation(ring_hi[:, part_slot(m), :], ring[:, slot(m), :],
                                 ACT.Copy).then_inc(S("high"), 1)

        def make_low(eng, ns, n, at=None):
            eng.wait_ge(S("high"), more(at) + (split_no[n] + 1))
            ns.tensor_tensor(ring_lo[:, part_slot(n), :], ring[:, slot(n), :],
                             ring_hi[:, part_slot(n), :].bitcast(fp32), ALU.subtract)\
                .then_inc(S(f"low_{blocks[n][3]}"), 1)

        def full(eng, n):
            eng.wait_ge(S(f"block_in{slot(n)}"), 16 * (n // RING + 1))

        block = ctx.enter_context(nc.Block())

        @block.sync
        def _(sp):
            ADA_Q = 4

            def ada_load(s, k):
                buf = (ada_buf if s < 4 else ada_buf_late)[s % 2]
                w = KC * D // ADA_Q
                sp.dma_start(buf.rearrange("p c n -> p (c n)")[:, k * w:(k + 1) * w],
                             A["w_ada"][s][:, k * w:(k + 1) * w]).then_inc(S(f"ada_in{s % 2}_{k}"), 16)

            sp.dma_start(prm[:, :], A["prm"]).then_inc(S("prm_in"), 16)
            sp.dma_start(cst[:, :], A["cst"]).then_inc(S("cst_in"), 16)
            sp.dma_start(xT[:, :, :], A["xT"]).then_inc(S("x_in"), 16)
            for s in range(2):
                for k in range(ADA_Q):
                    ada_load(s, k)

            def load(n, src, width):
                wait_slot(sp, n)
                sp.dma_start(ring[:, slot(n), 0:width], src).then_inc(S(f"block_in{slot(n)}"), 16)

            def experts(l):
                def table_load(name, i2, m, at=None):
                    if at:
                        sp.wait_ge(S(f"low_{blocks[m - RING][3]}"), more(at) + (low_no[m - RING] + 1))
                        src = A[f"{name}{l}"][ds(i2, 1), :, :].rearrange("a p n -> (a p) n")
                    else:
                        wait_slot(sp, m)
                        src = A[f"{name}{l}"][i2]
                    sp.dma_start(ring[:, slot(m), :], src).then_inc(S(f"block_in{slot(m)}"), 16)

                def down_loads(p, at=None):
                    for k in range(2):
                        table_load("down", more(at) + (2 * p + k), down_ahead(l, p) + k, at)

                for p in range(4):
                    down_loads(p)
                with sp.Fori(0, 5) as q:
                    for p in range(4, 10):
                        down_loads(p, (q, 12))
                for p in range(34, AHEAD + 1):
                    down_loads(p)

                def z_load(p, at=None):
                    if p >= 3:
                        sp.wait_ge(S(f"wf_ready{l}"), more_pairs(at) + (p - 2))
                    src = A[f"z{l}"][ds(more_pairs(at) + p, 1), :, :].rearrange("a p n -> (a p) n") if at \
                        else A[f"z{l}"][p]
                    sp.dma_start(z_back[p % 3], src).then_inc(S(f"z_in{l}_{p % 3}"), 16)

                def up_loads(p, at=None):
                    for k in range(2):
                        table_load("up", more(at) + (2 * p + k), up_ahead(l, p) + k, at)

                up_loads(0)
                sp.wait_ge(S(f"g_ps{l}"), T // 4)
                for k in range(2):
                    sp.wait_ge(S(f"z_out{l}_{k}"), 16 * (AHEAD_TOP // 2))
                z_load(0)
                z_load(1)
                for p in range(1, 3):
                    up_loads(p)
                    z_load(p + 1)
                with sp.Fori(0, 5) as q:
                    for p in range(3, 9):
                        up_loads(p, (q, 12))
                        if p == 8:
                            for k in range(2):
                                sp.wait_ge(S(f"z_out{l}_{k}"), 16 * AHEAD // 2)
                        z_load(p + 1, (q, 12))
                for p in range(33, AHEAD):
                    up_loads(p)
                    if p + 1 < AHEAD:
                        z_load(p + 1)

                table = [("down", 2), ("down", 3), ("up", 0), ("up", 1), ("down", 4), ("down", 5), ("up", 2), ("up", 3)]

                def turn_loads(s, q=None, rows=range(8)):
                    for k, (name, add_i) in enumerate([table[r] for r in rows]):
                        i2 = 2 * AHEAD + 4 * s + add_i
                        table_load(name, 12 * q + i2 if q is not None else i2, turn_block(l, s) + k,
                                   (q, 24) if q is not None else None)

                turn_loads(0)
                turn_loads(1)
                with sp.Fori(0, 3) as q:
                    for r in range(3):
                        turn_loads(2 + r, q)
                turn_loads(11)
                turn_loads(12)
                turn_loads(TURNS - 1, rows=(0, 1, 2, 3, 6, 7))
                sp.wait_ge(S(f"wf_ready{l}"), AHEAD)
                sp.dma_start(xT[:, :, :], A["x_spill"]).then_inc(S(f"x_back{l}"), 16)

            n = 0
            while n < len(blocks):
                label, src, width, _ = blocks[n]
                if label == "exp":
                    l = 0 if n == first["exp0"] else 1
                    experts(l)
                    n += 4 * PAIRS
                else:
                    load(n, src, width)
                    i = n - first["w_in"] - RING
                    if i == 0:
                        sp.dma_start(inv[:, :, :], A["inv"]).then_inc(S("inv_in"), 16)
                    if 0 <= i < 16 and i % 2 == 0:
                        if i % 8 == 0:
                            sp.wait_ge(S("ada_acc"), i // 8 + 1)
                        ada_load(2 + i // 8, i // 2 % 4)
                    if label == "pool_w":
                        sp.wait_ge(S("conv_ready"), 1)
                        sp.wait_ge(S("block_used"), first["w_dt"] + 1)
                        ada_load(4, 2)
                        ada_load(4, 3)
                    i = (n - first["w_out"]) // 2
                    if label == "w_out" and (n - first["w_out"]) % 2 == 1 and i < 6:
                        if i == 0:
                            sp.wait_ge(S("y_gated"), 1)
                            sp.wait_ge(S("pool_out"), 1)
                        ada_load(*[(4, 0), (4, 1), (5, 0), (5, 1), (5, 2), (5, 3)][i])
                    n += 1
            normed(sp, "fin")
            sp.dma_start(out, hT[:, :, :]).then_inc(S("out_done"), 16)
            sp.wait_ge(S("out_done"), 16)

        @block.tensor
        def _(pe):
            mm = nc.tensor.matmul

            def norm_sum(tag, bank=4):
                for c in range(KC):
                    if c % HC == 0:
                        pe.wait_ge(S("sq_ready"), 2 * NORMS.index(tag) + c // HC + 1)
                    last = mm(PS[bank][:, 0:T], ones, sq[:, c, :], start=(c == 0), stop=(c == KC - 1))
                last.then_inc(S("sumsq"), 1)

            def ada(s):
                pe.wait_ge(S("ada_acc"), s + 1)
                for j in range(KC):
                    last = mm(PS[7][:, s * KC + j:s * KC + j + 1], ada_acc[:, s % 2, j * P:(j + 1) * P],
                              ones[:, 0:1], start=True, stop=True)
                last.then_inc(S("ada_ps"), 1)

            def product(psum, stat, move, start, stop):
                (s_hi, s_lo), (m_hi, m_lo) = stat, move
                mm(psum, s_lo, m_hi, start=start, stop=False)
                mm(psum, s_hi, m_lo, start=False, stop=False)
                return mm(psum, s_hi, m_hi, start=False, stop=stop)

            def parts(n, a, b):
                return ring_hi[:, part_slot(n), a:b], ring_lo[:, part_slot(n), a:b]

            def split_linear(n, psum, at=None, tag=None):
                wait_parts(pe, n, at)
                for c in range(KC):
                    if tag and c % HC == 0:
                        split_ready(pe, tag, c // HC + 1)
                    last = product(psum, parts(n, c * P, (c + 1) * P), (h_hi[:, c, :], h_lo[:, c, :]),
                                   c == 0, c == KC - 1)
                last.then_inc(S("block_used"), 1)

            def linear(n, psum, src, width=P, chunks=KC):
                full(pe, n)
                for c in range(chunks):
                    last = mm(psum, ring[:, slot(n), c * width:(c + 1) * width], src[:, c, :],
                              start=(c == 0), stop=(c == chunks - 1))
                last.then_inc(S("block_used"), 1)

            pe.wait_ge(S("cst_in"), 16)
            norm_sum("mix")
            ada(0)
            ada(1)

            def in_product(i):
                if i >= 3:
                    pe.wait_ge(S("w_in_evac"), i - 2 + (i - 3 >= XBC_TILES))
                split_linear(w_in_block(i), PS[i % 3][:, 0:T], tag="mix" if i == 0 else None)

            for i in range(XBC_TILES):
                in_product(i)
                if i == 10:
                    pe.wait_ge(S("mod_ready"), 2)
                    ada(2)
            linear(first["w_dt"], PS[5][0:HEADS, 0:T], hT, width=HEADS)
            for i in range(XBC_TILES, XBC_TILES + 8):
                in_product(i)

            pe.wait_ge(S("acs_ready"), 1)
            pe.wait_ge(S("dte_ready"), 1)
            for i, (row, c) in enumerate([(2, 0), (2, 1), (4, 0), (4, 1), (5, 0)]):
                last = nc.tensor.transpose(PS[7][:, P + i * HEADS:P + (i + 1) * HEADS],
                                           dts[0:HEADS, row, c * CH:(c + 1) * CH], ident[0:HEADS, 0:HEADS])
            last.then_inc(S("tok_ps"), 1)
            pe.wait_ge(S("xbc_ready"), 1)
            for g in range(2):
                last = nc.tensor.transpose(PS[7][:, (2 + g) * P:(3 + g) * P], xbc[:, 8 + g, 0:CH], ident)
            last.then_inc(S("btok_ps"), 1)
            for b in range(4):
                for k in range(4):
                    last = nc.tensor.transpose(PS[3 + b][:, k * P:(k + 1) * P],
                                               xbc[:, (b % 2) * 4 + k, (b // 2) * CH:(b // 2 + 1) * CH], ident)
                last.then_inc(S("xtok_ps"), 1)
            in_product(20)
            pe.wait_ge(S("tok_ready"), 1)
            pe.wait_ge(S("btok_ready"), 1)
            ada(3)
            in_product(21)
            pe.wait_ge(S("xdt_ready"), 1)
            for g in range(2):
                for c in range(NCH):
                    k = g * NCH + c
                    last = mm(PS[3][:, k * P:(k + 1) * P], xbc[:, 8 + g, c * CH:(c + 1) * CH],
                              xbc[:, 10 + g, c * CH:(c + 1) * CH], start=True, stop=True)
            last.then_inc(S("cb_ps"), 1)
            in_product(22)
            pe.wait_ge(S("btok_ready"), 1)
            pe.wait_ge(S("xdte_ready"), 1)
            for g in range(2):
                last = mm(PS[4 + g][:, :], btok[:, g, :], xdte[:, g * 512:(g + 1) * 512], start=True, stop=True)
            last.then_inc(S("st_ps"), 1)
            in_product(23)

            def head_rows(h):
                if h >= len(ROW_BANKS):
                    pe.wait_ge(S("ecs_ready"), h - len(ROW_BANKS) + 1)
                mm(PS[ROW_BANKS[h % 4]][:, 0:T], ident[0:HEADS, h:h + 1].to_broadcast([HEADS, P]),
                   dts[0:HEADS, 4, :], start=True, stop=True).then_inc(S("rows_ps"), 1)

            pe.wait_ge(S("xdt_ready"), 4)
            pe.wait_ge(S("btok_ready"), 1)
            pe.wait_ge(S("mod_ready"), 4)
            pe.wait_ge(S("w_in_evac"), 25)
            pe.wait_ge(S("cb_ready"), 1)
            for h in range(4):
                head_rows(h)
            pe.wait_ge(S("st_ready"), 1)
            for h in range(HEADS):
                g, j = h // HPG, h // 2
                pe.wait_ge(S("mdec_ready"), h + 1)
                pe.wait_ge(S("cexp_ready"), h + 1)
                if j >= 2 and h % 2 == 0:
                    pe.wait_ge(S("y_evac"), j - 1)
                o = (h % 2) * HD
                dst = PS[2 + j % 2]
                mm(dst[o:o + HD, 0:CH], xdt[:, 0, h * HD:(h + 1) * HD], mdec[:, h % 2, 0:CH],
                   start=True, stop=True)
                mm(dst[o:o + HD, CH:2 * CH], xdt[:, 1, h * HD:(h + 1) * HD], mdec[:, h % 2, CH:2 * CH],
                   start=True, stop=False)
                mm(dst[o:o + HD, CH:2 * CH], stT[:, h * HD:(h + 1) * HD], cexp[:, h % 2, :],
                   start=False, stop=True).then_inc(S("y_ps"), 1)
                if h + 4 < HEADS:
                    head_rows(h + 4)
            n = first["pool_w"]
            full(pe, n)
            pe.wait_ge(S("pmix_ready"), 1)
            pe.wait_ge(S("st_ready"), 1)
            for g in range(NPOOL):
                last = mm(PS[4 + g // 2][:, (g % 2) * T:(g % 2 + 1) * T], ring[:, slot(n), g * P:(g + 1) * P],
                          p_mix[:, g, :], start=True, stop=True)
            last.then_inc(S("block_used"), 1)
            norm_sum("ssd", bank=6)
            pe.wait_ge(S("pool_out"), 1)
            for m in range(KC):
                n = first["w_out"] + 2 * m
                if m >= 4:
                    pe.wait_ge(S("w_out_evac"), m - 3)
                full(pe, n)
                for c in range(KC):
                    if m == 0 and c == NPOOL:
                        normed(pe, "ssd", 1)
                    last = mm(PS[m % 4][:, 0:T], ring[:, slot(n), c * P:(c + 1) * P], mixT[:, c, :],
                              start=(c == 0), stop=False)
                last.then_inc(S("block_used"), 1)
                full(pe, n + 1)
                if m == 0:
                    normed(pe, "ssd")
                for c in range(4):
                    last = mm(PS[m % 4][:, 0:T], ring[:, slot(n + 1), c * P:(c + 1) * P], mixT[:, KC + c, :],
                              start=False, stop=(c == 3))
                last.then_inc(S("block_used"), 1)
                if m == 5:
                    ada(4)

            def peer(l):
                norm_sum(f"ffn{l}")
                if l == 0:
                    ada(5)
                for j in range(LISTS):
                    if j >= 4:
                        pe.wait_ge(S(f"q_evac{l}"), j - 3)
                    split_linear(first[f"wq{l}"] + j, PS[j % 4][:, 0:T], tag=f"ffn{l}" if j == 0 else None)
                pe.wait_ge(S(f"q_evac{l}"), LISTS)
                for half in range(2):
                    n = first[f"keys{l}"] + half
                    full(pe, n)
                    for tt in range(TT):
                        for q in range(2):
                            for k in range(4):
                                i = half * 8 + q * 4 + k
                                last = mm(PS[(1 - tt) * 4 + half * 2 + q][:, k * P:(k + 1) * P],
                                          qT[:, i, tt * P:(tt + 1) * P],
                                          ring[:, slot(n), (i % 8) * P:(i % 8 + 1) * P], start=True, stop=True)
                    last.then_inc(S("block_used"), 1)
                def down_block(m, p, k, at=None):
                    split_linear(m + k, PS[4 + p % 2][:, k * T:(k + 1) * T], at)

                def down_ahead_pair(p, at=None, gate_turn=None):
                    if p >= 2:
                        pe.wait_ge(S(f"act_done{l}"), more_pairs(at) + (p - 1))
                    for k in range(2):
                        if gate_turn is not None:
                            gates(gate_turn + k)
                        down_block(down_ahead(l, p), p, k, at)

                def gates(it):
                    for half in range(2):
                        pe.wait_ge(S(f"onehot{l}"), 2 * it + (half + 1))
                        if not (isinstance(it, int) and it == 0):
                            pe.wait_ge(S(f"g_evac{l}"), 2 * it + (half - 1))
                        for k in range(4):
                            last = mm(PS[half][:, k * P:(k + 1) * P], onehot[0][half][:, k * P:(k + 1) * P],
                                      onehot[1][half][:, k * P:(k + 1) * P], start=True, stop=True)
                        last.then_inc(S(f"g_ps{l}"), 1)

                pe.wait_ge(S(f"sc_ready{l}"), 1)
                for p in range(6):
                    down_ahead_pair(p)
                with pe.Fori(0, 2) as q:
                    for p in range(6, 12):
                        down_ahead_pair(p, (q, 12))
                down_ahead_pair(AHEAD_TOP - 1)
                pe.wait_ge(S(f"sc_ready{l}"), 2)
                for tt in range(TT):
                    pe.wait_ge(S(f"pick_ready{l}"), tt + 1)
                    for k in range(3):
                        last = nc.tensor.transpose(PS[2 + tt][:, k * P:(k + 1) * P], pick[:, tt, k, :], ident)
                    last.then_inc(S(f"pickT_ps{l}"), 1)
                down_ahead_pair(AHEAD_TOP)
                p0 = AHEAD_TOP + 1
                for p in range(p0, p0 + 4):
                    down_ahead_pair(p, None, 2 * (p - p0))
                with pe.Fori(0, 2) as q:
                    for p in range(p0 + 4, p0 + 10):
                        down_ahead_pair(p, (q, 12), 12 * q + 2 * (p - p0))
                down_ahead_pair(AHEAD)

                def up(m, p, at=None, start=False, stop=False):
                    pe.wait_ge(S(f"w_ready{l}"), more_pairs(at) + (p + 1))
                    for k in range(2):
                        wait_parts(pe, m + k, at)
                        for tt in range(TT):
                            a = k * T + tt * P
                            for f in range(2):
                                last = product(PS[tt * 2 + f][:, :],
                                               (w_hi[:, p % 2, a:a + P], w_lo[:, p % 2, a:a + P]),
                                               parts(m + k, f * 512, (f + 1) * 512),
                                               start and k == 0, stop and k == 1)
                        last.then_inc(S("block_used"), 1)

                def down(m, p, at=None):
                    pe.wait_ge(S(f"wf_ready{l}"), more_pairs(at) + (p - 1))
                    for k in range(2):
                        down_block(m, p, k, at)

                pe.wait_ge(S(f"pickT_ready{l}"), TT)
                pe.wait_ge(S(f"g_evac{l}"), T // 4)
                for p in range(3):
                    up(up_ahead(l, p), p, start=p == 0)
                with pe.Fori(0, 5) as q:
                    for p in range(3, 9):
                        up(up_ahead(l, p), p, (q, 12))
                for p in range(33, AHEAD):
                    up(up_ahead(l, p), p)

                def turn(s, at=None):
                    m, p = turn_block(l, s), AHEAD + 2 * s
                    down(m, p + 1, at)
                    up(m + 2, p, at)
                    down(m + 4, p + 2, at)
                    up(m + 6, p + 1, at)

                turn(0)
                turn(1)
                with pe.Fori(0, 3) as q:
                    for r in range(3):
                        turn(2 + r, (q, 24))
                turn(11)
                turn(12)
                m = turn_block(l, TURNS - 1)
                down(m, PAIRS - 1)
                up(m + 2, PAIRS - 2)
                up(m + 4, PAIRS - 1, stop=True)

                for q in range(2):
                    for tt in range(TT):
                        pe.wait_ge(S(f"ytok_ready{l}"), 2 * q + tt + 1)
                        for k in range(4):
                            last = nc.tensor.transpose(PS[4 + tt * 2 + q][:, k * P:(k + 1) * P],
                                                       ytok[:, tt, (q * 4 + k) * P:(q * 4 + k + 1) * P], ident)
                        last.then_inc(S(f"yT_ps{l}"), 1)

            peer(0)
            norm_sum("final")
            norm_sum("mix2")
            for s in range(SECT * KC):
                if s >= 4:
                    pe.wait_ge(S("in2_evac"), s - 3)
                if s == 3 * KC:
                    n = first["gates2"]
                    pe.wait_ge(S("xc_ready"), 1)
                    for j in range(KC):
                        if j % 4 == 0:
                            full(pe, n + j // 4)
                        if j >= 4:
                            pe.wait_ge(S("gate_evac"), j - 3)
                        for k in range(2):
                            last = mm(PS[4 + j % 4][:, k * T:(k + 1) * T],
                                      ring[:, slot(n + j // 4), (j % 4 * 2 + k) * P:(j % 4 * 2 + k + 1) * P],
                                      xc[:, j, :], start=True, stop=True)
                        last.then_inc(S("block_used" if j % 4 == 3 else "gate_ps"), 1)
                n = (first["w_in2"] if s < 3 * KC else first["w_in2b"] - 3 * KC) + s
                split_linear(n, PS[s % 4][:, 0:T], tag="mix2" if s == 0 else None)
            pe.wait_ge(S("in2_evac"), SECT * KC)
            for m in range(KC):
                if m >= 4:
                    pe.wait_ge(S("w_out2_evac"), m - 3)
                split_linear(first["w_out2"] + m, PS[m % 4][:, 0:T], tag="merged" if m == 0 else None)
            peer(1)
            norm_sum("fin")

        @block.scalar
        def _(act):
            A_ = nc.scalar.activation

            def norm_act(tag, src, sem, vals, bank=4, first_blocks=None):
                for f in range(2):
                    act.wait_ge(S(sem), vals[f])
                    A_(sq[:, f * HC:(f + 1) * HC, :], src[:, f * HC:(f + 1) * HC, :], ACT.Square)\
                        .then_inc(S("sq_ready"), 1)
                if first_blocks is not None:
                    for k in range(RING):
                        make_high(act, first_blocks + k)
                act.wait_ge(S("sumsq"), NORMS.index(tag) + 1)
                A_(rstd, PS[bank][:, 0:T], ACT.Sqrt, bias=epsc[:, 0:1], scale=1.0 / D).then_inc(S("rms"), 1)

            def split_h(tag, src):
                for f in range(2):
                    normed(act, tag, f + 1)
                    A_(h_hi[:, f * HC:(f + 1) * HC, :], src[:, f * HC:(f + 1) * HC, :], ACT.Copy)\
                        .then_inc(S("h_high"), 1)

            def highs(n, count, evac):
                for j in range(count):
                    if j + RING < count:
                        make_high(act, n + j + RING)
                    evac(j)

            act.wait_ge(S("prm_in"), 16)
            A_(cact[:, :], col("c", 0, 8), ACT.Silu).then_inc(S("cact_ready"), 1)
            act.wait_ge(S("eps_ready"), 1)
            norm_act("mix", xT[:, :, :], "x_in", (16, 16))
            act.wait_ge(S("pads_ready"), 1)
            for i in range(RING):
                make_high(act, w_in_block(i))
            split_h("mix", hT[:, :, :])

            def evac_in(i):
                act.wait_ge(S("block_used"), w_in_block(i) + 1)
                src = PS[i % 3][:, 0:T]
                if i < 12:
                    A_(xbc_in[:, i, TAPS - 1:], src, ACT.Copy).then_inc(S("w_in_evac"), 1)
                elif i < 16:
                    A_(u_pad[:, i - 12, UPAD:], src, ACT.Copy).then_inc(S("w_in_evac"), 1)
                else:
                    A_(zs[:, i - 16, :], src, ACT.Silu).then_inc(S("w_in_evac"), 1)
                if i == 11:
                    act.wait_ge(S("block_used"), first["w_dt"] + 1)
                    A_(dts[0:HEADS, 0, :], PS[5][0:HEADS, 0:T], ACT.Identity,
                       bias=prm[0:HEADS, COL["dt_bias"][0]:COL["dt_bias"][0] + 1]).then_inc(S("w_in_evac"), 1)
                    act.wait_ge(S("w_in_evac"), 13)
                    A_(dts[0:HEADS, 1, :], dts[0:HEADS, 0, :], ACT.Abs).then_inc(S("dt_abs"), 1)
                    act.wait_ge(S("dt_abs"), 1)
                    A_(dts[0:HEADS, 1, :], dts[0:HEADS, 1, :], ACT.Exp, scale=-1.0).then_inc(S("dt_exp"), 1)
                    A_(lru_s[0:HEADS, 0, 0:1], prm[0:HEADS, COL["a_log"][0]:COL["a_log"][0] + 1], ACT.Exp)\
                        .then_inc(S("alog_exp"), 1)
                if i == 14:
                    act.wait_ge(S("dt_1pe"), 1)
                    A_(dts[0:HEADS, 3, :], dts[0:HEADS, 2, :], ACT.Ln).then_inc(S("dt_ln"), 1)
                if i == 16:
                    act.wait_ge(S("conv_ready"), 1)
                    A_(xbc[:, :, :], xbc[:, :, :], ACT.Silu).then_inc(S("xbc_ready"), 1)
                if i == 17:
                    act.wait_ge(S("acs_ready"), 1)
                    A_(dts[0:HEADS, 5, 0:CH], dts[0:HEADS, 4, 0:CH], ACT.Exp, scale=-1.0,
                       bias=dts[0:HEADS, 4, CH - 1:CH]).then_inc(S("dte_ready"), 1)
                if i == 20:
                    act.wait_ge(S("btok_ps"), 1)
                    act.wait_ge(S("tok_ready"), 1)
                    A_(btok[:, :, :], PS[7][:, 2 * P:4 * P].rearrange("p (g n) -> p g n", g=2), ACT.Copy)\
                        .then_inc(S("btok_ready"), 1)

            for i in range(24):
                if i + RING < 24:
                    make_high(act, w_in_block(i + RING))
                evac_in(i)
                if i == 22:
                    act.wait_ge(S("cb_ps"), 1)
                    A_(cbt[:, :, :], PS[3][:, :].rearrange("p (g n) -> p g n", g=2), ACT.Copy)\
                        .then_inc(S("cb_ready"), 1)
            act.wait_ge(S("st_ps"), 1)
            A_(stT[:, 0:512], PS[4][:, :], ACT.Copy)
            A_(stT[:, 512:1024], PS[5][:, :], ACT.Copy).then_inc(S("st_ready"), 1)
            act.wait_ge(S("tok_ready"), 1)
            for h in range(HEADS):
                act.wait_ge(S("seg_ready"), h + 1)
                if h >= 2:
                    act.wait_ge(S("cexp_ready"), h - 1)
                    act.wait_ge(S("mdec_ready"), h - 1)
                A_(ecs[:, h % 2, :], PS[ROW_BANKS[h % 4]][:, CH:2 * CH], ACT.Exp).then_inc(S("ecs_ready"), 1)
                for c in range(NCH):
                    last = A_(dec[:, h % 2, c * CH:(c + 1) * CH], seg[:, h % 2, c * CH:(c + 1) * CH], ACT.Exp,
                              bias=tok[:, 2 + c, h:h + 1])
                last.then_inc(S("dec_ready"), 1)
            norm_act("ssd", mixT[:, NPOOL:, :], "y_gated", (1, 1), bank=6)

            def peer(l, x_sem):
                gelu = ACT.Gelu if l == 0 else ACT.Gelu_apprx_tanh
                norm_act(f"ffn{l}", xT[:, :, :], x_sem, (HC, KC), first_blocks=first[f"wq{l}"])
                split_h(f"ffn{l}", hT[:, :, :])

                def evac_q(j):
                    act.wait_ge(S("block_used"), first[f"wq{l}"] + j + 1)
                    A_(qT[:, j, :], PS[j % 4][:, 0:T], ACT.Copy).then_inc(S(f"q_evac{l}"), 1)

                highs(first[f"wq{l}"], LISTS, evac_q)
                make_high(act, down_ahead(l, 0))
                for half in range(2):
                    act.wait_ge(S("block_used"), first[f"keys{l}"] + half + 1)
                    for tt in range(TT):
                        for q in range(2):
                            i = half * 8 + q * 4
                            last = A_(sc[:, tt, i:i + 4, :],
                                      PS[(1 - tt) * 4 + half * 2 + q][:, :].rearrange("p (a n) -> p a n", a=4),
                                      ACT.Copy)
                    last.then_inc(S(f"sc_ready{l}"), 1)
                    make_high(act, down_ahead(l, 0) + 1 + half)

                def ahead_pair(p, at=None, gate_turn=None):
                    m = down_ahead(l, p)
                    for k in range(2):
                        if gate_turn is not None:
                            gates(gate_turn + k)
                        make_high(act, m + RING + k, at)
                    act.wait_ge(S("block_used"), more(at) + (m + 2))
                    if p >= 2:
                        act.wait_ge(S(f"z_out{l}_{p % 2}"), 8 * more_pairs(at) + 16 * (p // 2))
                    A_(wf[:, p % 2, :], PS[4 + p % 2][:, :], gelu).then_inc(S(f"act_done{l}"), 1)
                    act.wait_ge(S(f"act_done{l}"), more_pairs(at) + (p + 1))
                    dst = A[f"z{l}"][ds(more_pairs(at) + p, 1), :, :].rearrange("a p n -> (a p) n") if at \
                        else A[f"z{l}"][p]
                    act.dma_start(dst, wf[:, p % 2, :]).then_inc(S(f"z_out{l}_{p % 2}"), 16)

                def gates(it):
                    for half in range(2):
                        act.wait_ge(S(f"g_ps{l}"), 2 * it + (half + 1))
                        t0 = it * 8 + half * 4
                        dst = G[:, :, t0:t0 + 4] if isinstance(it, int) else G[:, :, ds(t0, 4)]
                        A_(dst, PS[half][:, :].rearrange("p (t i) -> p i t", t=4), ACT.Copy)\
                            .then_inc(S(f"g_evac{l}"), 1)

                for p in range(6):
                    ahead_pair(p)
                with act.Fori(0, 2) as q:
                    for p in range(6, 12):
                        ahead_pair(p, (q, 12))
                for tt in range(TT):
                    act.wait_ge(S(f"gate_sub{l}"), tt + 1)
                    A_(tv[:, tt, :, :], tv[:, tt, :, :], ACT.Exp).then_inc(S(f"gate_exp{l}"), 1)
                ahead_pair(AHEAD_TOP - 1)
                ahead_pair(AHEAD_TOP)
                p0 = AHEAD_TOP + 1
                for p in range(p0, p0 + 4):
                    ahead_pair(p, None, 2 * (p - p0))
                with act.Fori(0, 2) as q:
                    for p in range(p0 + 4, p0 + 10):
                        ahead_pair(p, (q, 12), 12 * q + 2 * (p - p0))

                def weights_high(p, at=None, used=None):
                    act.wait_ge(S(f"wf_ready{l}"), more_pairs(at) + (p + 1))
                    if used is not None:
                        act.wait_ge(S("block_used"), more(at) + used)
                    A_(w_hi[:, p % 2, :], wf[:, p % 2, :], ACT.Copy).then_inc(S(f"w_high{l}"), 1)

                def up_pair(p, at=None, following=True):
                    m = up_ahead(l, p)
                    if following:
                        weights_high(p + 1, at, used=m)
                    for k in range(2):
                        make_high(act, m + RING + k, at)

                def apply_gelu(m, p, at=None):
                    act.wait_ge(S("block_used"), more(at) + (m + 2))
                    A_(PS[4 + p % 2][:, :], PS[4 + p % 2][:, :], gelu).then_inc(S(f"act_done{l}"), 1)

                m = down_ahead(l, AHEAD)
                weights_high(0)
                make_high(act, m + RING)
                make_high(act, m + RING + 1)
                apply_gelu(m, AHEAD)
                for p in range(3):
                    up_pair(p)
                with act.Fori(0, 5) as q:
                    for p in range(3, 9):
                        up_pair(p, (q, 12))
                for p in range(33, AHEAD):
                    up_pair(p, following=p + 1 < AHEAD)

                def turn(s, at=None):
                    m, p = turn_block(l, s), AHEAD + 2 * s
                    make_high(act, m + 3, at)
                    make_high(act, m + 4, at)
                    apply_gelu(m, p + 1, at)
                    make_high(act, m + 5, at)
                    weights_high(p + 1, at)
                    if s == TURNS - 1:
                        return
                    for k in (6, 7, 8):
                        make_high(act, m + k, at)
                    apply_gelu(m + 4, p + 2, at)
                    make_high(act, m + 9, at)
                    weights_high(p + 2, at)
                    make_high(act, m + 10, at)

                weights_high(AHEAD)
                turn(0)
                turn(1)
                with act.Fori(0, 3) as q:
                    for r in range(3):
                        turn(2 + r, (q, 24))
                turn(11)
                turn(12)
                turn(TURNS - 1)
                act.wait_ge(S("block_used"), turn_block(l, TURNS - 1) + 6)
                for f in range(2):
                    for tt in range(TT):
                        A_(ytok[:, tt, f * 512:(f + 1) * 512], PS[tt * 2 + f][:, :], ACT.Copy)\
                            .then_inc(S(f"ytok_ready{l}"), 1)

            peer(0, "w_out_evac")
            norm_act("final", xT[:, :, :], "x_peer0", (1, 2), first_blocks=first["w_in2"])
            norm_act("mix2", xT[:, :, :], "norm_done",
                     [2 * NORMED.index("final") + f + 1 for f in range(2)])
            split_h("mix2", hT[:, :, :])
            A_(lru_s[:, 1, :], col("lam", 0, 8), ACT.Abs).then_inc(S("lam_abs"), 1)
            act.wait_ge(S("lam_abs"), 1)
            A_(lru_s[:, 1, :], lru_s[:, 1, :], ACT.Exp, scale=-1.0).then_inc(S("lam_exp"), 1)
            act.wait_ge(S("lam_1pe"), 1)
            A_(lru_s[:, 3, :], lru_s[:, 2, :], ACT.Ln).then_inc(S("lam_ln"), 1)
            act.wait_ge(S("pads2_ready"), 1)

            def w_in2_block(s):
                if s >= SECT * KC:
                    return first["w_out2"] + s - SECT * KC
                return (first["w_in2"] if s < 3 * KC else first["w_in2b"] - 3 * KC) + s

            for s in range(SECT * KC):
                sec, j = s // KC, s % KC
                if s == 3 * KC:
                    for k in range(KC):
                        if k % 4 == 3:
                            act.wait_ge(S("block_used"), first["gates2"] + k // 4 + 1)
                        else:
                            act.wait_ge(S("gate_ps"), k - k // 4 + 1)
                        A_(rg[:, k, :], PS[4 + k % 4][:, 0:T], ACT.Sigmoid, bias=col("b_a", k))
                        A_(ig[:, k, :], PS[4 + k % 4][:, T:2 * T], ACT.Sigmoid, bias=col("b_x", k))\
                            .then_inc(S("gate_evac"), 1)
                    make_high(act, w_in2_block(s + 1))
                    make_high(act, w_in2_block(s + 2))
                if s not in (3 * KC - 2, 3 * KC - 1):
                    make_high(act, w_in2_block(s + RING))
                act.wait_ge(S("block_used"), w_in2_block(s) + 1)
                src = PS[s % 4][:, 0:T]
                dst, fn = [(xa[:, j, TAPS - 1:], ACT.Copy), (sma[:, j, :], ACT.Sigmoid), (smb[:, j, :], ACT.Sigmoid),
                           (vb[:, j, :], ACT.Copy), (cbv[:, j, TAPS_B - 1:], ACT.Copy), (bb[:, j, :], ACT.Copy),
                           (gg[:, j, :], ACT.Gelu_apprx_tanh)][sec]
                if s == 4 * KC:
                    act.wait_ge(S("lam_ready"), 1)
                    act.wait_ge(S("gate_evac"), KC)
                    for k in range(KC):
                        last = A_(av[:, k, :], rg[:, k, :], ACT.Exp, scale=lru_s[:, 4, k:k + 1])
                    last.then_inc(S("av_ready"), 1)
                if s == 4 * KC + 3:
                    for k in range(KC):
                        last = A_(th[:, k, :], rg[:, k, :], ACT.Tanh, scale=lru_s[:, 5, k:k + 1])
                    last.then_inc(S("th_ready"), 1)
                if s == 5 * KC:
                    act.wait_ge(S("mult_sq"), 1)
                    A_(th[:, :, :], th[:, :, :], ACT.Sqrt).then_inc(S("mult_ready"), 1)
                A_(dst, src, fn).then_inc(S("in2_evac"), 1)
            split_h("merged", gg[:, :, :])
            highs(first["w_out2"], KC, lambda j: None)
            peer(1, "w_out2_evac")
            norm_act("fin", xT[:, :, :], "x_peer1", (1, 2))

        @block.vector
        def _(dve):
            v = nc.vector
            counts = {}

            def link(ins, signal="dve_chain", by=1):
                counts[signal] = counts.get(signal, 0) + by
                ins.then_inc(S(signal), by)
                dve.wait_ge(S(signal), counts[signal])

            TTn, TS, STT = v.tensor_tensor, v.tensor_scalar, v.scalar_tensor_tensor

            def norm_dve(tag, src, dst, scale, shift=None):
                dve.wait_ge(S("rms"), NORMS.index(tag) + 1)
                link(v.reciprocal(rstd, rstd))
                for f in range(2):
                    half = range(f * HC, (f + 1) * HC)
                    for c in half:
                        last = STT(dst[:, c, :], src[:, c, :], scale(c), rstd, ALU.mult, ALU.mult)
                    if shift is not None:
                        link(last)
                        for c in half:
                            last = TS(dst[:, c, :], dst[:, c, :], shift(c), None, ALU.add)
                    link(last, "norm_done")

            def split_low(tag, src):
                for f in range(2):
                    half = slice(f * HC, (f + 1) * HC)
                    dve.wait_ge(S("h_high"), 2 * SPLITS.index(tag) + f + 1)
                    link(TTn(h_lo[:, half, :], src[:, half, :], h_hi[:, half, :].bitcast(fp32), ALU.subtract),
                         "h_split")

            def ada(s):
                for k in range(4):
                    ada_piece(s, k)

            def ada_piece(s, k):
                if k == ada_order(s)[0] and s >= 2:
                    dve.wait_ge(S("ada_ps"), s - 1)
                dve.wait_ge(S(f"ada_in{s % 2}_{k}"), 16 * (s // 2 + 1))
                w = (ada_buf if s < 4 else ada_buf_late)[s % 2]
                acc = ada_acc[:, s % 2, :]
                order = ada_order(s)
                for c in (2 * k, 2 * k + 1):
                    if c == 2 * order[0]:
                        link(TS(acc, w[:, c, :], cact[:, c:c + 1], None, ALU.mult))
                    else:
                        link(STT(acc, w[:, c, :], cact[:, c:c + 1], acc, ALU.mult, ALU.add),
                             "ada_acc" if c == 2 * order[-1] + 1 else "dve_chain")

            def ada_out(s):
                dve.wait_ge(S("ada_ps"), {0: 2, 2: 4}.get(s, s + 1))
                m = mod[:, s * KC:(s + 1) * KC]
                link(TTn(m, PS[7][:, s * KC:(s + 1) * KC], col("b_ada", s * KC, KC), ALU.add), "mod_ready")
                if s in (1, 4):
                    link(STT(m, m, 1.0, col("norm_mix" if s == 1 else "norm_ffn", 0, KC), ALU.add, ALU.mult))

            link(v.memset(epsc[:, :], EPS), "eps_ready")
            v.memset(u_pad[:, :, 0:UPAD], 0.0)
            link(v.memset(xbc_in[:, :, 0:TAPS - 1], 0.0), "pads_ready")
            dve.wait_ge(S("prm_in"), 16)
            dve.wait_ge(S("cact_ready"), 1)
            ada(0)
            dve.wait_ge(S("rms"), 1)
            link(v.reciprocal(rstd, rstd), "rstd_mix")
            ada(1)
            ada_out(0)
            ada_out(1)
            dve.wait_ge(S("x_scaled"), 1)
            for f in range(2):
                for c in range(f * HC, (f + 1) * HC):
                    last = TS(hT[:, c, :], hT[:, c, :], mod[:, KC + c:KC + c + 1], mod[:, c:c + 1],
                              ALU.mult, ALU.add)
                link(last, "norm_done")
            split_low("mix", hT[:, :, :])

            def conv_tile(j):
                link(TS(xbc[:, j, :], xbc_in[:, j, 0:T], col("conv_w", j), col("conv_b", j), ALU.mult, ALU.add))
                for k in range(1, TAPS):
                    link(STT(xbc[:, j, :], xbc_in[:, j, k:k + T], col("conv_w", k * XBC_TILES + j), xbc[:, j, :],
                             ALU.mult, ALU.add), "conv_ready" if (j, k) == (XBC_TILES - 1, TAPS - 1) else "dve_chain")

            for k in range(4):
                ada_piece(2, k)
                if k:
                    for j in (2 * k - 2, 2 * k - 1):
                        dve.wait_ge(S("w_in_evac"), j + 1)
                        conv_tile(j)
            for j in range(6, XBC_TILES):
                dve.wait_ge(S("w_in_evac"), j + 1)
                conv_tile(j)

            def softplus_u(e, u, sem_in, sem_out):
                dve.wait_ge(S(sem_in), 1)
                link(TS(u, e, 1.0, None, ALU.add), sem_out)

            def log1p(e, u, ln, tmp):
                link(TS(u, u, -1.0, None, ALU.add))
                link(TS(tmp, u, 0.0, None, ALU.is_equal))
                link(TTn(u, u, tmp, ALU.add))
                link(v.reciprocal(u, u))
                link(TTn(u, u, ln, ALU.mult))
                link(TTn(u, u, tmp, ALU.add))
                link(TTn(ln, u, e, ALU.mult))

            H16 = slice(0, HEADS)
            softplus_u(dts[H16, 1, :], dts[H16, 2, :], "dt_exp", "dt_1pe")
            dve.wait_ge(S("dt_ln"), 1)
            log1p(dts[H16, 1, :], dts[H16, 2, :], dts[H16, 3, :], dts[H16, 4, :])
            link(STT(dts[H16, 2, :], dts[H16, 0, :], 0.0, dts[H16, 3, :], ALU.max, ALU.add))
            dve.wait_ge(S("alog_exp"), 1)
            link(TS(dts[H16, 3, :], dts[H16, 2, :], lru_s[H16, 0, 0:1], -1.0, ALU.mult, ALU.mult))
            for c in range(NCH):
                last = v.tensor_tensor_scan(dts[H16, 4, c * CH:(c + 1) * CH], cst[H16, CONES:CONES + CH],
                                            dts[H16, 3, c * CH:(c + 1) * CH], 0.0, ALU.mult, ALU.add)
            link(last, "acs_ready")
            ada(3)
            link(v.memset(p_sum[:, :, 0:UPAD], 0.0), "ada_free")
            dve.wait_ge(S("tok_ps"), 1)
            dve.wait_ge(S("btok_ps"), 1)
            tok_ps = PS[7][:, P:P + 5 * HEADS]
            v.tensor_copy(tok[:, 0:2, :], tok_ps[:, 0:2 * HEADS].rearrange("p (a h) -> p a h", a=2))
            TS(tok[:, 2:4, :], tok_ps[:, 2 * HEADS:4 * HEADS].rearrange("p (a h) -> p a h", a=2), -1.0, None, ALU.mult)
            link(v.tensor_copy(tok[:, 4, :], tok_ps[:, 4 * HEADS:5 * HEADS]), "tok_ready")
            for b in range(4):
                c, hf = b // 2, b % 2
                dve.wait_ge(S("xtok_ps"), b + 1)
                last = TTn(xdt[:, c, hf * 512:(hf + 1) * 512].rearrange("p (h d) -> p h d", d=HD),
                           PS[3 + b][:, :].rearrange("p (h d) -> p h d", d=HD),
                           tok[:, c, hf * HPG:(hf + 1) * HPG][:, :, None].to_broadcast([P, HPG, HD]), ALU.mult)
                link(last, "xdt_ready")
            link(TTn(xdte.rearrange("p (h d) -> p h d", d=HD), xdt[:, 0, :].rearrange("p (h d) -> p h d", d=HD),
                     tok[:, 4, :][:, :, None].to_broadcast([P, HEADS, HD]), ALU.mult), "xdte_ready")
            dve.wait_ge(S("btok_ready"), 1)
            ada_out(2)
            ada_out(3)
            dve.wait_ge(S("cb_ready"), 1)

            def seg_head(h):
                dve.wait_ge(S("rows_ps"), h + 1)
                if h >= 2:
                    dve.wait_ge(S("dec_ready"), h - 1)
                TTn(seg[:, h % 2, :].rearrange("p (c l) -> p c l", c=NCH),
                    PS[ROW_BANKS[h % 4]][:, 0:T].rearrange("p (c l) -> p c l", c=NCH),
                    mask[:, None, :].to_broadcast([P, NCH, CH]), ALU.add).then_inc(S("seg_ready"), 1)

            def y_pair(j):
                dve.wait_ge(S("y_ps"), 2 * j + 2)
                STT(mixT[:, NPOOL + j, :], xbc[:, j, :], col("d_skip", j), PS[2 + j % 2][:, 0:T],
                    ALU.mult, ALU.add).then_inc(S("y_evac"), 1)

            seg_head(0)
            for h in range(HEADS):
                if h + 1 < HEADS:
                    seg_head(h + 1)
                g = h // HPG
                dve.wait_ge(S("ecs_ready"), h + 1)
                if h >= 2:
                    dve.wait_ge(S("y_ps"), h - 1)
                TTn(cexp[:, h % 2, :], xbc[:, 10 + g, CH:2 * CH], ecs[:, h % 2, :], ALU.mult)\
                    .then_inc(S("cexp_ready"), 1)
                dve.wait_ge(S("dec_ready"), h + 1)
                TTn(mdec[:, h % 2, :], dec[:, h % 2, :], cbt[:, g, :], ALU.mult).then_inc(S("mdec_ready"), 1)
                if h % 2 == 1 and h >= 3:
                    y_pair(h // 2 - 1)
            y_pair(HEADS // 2 - 1)
            dve.wait_ge(S("y_evac"), HEADS // 2)
            link(TTn(mixT[:, NPOOL:, :], mixT[:, NPOOL:, :], zs[:, :, :], ALU.mult), "y_gated")
            dve.wait_ge(S("block_used"), first["pool_w"] + 1)
            for g in range(NPOOL):
                last = TS(mixT[:, g, :], PS[4 + g // 2][:, (g % 2) * T:(g % 2 + 1) * T], col("pool_b", g),
                          col("pool_scale", g), ALU.add, ALU.mult)
            last.then_inc(S("pool_out"), 1)
            norm_dve("ssd", mixT[:, NPOOL:, :], mixT[:, NPOOL:, :], lambda c: col("ssd_norm", c))
            for m in range(KC):
                ada_piece(4 + m // 4, ada_order(4 + m // 4)[m % 4])
                if m == 7:
                    ada_out(4)
                dve.wait_ge(S("block_used"), first["w_out"] + 2 * m + 2)
                STT(xT[:, m, :], PS[m % 4][:, 0:T], mod[:, 2 * KC + m:2 * KC + m + 1], xT[:, m, :],
                    ALU.mult, ALU.add).then_inc(S("w_out_evac"), 1)
            dve.wait_ge(S("w_out_evac"), KC)

            def top16(src, src2, vals, idx, rows, finish):
                for r in rows:
                    last = v.max(vals(r)[:, 0:8], src(r))
                link(last)
                for r in rows:
                    last = v.max_index(idx(r)[:, 0:8], vals(r)[:, 0:8], src(r))
                for r in rows:
                    last = v.match_replace(src2(r), vals(r)[:, 0:8], src(r), LOWEST)
                link(last)
                for r in rows:
                    last = v.max(vals(r)[:, 8:16], src2(r))
                link(last)
                for r in rows:
                    last = v.max_index(idx(r)[:, 8:16], vals(r)[:, 8:16], src2(r))
                link(last, finish)

            def peer(l, scale, shift):
                for j in range(RING):
                    make_low(dve, v, first[f"wq{l}"] + j)
                norm_dve(f"ffn{l}", xT[:, :, :], hT[:, :, :], scale, shift)
                if l == 0:
                    ada_out(5)
                split_low(f"ffn{l}", hT[:, :, :])
                for j in range(RING, LISTS):
                    make_low(dve, v, first[f"wq{l}"] + j)
                dve.wait_ge(S(f"sc_ready{l}"), 2)
                for tt in range(TT):
                    top16(lambda r: sc[:, tt, r, :], lambda r: sc2[:, tt, r, :], lambda r: vv[:, tt, r, :],
                          lambda r: ii[:, tt, r, :], range(LISTS), "dve_chain")
                    link(v.tensor_copy(iif[:, tt, :, :], ii[:, tt, :, :]))
                    v4 = vv[:, tt, :, :].rearrange("p (h s) k -> p h s k", s=2)
                    for h in range(PH):
                        last = TTn(cand[:, tt, h, :].rearrange("p (a b) -> p a b", a=TOPK),
                                   v4[:, h, 0, :][:, :, None].to_broadcast([P, TOPK, TOPK]),
                                   v4[:, h, 1, :][:, None, :].to_broadcast([P, TOPK, TOPK]), ALU.add)
                    link(last)
                    top16(lambda r: cand[:, tt, r, :], lambda r: cand2[:, tt, r, :], lambda r: tv[:, tt, r, :],
                          lambda r: tp[:, tt, r, :], range(PH), "dve_chain")
                    pos = tp[:, tt, :, :].rearrange("p h k -> p (h k)")
                    TS(ab[:, tt, 0, :], pos, 4, None, ALU.logical_shift_right)
                    link(TS(ab[:, tt, 1, :], pos, TOPK - 1, None, ALU.bitwise_and))
                    link(v.tensor_copy(abf[:, tt, :, :], ab[:, tt, :, :]))
                    link(TTn(pick[:, tt, 2, :].rearrange("p (h k) -> p h k", h=PH), tv[:, tt, :, :],
                             tv[:, tt, :, 0:1].to_broadcast([P, PH, TOPK]), ALU.subtract))
                    link(v.tensor_copy(tv[:, tt, :, :], pick[:, tt, 2, :].rearrange("p (h k) -> p h k", h=PH)),
                         f"gate_sub{l}")
                    i4 = iif[:, tt, :, :].rearrange("p (h s) k -> p h s k", s=2)
                    for s in range(2):
                        rk = abf[:, tt, s, :]
                        link(TTn(oh[:, :, :, :].rearrange("p h k a -> p (h k) a"),
                                 rk[:, :, None].to_broadcast([P, PH * TOPK, TOPK]),
                                 iota[:, None, 0:TOPK].to_broadcast([P, PH * TOPK, TOPK]), ALU.is_equal))
                        for h in range(PH):
                            last = TTn(oh[:, h, :, :], oh[:, h, :, :],
                                       i4[:, h, s, :][:, None, :].to_broadcast([P, TOPK, TOPK]), ALU.mult)
                        link(last)
                        link(v.tensor_reduce(pick[:, tt, s, :], oh[:, :, :, :].rearrange("p h k a -> p (h k) a"),
                                             AX.X, ALU.add))
                for tt in range(TT):
                    dve.wait_ge(S(f"gate_exp{l}"), tt + 1)
                    link(v.tensor_reduce(gsum[:, tt, :, 0], tv[:, tt, :, :], AX.X, ALU.add))
                    link(v.reciprocal(grec[:, tt, :, :], gsum[:, tt, :, :]))
                    link(TTn(pick[:, tt, 2, :].rearrange("p (h k) -> p h k", h=PH), tv[:, tt, :, :],
                             grec[:, tt, :, :].to_broadcast([P, PH, TOPK]), ALU.mult), f"pick_ready{l}")
                for tt in range(TT):
                    dve.wait_ge(S(f"pickT_ps{l}"), tt + 1)
                    link(v.tensor_copy(selT[:, :, tt * P:(tt + 1) * P],
                                       PS[2 + tt][:, 0:3 * P].rearrange("p (a t) -> p a t", a=3)), f"pickT_ready{l}")

                def gates(it, is_first):
                    src = selT[:, :, 0:8] if is_first else selT[:, :, ds(it * 8, 8)]
                    if not is_first:
                        dve.wait_ge(S(f"onehot{l}"), 2 * it)
                    v.tensor_copy(stage[:, :, :], src).then_inc(S(f"stage{l}"), 1)
                    dve.wait_ge(S(f"stage{l}"), it + 1)
                    for half in range(2):
                        if not is_first:
                            dve.wait_ge(S(f"g_ps{l}"), 2 * it + (half - 1))
                        for k in range(4):
                            t = half * 4 + k
                            TS(onehot[0][half][:, k * P:(k + 1) * P], iota, stage[:, 0, t:t + 1], None,
                               ALU.is_equal)
                            last = TS(onehot[1][half][:, k * P:(k + 1) * P], iota, stage[:, 1, t:t + 1],
                                      stage[:, 2, t:t + 1], ALU.is_equal, ALU.mult)
                        last.then_inc(S(f"onehot{l}"), 1)

                dve.wait_ge(S(f"x_out{l}"), 16)
                gates(0, True)
                with dve.Fori(1, T // 8) as it:
                    gates(it, False)

                def low(m, at=None):
                    make_low(dve, v, m, at)

                def weigh(p, src, at=None):
                    i2 = 2 * more_pairs(at) + 2 * p
                    g2 = G[:, ds(i2, 2), :] if at else G[:, i2:i2 + 2, :]
                    TTn(wf[:, p % 2, :].rearrange("p (i t) -> p i t", i=2),
                        src.rearrange("p (i t) -> p i t", i=2), g2, ALU.mult).then_inc(S(f"wf_ready{l}"), 1)

                def weigh_back(p, at=None):
                    in_loop = 32 * at[0] if at else 0
                    dve.wait_ge(S(f"z_in{l}_{p % 3}"), in_loop + 16 * (p // 3 + 1))
                    weigh(p, z_back[p % 3], at)

                def weigh_bank(p, at=None):
                    dve.wait_ge(S(f"act_done{l}"), more_pairs(at) + (p + 1))
                    weigh(p, PS[4 + p % 2][:, :], at)

                def weights_low(p, at=None):
                    dve.wait_ge(S(f"w_high{l}"), more_pairs(at) + (p + 1))
                    TTn(w_lo[:, p % 2, :], wf[:, p % 2, :], w_hi[:, p % 2, :].bitcast(fp32), ALU.subtract)\
                        .then_inc(S(f"w_ready{l}"), 1)

                dve.wait_ge(S(f"g_evac{l}"), T // 4)
                dve.wait_ge(S(f"z_out{l}_0"), 16 * AHEAD // 2)
                weigh_back(0)
                weights_low(0)
                for k in range(RING):
                    low(up_ahead(l, 0) + k)
                dve.wait_ge(S(f"z_out{l}_1"), 16 * AHEAD // 2)

                def up_pair(p, at=None, following=True):
                    m = up_ahead(l, p)
                    if following:
                        weigh_back(p + 1, at)
                        weights_low(p + 1, at)
                    low(m + RING, at)
                    low(m + RING + 1, at)

                for p in range(3):
                    up_pair(p)
                with dve.Fori(0, 5) as q:
                    for p in range(3, 9):
                        up_pair(p, (q, 12))
                for p in range(33, AHEAD):
                    up_pair(p, following=p + 1 < AHEAD)

                def turn(s, at=None):
                    m, p = turn_block(l, s), AHEAD + 2 * s
                    low(m + 3, at)
                    low(m + 4, at)
                    weigh_bank(p + 1, at)
                    low(m + 5, at)
                    weights_low(p + 1, at)
                    if s == TURNS - 1:
                        return
                    for k in (6, 7, 8):
                        low(m + k, at)
                    weigh_bank(p + 2, at)
                    low(m + 9, at)
                    weights_low(p + 2, at)
                    low(m + 10, at)

                weigh_bank(AHEAD)
                weights_low(AHEAD)
                turn(0)
                turn(1)
                with dve.Fori(0, 3) as q:
                    for r in range(3):
                        turn(2 + r, (q, 24))
                turn(11)
                turn(12)
                turn(TURNS - 1)
                dve.wait_ge(S(f"x_back{l}"), 16)
                for q in range(2):
                    for tt in range(TT):
                        dve.wait_ge(S(f"yT_ps{l}"), q * 2 + tt + 1)
                        for k in range(4):
                            c = q * 4 + k
                            d = xT[:, c, tt * P:(tt + 1) * P]
                            src = PS[4 + tt * 2 + q][:, k * P:(k + 1) * P]
                            if l == 0:
                                last = STT(d, src, mod[:, 5 * KC + c:5 * KC + c + 1], d, ALU.mult, ALU.add)
                            else:
                                last = TTn(d, src, d, ALU.add)
                    last.then_inc(S(f"x_peer{l}"), 1)
                dve.wait_ge(S(f"x_peer{l}"), 2)

            peer(0, lambda c: mod[:, 4 * KC + c:4 * KC + c + 1], lambda c: mod[:, 3 * KC + c:3 * KC + c + 1])
            norm_dve("final", xT[:, :, :], xT[:, :, :], lambda c: col("norm_final", c))
            norm_dve("mix2", xT[:, :, :], hT[:, :, :], lambda c: col("norm1", c))
            split_low("mix2", hT[:, :, :])
            v.memset(xa[:, :, 0:TAPS - 1], 0.0)
            link(v.memset(cbv[:, :, 0:TAPS_B - 1], 0.0), "pads2_ready")
            softplus_u(lru_s[:, 1, :], lru_s[:, 2, :], "lam_exp", "lam_1pe")
            dve.wait_ge(S("lam_ln"), 1)
            log1p(lru_s[:, 1, :], lru_s[:, 2, :], lru_s[:, 3, :], lru_s[:, 6, :])
            link(TS(lru_s[:, 2, :], col("lam", 0, 8), -1.0, 0.0, ALU.mult, ALU.max))
            link(TTn(lru_s[:, 3, :], lru_s[:, 3, :], lru_s[:, 2, :], ALU.add))
            link(TS(lru_s[:, 4, :], lru_s[:, 3, :], -8.0, None, ALU.mult))
            link(TS(lru_s[:, 5, :], lru_s[:, 3, :], 8.0, None, ALU.mult), "lam_ready")

            def conv(dst, src, name, bias, taps):
                for j in range(KC):
                    if bias:
                        last = TS(dst[:, j, :], src[:, j, 0:T], col(name, j), col(bias, j), ALU.mult, ALU.add)
                    else:
                        last = TS(dst[:, j, :], src[:, j, 0:T], col(name, j), None, ALU.mult)
                link(last)
                for k in range(1, taps):
                    for j in range(KC):
                        last = STT(dst[:, j, :], src[:, j, k:k + T], col(name, k * KC + j), dst[:, j, :],
                                   ALU.mult, ALU.add)
                    if k < taps - 1:
                        link(last)
                return last

            dve.wait_ge(S("in2_evac"), KC)
            link(conv(xc, xa, "conv_a_w", "conv_a_b", TAPS), "xc_ready")
            dve.wait_ge(S("av_ready"), 1)
            link(TTn(hs[:, :, :], av[:, :, :], av[:, :, :], ALU.mult))
            dve.wait_ge(S("th_ready"), 1)
            link(STT(th[:, :, :].rearrange("p a b -> p (a b)"), hs[:, :, :].rearrange("p a b -> p (a b)"), 1.0,
                     th[:, :, :].rearrange("p a b -> p (a b)"), ALU.add, ALU.mult), "mult_sq")
            link(TTn(ig[:, :, :], ig[:, :, :], xc[:, :, :], ALU.mult))
            dve.wait_ge(S("mult_ready"), 1)
            link(TTn(ig[:, :, :], ig[:, :, :], th[:, :, :], ALU.mult))
            for j in range(KC):
                last = v.tensor_tensor_scan(hs[:, j, :], av[:, j, :], ig[:, j, :], 0.0, ALU.mult, ALU.add)
            link(last)
            link(TTn(hs[:, :, :], hs[:, :, :], sma[:, :, :], ALU.mult))
            dve.wait_ge(S("in2_evac"), 5 * KC)
            link(TTn(cbv[:, :, TAPS_B - 1:], cbv[:, :, TAPS_B - 1:], vb[:, :, :], ALU.mult))
            link(conv(rg, cbv, "conv_b_w", None, TAPS_B))
            link(TTn(rg[:, :, :], rg[:, :, :], smb[:, :, :], ALU.mult))
            dve.wait_ge(S("in2_evac"), 6 * KC)
            link(TTn(rg[:, :, :], rg[:, :, :], bb[:, :, :], ALU.mult))
            def merge(f):
                half = slice(f * HC, (f + 1) * HC)
                dve.wait_ge(S("in2_evac"), 6 * KC + (f + 1) * HC)
                link(TTn(gg[:, half, :], gg[:, half, :], hs[:, half, :], ALU.mult))
                link(TTn(gg[:, half, :], gg[:, half, :], rg[:, half, :], ALU.add), "norm_done")

            merge(0)
            for m in range(RING):
                make_low(dve, v, first["w_out2"] + m)
            merge(1)
            split_low("merged", gg[:, :, :])
            for m in range(KC):
                if m + RING < KC:
                    make_low(dve, v, first["w_out2"] + m + RING)
                dve.wait_ge(S("block_used"), first["w_out2"] + m + 1)
                TTn(xT[:, m, :], PS[m % 4][:, 0:T], xT[:, m, :], ALU.add).then_inc(S("w_out2_evac"), 1)
            dve.wait_ge(S("w_out2_evac"), KC)
            peer(1, lambda c: col("norm2", c), None)
            norm_dve("fin", xT[:, :, :], hT[:, :, :], lambda c: col("final", c))

        @block.gpsimd
        def _(pool):
            pool.wait_ge(S("rstd_mix"), 1)
            nc.gpsimd.tensor_tensor(hT[:, :, :], xT[:, :, :], rstd[:, None, :].to_broadcast([P, KC, T]), ALU.mult)\
                .then_inc(S("x_scaled"), 1)
            for i in range(24):
                make_low(pool, nc.gpsimd, w_in_block(i))
            pool.wait_ge(S("w_in_evac"), 17)
            pool.wait_ge(S("ada_free"), 1)
            pool.wait_ge(S("inv_in"), 16)
            g_ = nc.gpsimd
            n = 0

            def link(ins):
                nonlocal n
                n += 1
                ins.then_inc(S("pool_chain"), 1)
                pool.wait_ge(S("pool_chain"), n)

            for g, w in enumerate(POOL_W):
                cur, half = u_pad[:, g, :], 0
                step = 1
                while step < w:
                    dst = p_sum[:, half, :]
                    link(g_.tensor_tensor(dst[:, UPAD:], cur[:, UPAD:], cur[:, UPAD - step:UPAD - step + T], ALU.add))
                    cur, half, step = dst, 1 - half, step * 2
                link(g_.tensor_tensor(p_t[:, g, :], cur[:, UPAD:], inv[:, g, :], ALU.mult))
                ins = g_.tensor_tensor(p_mix[:, g, :], p_t[:, g, :], u_pad[:, g, UPAD:], ALU.subtract)
                if g == NPOOL - 1:
                    ins.then_inc(S("pmix_ready"), 1)
                else:
                    link(ins)

            def peer(l):
                normed(pool, f"ffn{l}")
                pool.dma_start(A["x_spill"], xT[:, :, :]).then_inc(S(f"x_out{l}"), 16)
                for p in range(4):
                    for k in range(2):
                        make_low(pool, g_, down_ahead(l, p) + k)
                with pool.Fori(0, 5) as q:
                    for p in range(4, 10):
                        for k in range(2):
                            make_low(pool, g_, down_ahead(l, p) + k, (q, 12))
                for p in range(34, AHEAD + 1):
                    for k in range(2):
                        make_low(pool, g_, down_ahead(l, p) + k)

            peer(0)
            for s in range(SECT * KC):
                make_low(pool, nc.gpsimd, (first["w_in2"] if s < 3 * KC else first["w_in2b"] - 3 * KC) + s)
            peer(1)


def _chunks(w, n):
    k, m = w.shape
    return np.ascontiguousarray(w.reshape(k // P, P, m // n, n).transpose(2, 1, 0, 3)).reshape(m // n, P, -1)


def _columns(v):
    return np.ascontiguousarray(v.reshape(-1, P).T)


def kernel(**inputs):
    import concourse.bacc as bacc
    from concourse.bass_utils import run_bass_kernel_spmd

    I = {k: np.asarray(v) for k, v in inputs.items()}
    f = np.float32
    prm = {
        "c": _columns(I["c"][0]), "b_ada": _columns(I["b_ada"][0]), "norm_mix": _columns(I["norm_mix"][0]),
        "norm_ffn": _columns(I["norm_ffn"][0]), "pool_b": _columns(I["pool_b"][0]),
        "pool_scale": _columns(I["pool_scale"][0]), "conv_w": _columns(I["conv_w"][0]),
        "conv_b": _columns(I["conv_b"][0]), "d_skip": _columns(np.repeat(I["d_skip"][0], HD)),
        "ssd_norm": _columns(I["ssd_norm"][0]), "norm_final": _columns(I["norm_final"]),
        "dt_bias": np.pad(I["dt_bias"][0], (0, P - HEADS))[:, None],
        "a_log": np.pad(I["a_log"][0], (0, P - HEADS))[:, None],
        "norm1": _columns(I["norm1_g_2"][0]), "conv_a_w": _columns(I["conv_a_w_2"][0]),
        "conv_a_b": _columns(I["conv_a_b_2"][0]), "b_a": _columns(I["b_a_2"][0]), "b_x": _columns(I["b_x_2"][0]),
        "lam": _columns(I["lru_lambda_2"][0]), "conv_b_w": _columns(I["conv_b_w_2"][0]),
        "norm2": _columns(I["norm2_g_2"][0]), "final": _columns(I["final_g_2"]),
    }
    cst = np.zeros((P, NCONST), f)
    cst[:, CIDENT:CIDENT + P] = np.eye(P)
    cst[:, CONES:CONES + P] = 1.0
    cst[:, CMASK:CMASK + P] = np.where(np.arange(P)[:, None] <= np.arange(P)[None, :], 0.0, -1e38)
    cst[:, CIOTA:CIOTA + P] = np.arange(P)
    inv = np.zeros((P, NPOOL, T), f)
    for g, w in enumerate(POOL_W):
        inv[:, g] = 1.0 / np.minimum(np.arange(T) + 1, w)

    w_in = I["w_in"][0]
    w_in2 = I["w_in_2"][0].reshape(D, 7, D)[:, [0, 5, 6, 2, 4, 3, 1]].reshape(D, 7 * D)
    keys0 = np.stack([I["sub_keys1"][0], I["sub_keys2"][0]], axis=1)
    keys1 = I["peer_subkeys_2"][0]

    def down(t):
        return np.ascontiguousarray(t.reshape(NKEYS, NKEYS, KC, P).transpose(1, 3, 2, 0)).reshape(NKEYS, P, D)

    def up(t):
        return np.ascontiguousarray(t.reshape(NKEYS, NKEYS, D).transpose(1, 0, 2))

    def keys(k):
        return np.ascontiguousarray(k.reshape(LISTS, NKEYS, P).transpose(2, 0, 1)).reshape(P, LISTS * NKEYS)

    def heads(a, x):
        w = np.stack([a, x], axis=1).reshape(2, 4, 2, P, P)
        return np.ascontiguousarray(w.transpose(0, 3, 1, 2, 4)).reshape(2, P, BLK)

    arrays = {
        "prm": np.concatenate([prm[n] for n, _ in _COLS], axis=1),
        "cst": cst, "inv": inv,
        "xT": I["x"][0].T.reshape(KC, P, T).transpose(1, 0, 2),
        "w_ada": I["w_ada"][0].reshape(KC, P, 6, D).transpose(2, 1, 0, 3).reshape(6, P, KC * D),
        "w_in": _chunks(w_in[:, :24 * P], P), "w_dt": _chunks(w_in[:, 24 * P:], HEADS)[0],
        "pool_w": I["pool_w"][0].transpose(1, 0, 2).reshape(P, NPOOL * P),
        "w_out": _chunks(I["w_out"][0], P),
        "wq0": _chunks(I["w_query"][0], P), "keys0": keys(keys0),
        "down0": down(I["expert_down"][0]), "up0": up(I["expert_up"][0]),
        "w_in2": _chunks(w_in2, P), "w_gates2": heads(I["w_a_2"][0], I["w_x_2"][0]),
        "w_out2": _chunks(I["w_out_2"][0], P),
        "wq1": _chunks(I["peer_wq_2"][0], P), "keys1": keys(keys1),
        "down1": down(I["peer_u_2"][0]), "up1": up(I["peer_v_2"][0]),
    }
    nc = bacc.Bacc("TRN2", target_bir_lowering=False, num_devices=1)
    feed, A = {}, {}
    for name, a in arrays.items():
        a = np.ascontiguousarray(a)
        feed[f"in_{name}"] = a
        A[name] = nc.dram_tensor(f"in_{name}", a.shape, mybir.dt.from_np(a.dtype), kind="ExternalInput").ap()
    out = nc.dram_tensor("out", (P, KC, T), mybir.dt.float32, kind="ExternalOutput").ap()
    for name, shape in (("z0", (NKEYS // 2, P, 512)), ("z1", (NKEYS // 2, P, 512)), ("x_spill", (P, KC, T))):
        A[name] = nc.dram_tensor(f"kept_{name}", shape, mybir.dt.float32, kind="Internal").ap()
    decoder_kernel(nc, A, out)
    r = run_bass_kernel_spmd(nc, [feed], core_ids=[0])
    y = r.results[0]["out"]
    return np.ascontiguousarray(y.transpose(2, 1, 0)).reshape(1, T, D)
```
